# Optimizing a Trainium2 kernel written in Bass

```python
import math
import numpy as np
import jax
import jax.numpy as jnp
from jax import lax

D_MODEL = 1024
BATCH = 1
SEQ = 256
DEPTH = 2

HEAD_DIM = 64
ROPE_THETA = 10000.0
EPS = 1e-6
F32 = jnp.float32

A_HEADS = 4
MOBA_BLOCK = 256
MOBA_TOPK = 3
MOBA_QCHUNK = 32

B_HEADS = 4
IDX_HEADS = 8
IDX_DIM = 64
DSA_TOPK_MAX = 256
DSA_QCHUNK = 64

C_HEADS = 4
C_VDIM = 2 * HEAD_DIM
DIFF_QCHUNK = 128

N_GROUPS = 4
EXPERTS_PER_GROUP = 8
N_EXPERTS = N_GROUPS * EXPERTS_PER_GROUP
EXPERT_TOPK = 2
D_EXPERT = 512
MOE_BLOCK = 256

A_W = A_HEADS * HEAD_DIM
B_W = B_HEADS * HEAD_DIM
C_QK_W = C_HEADS * HEAD_DIM
C_W = C_HEADS * C_VDIM

IN_SIZES = (A_W, A_W, A_W, B_W, B_W, B_W, IDX_HEADS * IDX_DIM, IDX_DIM, IDX_HEADS,
            C_QK_W, C_QK_W, C_QK_W, C_QK_W, C_W, D_MODEL, D_MODEL, D_MODEL)
D_IN = 3 * A_W + 3 * B_W + IDX_HEADS * IDX_DIM + IDX_DIM + IDX_HEADS + 4 * C_QK_W + C_W + 3 * D_MODEL

kernel_name = 'hybrid_moba_dsa_diffattn_hiermoe'

def rms_norm(x, gain):
    xf = x.astype(F32)
    y = xf * lax.rsqrt(jnp.mean(xf * xf, axis=-1, keepdims=True) + EPS)
    return (y * gain.astype(F32)).astype(x.dtype)

def rope_tables(seq_len):
    inv_freq = 1.0 / (ROPE_THETA ** (jnp.arange(0, HEAD_DIM, 2, dtype=F32) / HEAD_DIM))
    ang = jnp.arange(seq_len, dtype=F32)[:, None] * inv_freq[None, :]
    return jnp.cos(ang), jnp.sin(ang)

def apply_rope(x, cos, sin):
    half = x.shape[-1] // 2
    xf = x.astype(F32)
    x1, x2 = xf[..., :half], xf[..., half:]
    c = cos[:, None, :]
    s = sin[:, None, :]
    return jnp.concatenate([x1 * c - x2 * s, x2 * c + x1 * s], axis=-1).astype(x.dtype)

def norm_rope(t, gain, cos, sin):
    return apply_rope(rms_norm(t, gain), cos, sin)

def to_chunks(t, size):
    b, s = t.shape[:2]
    return jnp.moveaxis(t.reshape((b, s // size, size) + t.shape[2:]), 1, 0)

def from_chunks(t):
    t = jnp.moveaxis(t, 0, 1)
    return t.reshape((t.shape[0], t.shape[1] * t.shape[2]) + t.shape[3:])

def split_points():
    return [int(v) for v in np.cumsum(np.array(IN_SIZES))[:-1]]

def moba_attention(q, k, v):
    b, s, h, dh = q.shape
    nb = -(-s // MOBA_BLOCK)
    pad = nb * MOBA_BLOCK - s

    def blocks(t):
        t = jnp.pad(t, ((0, 0), (0, pad), (0, 0), (0, 0)))
        return t.reshape(b, nb, MOBA_BLOCK, h, dh).transpose(0, 3, 1, 2, 4)

    kb, vb = blocks(k), blocks(v)
    k_mean = jnp.mean(kb.astype(F32), axis=3)
    n_sel = min(MOBA_TOPK, nb - 1)
    scale = dh ** -0.5
    b_idx = jnp.arange(b)[:, None, None, None]
    h_idx = jnp.arange(h)[None, :, None, None]
    blk_pos = jnp.arange(MOBA_BLOCK)
    n_sk = n_sel * MOBA_BLOCK

    def chunk_fn(args):
        ci, qc = args
        qh = qc.transpose(0, 2, 1, 3)
        start = ci * MOBA_QCHUNK
        pos = start + jnp.arange(MOBA_QCHUNK)
        own = start // MOBA_BLOCK
        k_own = lax.dynamic_index_in_dim(kb, own, axis=2, keepdims=False)
        v_own = lax.dynamic_index_in_dim(vb, own, axis=2, keepdims=False)
        s_own = jnp.einsum('bhcd,bhkd->bhck', qh, k_own).astype(F32) * scale
        s_own = jnp.where((own * MOBA_BLOCK + blk_pos)[None, :] <= pos[:, None], s_own, -jnp.inf)
        if n_sel == 0:
            p = jax.nn.softmax(s_own, axis=-1).astype(v.dtype)
            return jnp.einsum('bhck,bhkd->bchd', p, v_own)
        gate = jnp.einsum('bhcd,bhnd->bhcn', qh.astype(F32), k_mean)
        gate = jnp.where(jnp.arange(nb) < own, gate, -jnp.inf)
        _, sel = lax.top_k(gate, n_sel)
        k_sel = kb[b_idx, h_idx, sel]
        v_sel = vb[b_idx, h_idx, sel]
        s_sel = jnp.einsum('bhcd,bhcnkd->bhcnk', qh, k_sel).astype(F32) * scale
        s_sel = jnp.where((jnp.arange(n_sel) < own)[:, None], s_sel, -jnp.inf)
        s_all = jnp.concatenate([s_sel.reshape(b, h, MOBA_QCHUNK, n_sk), s_own], axis=-1)
        p = jax.nn.softmax(s_all, axis=-1).astype(v.dtype)
        p_sel = p[..., :n_sk].reshape(b, h, MOBA_QCHUNK, n_sel, MOBA_BLOCK)
        return (jnp.einsum('bhcnk,bhcnkd->bchd', p_sel, v_sel)
                + jnp.einsum('bhck,bhkd->bchd', p[..., n_sk:], v_own))

    n = s // MOBA_QCHUNK
    out = lax.map(chunk_fn, (jnp.arange(n), to_chunks(q, MOBA_QCHUNK)))
    return from_chunks(out)

def dsa_attention(q, k, v, q_idx, k_idx, w_idx):
    b, s, h, dh = q.shape
    n_keep = min(DSA_TOPK_MAX, s // 4)
    scale = dh ** -0.5
    key_pos = jnp.arange(s)
    b_idx = jnp.arange(b)[:, None, None]
    k_idx_f = k_idx.astype(F32)

    def chunk_fn(args):
        ci, qc, qic, wc = args
        pos = ci * DSA_QCHUNK + jnp.arange(DSA_QCHUNK)
        logits = jnp.einsum('bchd,bsd->bchs', qic.astype(F32), k_idx_f) * (IDX_DIM ** -0.5)
        score = jnp.einsum('bch,bchs->bcs', wc.astype(F32), jax.nn.relu(logits))
        score = jnp.where(key_pos[None, None, :] <= pos[None, :, None], score, -jnp.inf)
        _, sel = lax.top_k(score, n_keep)
        k_sel = k[b_idx, sel]
        v_sel = v[b_idx, sel]
        sc = jnp.einsum('bchd,bckhd->bhck', qc, k_sel).astype(F32) * scale
        valid = (sel <= pos[None, :, None])[:, None]
        p = jax.nn.softmax(jnp.where(valid, sc, -jnp.inf), axis=-1).astype(v.dtype)
        return jnp.einsum('bhck,bckhd->bchd', p, v_sel)

    n = s // DSA_QCHUNK
    out = lax.map(chunk_fn, (jnp.arange(n), to_chunks(q, DSA_QCHUNK),
                             to_chunks(q_idx, DSA_QCHUNK), to_chunks(w_idx, DSA_QCHUNK)))
    return from_chunks(out)

def diff_attention(q1, q2, k1, k2, v, lam):
    b, s, h, dh = q1.shape
    scale = dh ** -0.5
    key_pos = jnp.arange(s)

    def chunk_fn(args):
        ci, q1c, q2c = args
        pos = ci * DIFF_QCHUNK + jnp.arange(DIFF_QCHUNK)
        causal = key_pos[None, :] <= pos[:, None]
        s1 = jnp.einsum('bchd,bshd->bhcs', q1c, k1).astype(F32) * scale
        s2 = jnp.einsum('bchd,bshd->bhcs', q2c, k2).astype(F32) * scale
        a1 = jax.nn.softmax(jnp.where(causal, s1, -jnp.inf), axis=-1)
        a2 = jax.nn.softmax(jnp.where(causal, s2, -jnp.inf), axis=-1)
        a = (a1 - lam * a2).astype(v.dtype)
        return jnp.einsum('bhcs,bshe->bche', a, v)

    n = s // DIFF_QCHUNK
    out = lax.map(chunk_fn, (jnp.arange(n), to_chunks(q1, DIFF_QCHUNK), to_chunks(q2, DIFF_QCHUNK)))
    return from_chunks(out)

def mixer_sublayer(x, cos, sin, layer_idx, norm_g, w_in, qk_gain, idx_k_gain, diff_lambda,
                   diff_subln_gain, w_proj_a, w_proj_b, w_proj_c, w_out):
    b, s, _ = x.shape
    hn = rms_norm(x, norm_g)
    proj = hn @ w_in
    (qa, ka, va, qb, kb, vb, qi, ki, wi, q1, q2, k1, k2, vc, ga, gb, gc) = jnp.split(proj, split_points(), axis=-1)

    qa = norm_rope(qa.reshape(b, s, A_HEADS, HEAD_DIM), qk_gain[0], cos, sin)
    ka = norm_rope(ka.reshape(b, s, A_HEADS, HEAD_DIM), qk_gain[1], cos, sin)
    o_a = moba_attention(qa, ka, va.reshape(b, s, A_HEADS, HEAD_DIM)).reshape(b, s, A_W)

    qb = norm_rope(qb.reshape(b, s, B_HEADS, HEAD_DIM), qk_gain[2], cos, sin)
    kb = norm_rope(kb.reshape(b, s, B_HEADS, HEAD_DIM), qk_gain[3], cos, sin)
    qi = apply_rope(qi.reshape(b, s, IDX_HEADS, IDX_DIM), cos, sin)
    ki = apply_rope(rms_norm(ki, idx_k_gain)[:, :, None, :], cos, sin)[:, :, 0, :]
    wi = wi * (IDX_HEADS ** -0.5)
    o_b = dsa_attention(qb, kb, vb.reshape(b, s, B_HEADS, HEAD_DIM), qi, ki, wi).reshape(b, s, B_W)

    q1 = norm_rope(q1.reshape(b, s, C_HEADS, HEAD_DIM), qk_gain[4], cos, sin)
    q2 = norm_rope(q2.reshape(b, s, C_HEADS, HEAD_DIM), qk_gain[4], cos, sin)
    k1 = norm_rope(k1.reshape(b, s, C_HEADS, HEAD_DIM), qk_gain[5], cos, sin)
    k2 = norm_rope(k2.reshape(b, s, C_HEADS, HEAD_DIM), qk_gain[5], cos, sin)
    lam_init = 0.8 - 0.6 * math.exp(-0.3 * layer_idx)
    dl = diff_lambda.astype(F32)
    lam = jnp.exp(jnp.sum(dl[0] * dl[1])) - jnp.exp(jnp.sum(dl[2] * dl[3])) + lam_init
    o_c = diff_attention(q1, q2, k1, k2, vc.reshape(b, s, C_HEADS, C_VDIM), lam)
    o_c = (rms_norm(o_c, diff_subln_gain) * (1.0 - lam_init)).reshape(b, s, C_W)

    merged = (jax.nn.sigmoid(ga) * (o_a @ w_proj_a)
              + jax.nn.sigmoid(gb) * (o_b @ w_proj_b)
              + jax.nn.sigmoid(gc) * (o_c @ w_proj_c))
    return x + merged @ w_out

def hier_moe(xn, w_group, b_group, w_router, b_router, w_e_gate, w_e_up, w_e_down):
    n, d = xn.shape
    xf = xn.astype(F32)
    g_logits = xf @ w_group.astype(F32) + b_group.astype(F32)
    g_prob = jax.nn.softmax(g_logits, axis=-1)
    _, g_idx = lax.top_k(g_logits, 1)
    g_w = jnp.take_along_axis(g_prob, g_idx, axis=1)[:, 0]
    e_logits = (xf @ w_router.astype(F32) + b_router.astype(F32)).reshape(n, N_GROUPS, EXPERTS_PER_GROUP)
    e_logits_g = jnp.take_along_axis(e_logits, g_idx[:, :, None], axis=1)[:, 0]
    e_top, e_idx = lax.top_k(e_logits_g, EXPERT_TOPK)
    weights = g_w[:, None] * jax.nn.softmax(e_top, axis=-1)
    expert = g_idx * EXPERTS_PER_GROUP + e_idx

    n_slots = n * EXPERT_TOPK
    flat_e = expert.reshape(-1)
    flat_tok = jnp.repeat(jnp.arange(n), EXPERT_TOPK)
    flat_w = weights.reshape(-1)
    order = jnp.argsort(flat_e)
    se, st, sw = flat_e[order], flat_tok[order], flat_w[order]
    counts = jax.ops.segment_sum(jnp.ones_like(flat_e), flat_e, num_segments=N_EXPERTS)
    padded = ((counts + MOE_BLOCK - 1) // MOE_BLOCK) * MOE_BLOCK
    start = jnp.cumsum(counts) - counts
    pend = jnp.cumsum(padded)
    pstart = pend - padded
    dest = pstart[se] + (jnp.arange(n_slots) - start[se])
    n_blocks = -(-(n_slots + N_EXPERTS * (MOE_BLOCK - 1)) // MOE_BLOCK)
    rows = n_blocks * MOE_BLOCK
    tok_pad = jnp.zeros((rows,), jnp.int32).at[dest].set(st)
    w_pad = jnp.zeros((rows,), F32).at[dest].set(sw)
    block_expert = jnp.clip(jnp.searchsorted(pend, jnp.arange(n_blocks) * MOE_BLOCK, side='right'),
                            0, N_EXPERTS - 1)
    xb = xn[tok_pad].reshape(n_blocks, MOE_BLOCK, d)

    def block_fn(args):
        xi, e = args
        hid = jax.nn.silu(xi @ w_e_gate[e]) * (xi @ w_e_up[e])
        return hid @ w_e_down[e]

    yb = lax.map(block_fn, (xb, block_expert)).reshape(rows, d)
    contrib = (yb.astype(F32) * w_pad[:, None]).astype(xn.dtype)
    return jnp.zeros((n, d), xn.dtype).at[tok_pad].add(contrib)

def setup_inputs(seed: int = 0) -> dict:
    key = jax.random.key(seed)
    ks = jax.random.split(key, 20)

    def nrm(k, shape, scale):
        return jax.random.normal(k, shape, F32) * scale

    return {
        'x': nrm(ks[0], (BATCH, SEQ, D_MODEL), 1.0),
        'norm_attn': 1.0 + nrm(ks[1], (DEPTH, D_MODEL), 0.02),
        'w_in': nrm(ks[2], (DEPTH, D_MODEL, D_IN), D_MODEL ** -0.5),
        'qk_gain': 1.0 + nrm(ks[3], (DEPTH, 6, HEAD_DIM), 0.02),
        'idx_k_gain': 1.0 + nrm(ks[4], (DEPTH, IDX_DIM), 0.02),
        'diff_lambda': nrm(ks[5], (DEPTH, 4, HEAD_DIM), 0.1),
        'diff_subln_gain': 1.0 + nrm(ks[6], (DEPTH, C_VDIM), 0.02),
        'w_proj_a': nrm(ks[7], (DEPTH, A_W, D_MODEL), A_W ** -0.5),
        'w_proj_b': nrm(ks[8], (DEPTH, B_W, D_MODEL), B_W ** -0.5),
        'w_proj_c': nrm(ks[9], (DEPTH, C_W, D_MODEL), C_W ** -0.5),
        'w_out': nrm(ks[10], (DEPTH, D_MODEL, D_MODEL), D_MODEL ** -0.5),
        'norm_ffn': 1.0 + nrm(ks[11], (DEPTH, D_MODEL), 0.02),
        'w_group': nrm(ks[12], (DEPTH, D_MODEL, N_GROUPS), D_MODEL ** -0.5),
        'b_group': nrm(ks[13], (DEPTH, N_GROUPS), 0.01),
        'w_router': nrm(ks[14], (DEPTH, D_MODEL, N_EXPERTS), D_MODEL ** -0.5),
        'b_router': nrm(ks[15], (DEPTH, N_EXPERTS), 0.01),
        'w_e_gate': nrm(ks[16], (DEPTH, N_EXPERTS, D_MODEL, D_EXPERT), D_MODEL ** -0.5),
        'w_e_up': nrm(ks[17], (DEPTH, N_EXPERTS, D_MODEL, D_EXPERT), D_MODEL ** -0.5),
        'w_e_down': nrm(ks[18], (DEPTH, N_EXPERTS, D_EXPERT, D_MODEL), D_EXPERT ** -0.5),
    }

def reference(x, norm_attn, w_in, qk_gain, idx_k_gain, diff_lambda, diff_subln_gain, w_proj_a,
              w_proj_b, w_proj_c, w_out, norm_ffn, w_group, b_group, w_router, b_router,
              w_e_gate, w_e_up, w_e_down):
    b, s, d = x.shape
    cos, sin = rope_tables(s)
    for l in range(DEPTH):
        x = mixer_sublayer(x, cos, sin, l, norm_attn[l], w_in[l], qk_gain[l], idx_k_gain[l],
                           diff_lambda[l], diff_subln_gain[l], w_proj_a[l], w_proj_b[l],
                           w_proj_c[l], w_out[l])
        hn = rms_norm(x, norm_ffn[l]).reshape(b * s, d)
        x = x + hier_moe(hn, w_group[l], b_group[l], w_router[l], b_router[l],
                         w_e_gate[l], w_e_up[l], w_e_down[l]).reshape(b, s, d)
    return x


_drawn_inputs = setup_inputs


def setup_inputs(seed=0):
    import zlib

    import numpy as np

    out = dict(_drawn_inputs(seed))
    spreads = {}
    factors = {'b_group': 8.101, 'b_router': 2.94}
    for name, (base, spread) in spreads.items():
        noise = np.random.default_rng([zlib.crc32(name.encode()), seed]).standard_normal(out[name].shape)
        drawn = base * np.exp(spread * noise) if base else spread * noise
        out[name] = jnp.asarray(drawn.astype(out[name].dtype))
    for name, factor in factors.items():
        out[name] = (out[name] * factor).astype(out[name].dtype)
    return out
```

```python
from contextlib import ExitStack

import concourse.bass as bass
from concourse import mybir

P = 128
T = 256
NT = T // P
D = 1024
KD = D // P
DEPTH = 2
HD = 64
EPS = 1e-6
SCALE = HD ** -0.5
NHEAD = 4
IDX_HEADS = 8
TOPK = min(256, T // 4)
CV = 2 * HD
NG = 4
EPG = 8
NE = NG * EPG
FE = 512
KF = FE // P
NR = NG + NE
D_IN = 6728
GATES = D_IN - 3 * D
RING = 6
W = 512
FULL = D_IN // W
TAIL = D_IN - FULL * W
QKV = GATES // W
MIX_ROUNDS = 3
PAIRS = NE // 2
SLOTS = 64
NEG = -1e30
TAKEN = -3e38

QA, VA, QB, VB, QI, KI, WI, Q1, VC = 0, 512, 768, 1280, 1536, 2048, 2112, 2120, 3144
GROUPS = [
    (QA, 2, 4, 0, 0, 0),
    (QB, 2, 4, 2, 8, 2),
    (QI, 1, 8, 7, None, 3),
    (KI, 1, 1, 6, 16, 4),
    (Q1, 2, 8, 4, 17, 6),
]
NSUM = 33
NSETS = 8
T_QA, T_KA, T_QB, T_KB, T_QI, T_Q1, T_Q2, T_K1, T_K2, T_KI = 0, 2, 4, 6, 8, 12, 14, 16, 18, 20
T_CHUNKS = [QA + P * k for k in range(4)] + [QB + P * k for k in range(4)] + \
           [QI + P * k for k in range(4)] + [Q1 + P * k for k in range(8)] + [None]
T_BATCH = 4
T_BATCHES = [(t, b) for t in range(NT) for b in range(-(-len(T_CHUNKS) // T_BATCH))]

MAPS = [("idx", t, T_QI + 2 * g, None) for t in range(NT) for g in range(2)]
MAPS += [("A", t, T_QA, T_KA) for t in range(NT)]
MAPS += [(c, t, q, k) for t in range(NT) for c, q, k in (("C1", T_Q1, T_K1), ("C2", T_Q2, T_K2))]
MAPS += [("B", t, T_QB, T_KB) for t in range(NT)]
NIDX = 4
SOFT = len(MAPS) - NIDX
UNIT_OF = {}
for _m, _map in enumerate(MAPS):
    if _map[0] in ("A", "B", "C2"):
        UNIT_OF[_m] = len(UNIT_OF)
UNITS = len(UNIT_OF)
V_OF = {"A": VA, "B": VB, "C2": VC}
O_OF = {"A": 0, "B": 256, "C2": 512}


def trunk(nc, x, norm_attn, w_in, qk_gain, idx_k_gain, diff_lambda, diff_subln_gain, w_proj_a,
          w_proj_b, w_proj_c, w_out, norm_ffn, w_group, b_group, w_router, b_router,
          w_e_gate, w_e_up, w_e_down, c_square, c_rope, c_causal, c_row, c_lam, out):
    F = mybir.dt.float32
    I32 = mybir.dt.int32
    U32 = mybir.dt.uint32
    ALU = mybir.AluOpType
    ACT = mybir.ActivationFunctionType
    AX = mybir.AxisListType

    ctx = ExitStack()
    with ctx:
        def sb(name, shape, dt=F):
            return ctx.enter_context(nc.sbuf_tensor(name, shape, dt))

        def sem(name):
            return ctx.enter_context(nc.semaphore(name))

        ring = [sb(f"ring{k}", [P, KD * W]) for k in range(RING)]
        qkv = sb("qkv", [P, NT, GATES])
        gates = sb("gates", [P, NT, 3 * D])
        xres = sb("xres", [P, NT, D])
        xs = sb("xs", [P, NT, KD, P])
        xs_flat = xs[:, :, :, :].rearrange("q t c p -> q t (c p)")
        hT = sb("hT", [P, KD, T])
        hT_flat = hT[:, :, :].rearrange("q c t -> q (c t)")
        qkT = sb("qkT", [P, len(T_CHUNKS), T])
        qkT_flat = qkT[:, :, :].rearrange("q c t -> q (c t)")
        gcos = qkT_flat[:, 0:1024].rearrange("q (t g d) -> q t g d", t=NT, g=NSETS)
        gsin = qkT_flat[:, 1024:2048].rearrange("q (t g d) -> q t g d", t=NT, g=NSETS)
        gain_b = qkT_flat[:, 2048:2048 + 7 * HD].rearrange("q (g d) -> q g d", g=7)
        oT = qkT_flat[:, 0:KD * T].rearrange("q (j t) -> q j t", j=KD)
        merged = qkT_flat[:, KD * T:2 * KD * T].rearrange("q (t n) -> q t n", t=NT)

        square = sb("square", [P, 3, P])
        ident, tri, ones = square[:, 0, :], square[:, 1, :], square[:, 2, :]
        rope = sb("rope", [P, 2, NT, HD])
        causal = sb("causal", [P, NT, T])
        row = sb("row", [P, 72])
        iota64, limits = row[:, 0:64], row[:, 64:67]
        lamc = sb("lamc", [P, DEPTH, 2])
        ki2 = sb("ki2", [P, NT, 2 * HD])
        g_attn = sb("g_attn", [P, KD])
        g_ffn = sb("g_ffn", [P, KD])
        w_route = sb("w_route", [P, KD, NR])
        b_route = sb("b_route", [P, NR])
        dlam = sb("dlam", [P, 4, HD])
        subln = sb("subln", [P, CV])
        eps = sb("eps", [P, 1])
        ssq = sb("ssq", [P, NT])
        rt = sb("rt", [P, NT])
        rstd = sb("rstd", [P, NT])
        hss = sb("hss", [P, NT, NSUM])
        hrt = sb("hrt", [P, NT, NSUM])
        hrs = sb("hrs", [P, NT, NSUM])
        wis = sb("wis", [P, NT, IDX_HEADS])
        m8 = sb("m8", [P, 8])
        mx = sb("mx", [P, 2, NHEAD])
        nb = sb("nb", [P, 2, NHEAD])
        den = sb("den", [P, 2, NHEAD])
        rden = sb("rden", [P, 2, NHEAD])
        oss = sb("oss", [P, NHEAD])
        ort = sb("ort", [P, NHEAD])
        ors = sb("ors", [P, NHEAD])
        ldot = sb("ldot", [P, 2])
        lexp = sb("lexp", [P, 2])
        nlam = sb("nlam", [P, 1])
        lg = sb("lg", [P, NT, NR])
        gpad = sb("gpad", [P, NT, 8])
        gm8 = sb("gm8", [P, NT, 8])
        gi8 = sb("gi8", [P, NT, 8], U32)
        e8 = sb("e8", [P, NT, 8])
        ei8 = sb("ei8", [P, NT, 8], U32)
        gsub = sb("gsub", [P, NT, NG])
        gexp = sb("gexp", [P, NT, NG])
        gsum = sb("gsum", [P, NT])
        gw = sb("gw", [P, NT])
        gif = sb("gif", [P, NT])
        goh = sb("goh", [P, NT, NG])
        elm = sb("elm", [P, NT, NE])
        eif = sb("eif", [P, NT, 2])
        edif = sb("edif", [P, NT])
        eexp = sb("eexp", [P, NT])
        ew = sb("ew", [P, NT, 2])
        oh1 = sb("oh1", [P, NT, NE])
        oh2 = sb("oh2", [P, NT, NE])
        chosen = sb("chosen", [P, NT, NE])
        rank = sb("rank", [P, NT, NE + 2])
        wt = sb("wt", [P, NT, NE + 2])
        cmax = sb("cmax", [P, 1])
        over = sb("over", [P, 3])
        npf = sb("npf", [P, 1])
        npass = sb("npass", [P, 1], I32)

        sprob = [qkv[:, b, Q1:Q1 + NHEAD * T].rearrange("q (h k) -> q h k", h=NHEAD) for b in range(2)]
        score = [qkv[:, t, QI:QI + T] for t in range(NT)]
        left = [qkv[:, t, QI + T:QI + 2 * T] for t in range(NT)]
        picked = [qkv[:, t, QB:QB + T] for t in range(NT)]
        branch = qkv[:, 0, 0:W]
        probT = [hT_flat[:, 1024 * b:1024 * b + 1024].rearrange("q (k h t) -> q k h t", k=NT, h=NHEAD)
                 for b in range(2)]
        arena = gates[:, :, :].rearrange("q t n -> q (t n)")
        xgT = arena[:, 0:1024].rearrange("q (c s) -> q c s", c=KD)
        sg = arena[:, 1024:1536]
        hid = arena[:, 1536:2048].rearrange("q (c p) -> q c p", c=KF)
        hidT = arena[:, 2048:2560].rearrange("q (c s) -> q c s", c=KF)
        ysb = arena[:, 2560:3584]
        pick = arena[:, 3584:3840].rearrange("q (t s) -> q t s", t=NT)
        pickw = arena[:, 3840:4096].rearrange("q (t s) -> q t s", t=NT)
        pickwT = arena[:, 4096:4352].rearrange("q (t s) -> q t s", t=NT)

        bank = [ctx.enter_context(nc.psum_tensor(f"bank{b}", [P, 512], F)) for b in range(8)]

        consts_in = sem("consts_in")
        smalls_in = sem("smalls_in")
        smalls_free = sem("smalls_free")
        slab_loaded = [sem(f"slab_loaded{k}") for k in range(RING)]
        slab_credit = sem("slab_credit")
        NORMS = 2
        squared = sem("squared")
        rooted = sem("rooted")
        rstd_ready = sem("rstd_ready")
        xs_act = sem("xs_act")
        xs_dve = sem("xs_dve")
        hT_mm = sem("hT_mm")
        hT_ready = sem("hT_ready")
        in_mm = sem("in_mm")
        in_evac = sem("in_evac")
        sums_ready = sem("sums_ready")
        roots_ready = sem("roots_ready")
        rotated = sem("rotated")
        qkT_mm = sem("qkT_mm")
        qkT_act = sem("qkT_act")
        qkT_dve = sem("qkT_dve")
        map_mm = sem("map_mm")
        relu_done = sem("relu_done")
        idx_added = sem("idx_added")
        masked = sem("masked")
        exp_done = sem("exp_done")
        prob_ready = sem("prob_ready")
        probT_mm = sem("probT_mm")
        probT_act = sem("probT_act")
        probT_dve = sem("probT_dve")
        pv_mm = sem("pv_mm")
        o_ready = sem("o_ready")
        oss_ready = sem("oss_ready")
        ort_ready = sem("ort_ready")
        ldot_ready = sem("ldot_ready")
        lexp_ready = sem("lexp_ready")
        oT_mm = sem("oT_mm")
        oT_act = sem("oT_act")
        oT_dve = sem("oT_dve")
        branch_mm = sem("branch_mm")
        merged_ready = sem("merged_ready")
        mT_mm = sem("mT_mm")
        mT_ready = sem("mT_ready")
        out_mm = sem("out_mm")
        x_mixed = sem("x_mixed")
        route_mm = sem("route_mm")
        gsub_ready = sem("gsub_ready")
        gexp_ready = sem("gexp_ready")
        edif_ready = sem("edif_ready")
        eexp_ready = sem("eexp_ready")
        chosen_ready = sem("chosen_ready")
        rank_mm = sem("rank_mm")
        routed = sem("routed")
        pick_ready = sem("pick_ready")
        gather_mm = sem("gather_mm")
        xgT_ready = sem("xgT_ready")
        silu_done = sem("silu_done")
        hid_ready = sem("hid_ready")
        pickwT_mm = sem("pickwT_mm")
        pickwT_ready = sem("pickwT_ready")
        hidT_mm = sem("hidT_mm")
        hidT_act = sem("hidT_act")
        hidT_dve = sem("hidT_dve")
        down_mm = sem("down_mm")
        y_act = sem("y_act")
        y_dve = sem("y_dve")
        combined = sem("combined")
        x_act = sem("x_act")
        x_dve = sem("x_dve")
        stored = sem("stored")
        past_wait = sem("past_wait")
        SMALLS = 10

        x_view = x.rearrange("b (t p) d -> p (b t) d", p=P)
        out_view = out.rearrange("b (t p) d -> p (b t) d", p=P)

        def counters(eng, tag):
            rounds, passes = eng.alloc_register(f"rounds_{tag}"), eng.alloc_register(f"passes_{tag}")
            eng.reg_mov(rounds, 0)
            eng.reg_mov(passes, 0)
            return rounds, passes

        def counts(eng, rounds, passes):
            return (eng.snap(rounds, min_val=0, max_val=DEPTH * (MIX_ROUNDS + 4 * PAIRS)),
                    eng.snap(passes, min_val=0, max_val=4 * DEPTH))

        def wait_apart(eng, signal, value):
            eng.wait_ge(signal, value)
            eng.sem_inc(past_wait, 1)

        def count_on(eng, rounds, passes, n):
            eng.reg_add(rounds, rounds, n * PAIRS + MIX_ROUNDS)
            eng.reg_add(passes, passes, n)

        block = ctx.enter_context(nc.Block())

        @block.sync
        def _(sp):
            sp.dma_start(xres[:, :, :], x_view).then_inc(consts_in, 16)
            sp.dma_start(square[:, :, :], c_square).then_inc(consts_in, 16)
            sp.dma_start(rope[:, :, :, :], c_rope).then_inc(consts_in, 16)
            sp.dma_start(causal[:, :, :], c_causal).then_inc(consts_in, 16)
            sp.dma_start(row[:, :], c_row).then_inc(consts_in, 16)
            sp.dma_start(lamc[:, :, :], c_lam).then_inc(consts_in, 16)
            rounds, passes = counters(sp, "sp")

            with sp.Fori(0, DEPTH) as L:
                r0, p0 = counts(sp, rounds, passes)
                sp.wait_ge(smalls_free, L + 1)
                sp.dma_start(g_attn[:, :], norm_attn[L, :].rearrange("(p c) -> p c", c=KD)).then_inc(smalls_in, 16)
                sp.dma_start(g_ffn[:, :], norm_ffn[L, :].rearrange("(p c) -> p c", c=KD)).then_inc(smalls_in, 16)
                sp.dma_start(gain_b[:, 0:6, :].rearrange("q g d -> q (g d)"),
                             qk_gain[L, :, :].rearrange("g d -> (g d)").partition_broadcast(P)).then_inc(smalls_in, 16)
                sp.dma_start(gain_b[:, 6, :], idx_k_gain[L, :].partition_broadcast(P)).then_inc(smalls_in, 16)
                sp.dma_start(dlam[:, :, :].rearrange("q g d -> q (g d)"),
                             diff_lambda[L, :, :].rearrange("g d -> (g d)").partition_broadcast(P)).then_inc(smalls_in, 16)
                sp.dma_start(subln[:, :], diff_subln_gain[L, :].partition_broadcast(P)).then_inc(smalls_in, 16)
                sp.dma_start(w_route[:, :, 0:NG], w_group[L, :, :].rearrange("(p c) n -> p c n", c=KD)).then_inc(smalls_in, 16)
                sp.dma_start(w_route[:, :, NG:NR], w_router[L, :, :].rearrange("(p c) n -> p c n", c=KD)).then_inc(smalls_in, 16)
                sp.dma_start(b_route[:, 0:NG], b_group[L, :].partition_broadcast(P)).then_inc(smalls_in, 16)
                sp.dma_start(b_route[:, NG:NR], b_router[L, :].partition_broadcast(P)).then_inc(smalls_in, 16)

                w_in_v = w_in[L, :, :].rearrange("(p c) n -> p c n", c=KD)
                with sp.Fori(0, FULL // RING) as r:
                    for k in range(RING):
                        sp.wait_ge(slab_credit, 6 * (r0 + r) + k + 1)
                        sp.dma_start(ring[k][:, :].rearrange("q (c n) -> q c n", c=KD),
                                     w_in_v[:, :, bass.ds((r * RING + k) * W, W)]).then_inc(slab_loaded[k], 16)
                sp.wait_ge(slab_credit, 6 * (r0 + 2) + 1)
                sp.dma_start(ring[0][:, :].rearrange("q (c n) -> q c n", c=KD),
                             w_in_v[:, :, (FULL - 1) * W:FULL * W]).then_inc(slab_loaded[0], 16)
                sp.wait_ge(slab_credit, 6 * (r0 + 2) + 2)
                sp.dma_start(ring[1][:, 0:KD * TAIL].rearrange("q (c n) -> q c n", c=KD),
                             w_in_v[:, :, FULL * W:D_IN]).then_inc(slab_loaded[1], 16)
                for h in range(2):
                    sp.wait_ge(slab_credit, 6 * (r0 + 2) + 3 + h)
                    slab = ring[2 + h][:, :].rearrange("q (c n) -> q c n", c=KD)
                    for w, a, b in ((w_proj_a, 0, 2), (w_proj_b, 2, 4), (w_proj_c, 4, 8)):
                        sp.dma_start(slab[:, a:b, :],
                                     w[L, :, :].rearrange("(c p) n -> p c n", p=P)[:, :, h * W:h * W + W]).then_inc(slab_loaded[2 + h], 16)
                for h in range(2):
                    sp.wait_ge(slab_credit, 6 * (r0 + 2) + 5 + h)
                    sp.dma_start(ring[4 + h][:, :].rearrange("q (c n) -> q c n", c=KD),
                                 w_out[L, :, :].rearrange("(c p) n -> p c n", p=P)[:, :, h * W:h * W + W]).then_inc(slab_loaded[4 + h], 16)

                def load_pair(g, i):
                    for k in range(RING):
                        w = (w_e_gate, w_e_up, w_e_down)[k // 2]
                        sp.wait_ge(slab_credit, 6 * g + k + 1)
                        sp.dma_start(ring[k][:, :], w[L, 2 * i + k % 2, :, :].rearrange("(p c) n -> p (c n)", p=P)).then_inc(slab_loaded[k], 16)

                with sp.Fori(0, PAIRS) as i:
                    load_pair(r0 + MIX_ROUNDS + i, i)
                wait_apart(sp, routed, L + 1)
                n = sp.value_load(npass[0:1, 0:1], min_val=1, max_val=4)
                with sp.If(n > 1):
                    with sp.Fori(1, n) as more:
                        with sp.Fori(0, PAIRS) as i:
                            load_pair(r0 + MIX_ROUNDS + more * PAIRS + i, i)
                count_on(sp, rounds, passes, n)

            sp.wait_ge(x_act, DEPTH)
            sp.wait_ge(x_dve, DEPTH + 1)
            sp.dma_start(out_view, xres[:, :, :]).then_inc(stored, 16)
            sp.wait_ge(stored, 16)

        @block.tensor
        def _(pe):
            pe.sem_inc(slab_credit, RING)
            pe.wait_ge(consts_in, 96)
            rounds, passes = counters(pe, "pe")

            with pe.Fori(0, DEPTH) as L:
                r0, p0 = counts(pe, rounds, passes)

                def wait_slab(k, g, proj):
                    pe.wait_ge(slab_loaded[k], 16 * (g + 1 + (2 * proj if k in (2, 3) else 0)))

                def transpose_x(n):
                    for t in range(NT):
                        pe.wait_ge((xs_act, xs_dve)[t], NORMS * L + n + 1)
                        for h in range(2):
                            for c in range(4):
                                mm = nc.tensor.transpose(bank[4 + 2 * t + h][:, P * c:P * c + P], xs[:, t, 4 * h + c, :], ident)
                            mm.then_inc(hT_mm, 1)

                transpose_x(0)
                wait_apart(pe, hT_ready, 4 * (NORMS * L + 1))

                def project(k, s, g, w):
                    wait_slab(k, g, L)
                    slab = ring[k][:, 0:KD * w].rearrange("q (c n) -> q c n", c=KD)
                    for t in range(NT):
                        pe.wait_ge(in_evac, NT * ((FULL + 1) * L + s) + t + 1)
                        for c in range(KD):
                            mm = nc.tensor.matmul(bank[2 * (k % 2) + t][:, 0:w], hT[:, c, P * t:P * t + P], slab[:, c, :],
                                                  start=c == 0, stop=c == KD - 1)
                        mm.then_inc((in_mm, slab_credit)[t], 1)

                with pe.Fori(0, FULL // RING) as r:
                    for k in range(RING):
                        project(k, r * RING + k, r0 + r, W)
                project(0, FULL - 1, r0 + 2, W)
                project(1, FULL, r0 + 2, TAIL)

                pe.wait_ge(rotated, L + 1)
                for n, (t, b) in enumerate(T_BATCHES):
                    if n >= 4:
                        pe.wait_ge((qkT_act, qkT_dve)[n % 2], 6 * L + (n - 4) // 2 + 1)
                    batch = T_CHUNKS[T_BATCH * b:T_BATCH * b + T_BATCH]
                    for j, col in enumerate(batch):
                        src = ki2[:, t, :] if col is None else qkv[:, t, col:col + P]
                        mm = nc.tensor.transpose(bank[4 + n % 4][:, P * j:P * j + P], src, ident)
                    mm.then_inc(qkT_mm, 1)
                pe.wait_ge(qkT_act, 6 * L + 6)
                pe.wait_ge(qkT_dve, 6 * L + 6)

                def scores(m):
                    kind, t, tq, tk = MAPS[m]
                    if m < 2:
                        pe.wait_ge(in_evac, NT * ((FULL + 1) * L + FULL + 1) + 2 * NT)
                    elif m - 2 < NIDX:
                        pe.wait_ge(relu_done, NIDX * L + m - 1)
                    else:
                        pe.wait_ge(masked, SOFT * L + m - 1 - NIDX)
                    nk = P * (t + 1)
                    for h in range(NHEAD):
                        a = HD * (h % 2)
                        k = T_KI if tk is None else tk + h // 2
                        mm = nc.tensor.matmul(bank[2 * (m % 2) + h % 2][:, T * (h // 2):T * (h // 2) + nk],
                                              qkT[a:a + HD, tq + h // 2, P * t:P * t + P], qkT[a:a + HD, k, 0:nk],
                                              start=True, stop=True)
                    mm.then_inc(map_mm, 1)

                def values(m):
                    kind, t, _, _ = MAPS[m]
                    u = UNIT_OF[m]
                    src = sprob[(m - 1) % 2 if kind == "C2" else m % 2]
                    if kind == "C2":
                        pe.wait_ge(prob_ready, 2 * L + t + 1)
                    else:
                        pe.wait_ge(exp_done, SOFT * L + m - NIDX + 1)
                    for b in range(t + 1):
                        for h in range(NHEAD):
                            mm = nc.tensor.transpose(bank[4 + b][:, P * h:P * h + P], src[:, h, P * b:P * b + P], ident)
                        mm.then_inc(probT_mm, 1)
                    pe.wait_ge(probT_act, UNITS * L + u + 1)
                    if t == 1:
                        pe.wait_ge(probT_dve, 3 * L + u // 2 + 1)
                    if u >= 2:
                        pe.wait_ge(o_ready, UNITS * L + u - 1)
                    dv = CV if kind == "C2" else HD
                    for h in range(NHEAD):
                        for b in range(t + 1):
                            mm = nc.tensor.matmul(bank[6 + u % 2][:, dv * h:dv * h + dv], probT[u % 2][:, b, h, :],
                                                  qkv[:, b, V_OF[kind] + dv * h:V_OF[kind] + dv * h + dv],
                                                  start=b == 0, stop=b == t)
                    mm.then_inc(pv_mm, 1)

                scores(0)
                for m in range(len(MAPS)):
                    if m + 1 < len(MAPS):
                        scores(m + 1)
                    if m in UNIT_OF:
                        values(m)

                pe.wait_ge(o_ready, UNITS * (L + 1))
                for t in range(NT):
                    for h in range(2):
                        for j in range(4):
                            mm = nc.tensor.transpose(bank[4 + 2 * t + h][:, P * j:P * j + P], xs[:, t, 4 * h + j, :], ident)
                        mm.then_inc(oT_mm, 1)
                pe.wait_ge(oT_act, 2 * (L + 1))
                pe.wait_ge(oT_dve, 2 * (L + 1))

                for n in range(4):
                    h, t = n // 2, n % 2
                    if t == 0:
                        wait_slab(2 + h, r0 + 2, L + 1)
                    if n >= 2:
                        pe.wait_ge(merged_ready, 4 * L + n - 1)
                    for b, (j0, j1) in enumerate(((0, 2), (2, 4), (4, 8))):
                        for j in range(j0, j1):
                            mm = nc.tensor.matmul(bank[3 * (n % 2) + b][:, :], oT[:, j, P * t:P * t + P],
                                                  ring[2 + h][:, W * j:W * j + W], start=j == j0, stop=j == j1 - 1)
                    mm.then_inc((branch_mm, slab_credit)[t], 1)

                for n in range(4):
                    h, t = n // 2, n % 2
                    pe.wait_ge(merged_ready, 4 * L + n + 1)
                    if n >= 2:
                        pe.wait_ge(mT_ready, 4 * L + n - 1)
                    for j in range(4):
                        mm = nc.tensor.transpose(bank[6 + n % 2][:, P * j:P * j + P],
                                                 merged[:, t, W * h + P * j:W * h + P * j + P], ident)
                    mm.then_inc(mT_mm, 1)
                pe.wait_ge(mT_ready, 4 * L + 4)
                for n in range(4):
                    h, t = n // 2, n % 2
                    if t == 0:
                        wait_slab(4 + h, r0 + 2, L)
                    for c in range(KD):
                        mm = nc.tensor.matmul(bank[n][:, :], hT[:, c, P * t:P * t + P], ring[4 + h][:, W * c:W * c + W],
                                              start=c == 0, stop=c == KD - 1)
                    mm.then_inc((out_mm, slab_credit)[t], 1)

                transpose_x(1)
                pe.wait_ge(hT_ready, 4 * (NORMS * L + 2))
                for t in range(NT):
                    for c in range(KD):
                        mm = nc.tensor.matmul(bank[4][:, NR * t:NR * t + NR], hT[:, c, P * t:P * t + P], w_route[:, c, :],
                                              start=c == 0, stop=c == KD - 1)
                mm.then_inc(route_mm, 1)
                pe.wait_ge(x_mixed, 4 * L + 4)
                for t in range(NT):
                    for h in range(2):
                        nc.tensor.matmul(bank[2 * t + h][:, :], ident, xres[:, t, W * h:W * h + W], start=True, stop=True)
                pe.wait_ge(chosen_ready, L + 1)
                nc.tensor.matmul(bank[5][:, 0:NE], tri, chosen[:, 0, :], start=True, stop=True)
                nc.tensor.matmul(bank[5][:, NE:2 * NE], ones, chosen[:, 0, :], start=True, stop=False)
                nc.tensor.matmul(bank[5][:, NE:2 * NE], tri, chosen[:, 1, :], start=False, stop=True)
                nc.tensor.matmul(bank[5][:, 2 * NE:3 * NE], ones, chosen[:, 0, :], start=True, stop=False)
                nc.tensor.matmul(bank[5][:, 2 * NE:3 * NE], ones, chosen[:, 1, :], start=False, stop=True).then_inc(rank_mm, 1)

                wait_apart(pe, routed, L + 1)
                n_pass = pe.value_load(npass[0:1, 0:1], min_val=1, max_val=4)
                with pe.Fori(0, n_pass) as ps:
                    with pe.Fori(0, PAIRS) as i:
                        pairs = pe.snap((p0 + ps) * PAIRS + i)
                        g = pe.snap(r0 + MIX_ROUNDS + ps * PAIRS + i)
                        pe.wait_ge(pick_ready, (p0 + ps) * (PAIRS + 1) + i + 1)
                        for c in range(KD):
                            for t in range(NT):
                                mm = nc.tensor.matmul(bank[6 + c // 4][:, P * (c % 4):P * (c % 4) + P], xs[:, t, c, :], pick[:, t, :],
                                                      start=t == 0, stop=t == NT - 1)
                            if c % 4 == 3:
                                mm.then_inc(gather_mm, 1)
                        for m in range(2):
                            for e in range(2):
                                wait_slab(2 * m + e, g, L + 1)
                            for c in range(KD):
                                if m == 0 and c % 4 == 0:
                                    pe.wait_ge(xgT_ready, 2 * pairs + c // 4 + 1)
                                for e in range(2):
                                    mm = nc.tensor.matmul(bank[4 + m][SLOTS * e:SLOTS * e + SLOTS, :], xgT[:, c, SLOTS * e:SLOTS * e + SLOTS],
                                                          ring[2 * m + e][:, W * c:W * c + W], start=c == 0, stop=c == KD - 1)
                                    if c == KD - 1:
                                        mm.then_inc(slab_credit, 1)
                        for t in range(NT):
                            mm = nc.tensor.transpose(bank[6][:, P * t:P * t + P], pickw[:, t, :], ident)
                        mm.then_inc(pickwT_mm, 1)
                        pe.wait_ge(hid_ready, pairs + 1)
                        for c in range(KF):
                            mm = nc.tensor.transpose(bank[4 + c // 2][:, P * (c % 2):P * (c % 2) + P], hid[:, c, :], ident)
                            if c % 2 == 1:
                                mm.then_inc(hidT_mm, 1)
                        for e in range(2):
                            wait_slab(4 + e, g, L + 1)
                        pe.wait_ge(hidT_act, pairs + 1)
                        for h in range(2):
                            if h == 1:
                                pe.wait_ge(pickwT_ready, pairs + 1)
                            for c in range(KF):
                                if h == 0 and c == 2:
                                    pe.wait_ge(hidT_dve, pairs + 1)
                                for e in range(2):
                                    mm = nc.tensor.matmul(bank[7 - h][SLOTS * e:SLOTS * e + SLOTS, :], hidT[:, c, SLOTS * e:SLOTS * e + SLOTS],
                                                          ring[4 + e][:, D * c + W * h:D * c + W * h + W], start=c == 0, stop=c == KF - 1)
                                    if c == KF - 1 and h == 0 and e == 1:
                                        mm.then_inc(down_mm, 1)
                                    if c == KF - 1 and h == 1:
                                        mm.then_inc(slab_credit, 1)
                        for h in range(2):
                            pe.wait_ge((y_act, y_dve)[h], pairs + 1)
                            for t in range(NT):
                                mm = nc.tensor.matmul(bank[2 * t + h][:, :], pickwT[:, t, :], ysb[:, W * h:W * h + W],
                                                      start=False, stop=True, skip_group_check=True)
                        mm.then_inc(combined, 1)
                count_on(pe, rounds, passes, n_pass)

        @block.scalar
        def _(act):
            act.sem_inc(in_evac, 2 * NT)
            act.wait_ge(consts_in, 96)
            rounds, passes = counters(act, "act")

            with act.Fori(0, DEPTH) as L:
                r0, p0 = counts(act, rounds, passes)

                def norm(n):
                    for t in range(NT):
                        nc.scalar.activation(xs_flat[:, t, :], xres[:, t, :], ACT.Square, accum_out=ssq[:, t:t + 1]).then_inc(squared, 1)
                    act.wait_ge(squared, NT * (NORMS * L + n + 1))
                    nc.scalar.activation(rt[:, :], ssq[:, :], ACT.Sqrt, bias=eps[:, 0:1], scale=1.0 / D).then_inc(rooted, 1)
                    act.wait_ge(rstd_ready, NORMS * L + n + 1)
                    nc.scalar.activation(xs[:, 0, :, :].rearrange("q c p -> q p c"), xres[:, 0, :].rearrange("q (p c) -> q p c", c=KD),
                                         ACT.Copy, scale=rstd[:, 0:1]).then_inc(xs_act, 1)

                act.wait_ge(x_dve, L + 1)
                norm(0)

                for s in range(FULL + 1):
                    w = W if s < FULL else TAIL
                    for t in range(NT):
                        if t == 0:
                            act.wait_ge(in_mm, (FULL + 1) * L + s + 1)
                        else:
                            act.wait_ge(slab_credit, 6 * r0 + RING + s + 1)
                        src = bank[2 * (s % 2) + t]
                        if s < QKV:
                            nc.scalar.activation(qkv[:, t, W * s:W * s + w], src[:, 0:w], ACT.Copy).then_inc(in_evac, 1)
                        elif s == QKV:
                            v = GATES - QKV * W
                            nc.scalar.activation(qkv[:, t, W * s:GATES], src[:, 0:v], ACT.Copy)
                            nc.scalar.activation(gates[:, t, 0:W - v], src[:, v:W], ACT.Sigmoid).then_inc(in_evac, 1)
                        else:
                            nc.scalar.activation(gates[:, t, W * s - GATES:W * s - GATES + w], src[:, 0:w], ACT.Sigmoid).then_inc(in_evac, 1)
                    for n, (_, _, _, _, h0, last) in enumerate([q for q in GROUPS if q[4] is not None]):
                        if last + 1 == s:
                            nh = (8, 8, 1, 16)[n]
                            act.wait_ge(sums_ready, 4 * L + n + 1)
                            nc.scalar.activation(hrt[:, :, h0:h0 + nh], hss[:, :, h0:h0 + nh], ACT.Sqrt,
                                                 bias=eps[:, 0:1], scale=1.0 / HD).then_inc(roots_ready, 1)

                for n, (t, b) in enumerate(T_BATCHES):
                    if n % 2 == 0:
                        act.wait_ge(qkT_mm, 12 * L + n + 1)
                        k = len(T_CHUNKS[T_BATCH * b:T_BATCH * b + T_BATCH])
                        nc.scalar.activation(qkT[:, T_BATCH * b:T_BATCH * b + k, P * t:P * t + P],
                                             bank[4 + n % 4][:, 0:P * k].rearrange("q (j s) -> q j s", j=k), ACT.Copy).then_inc(qkT_act, 1)

                act.wait_ge(ldot_ready, L + 1)
                nc.scalar.activation(lexp[:, :], ldot[:, :], ACT.Exp).then_inc(lexp_ready, 1)

                def probabilities_out(m):
                    u = UNIT_OF[m]
                    act.wait_ge(probT_mm, 9 * L + (3 * u) // 2 + 1)
                    nc.scalar.activation(probT[u % 2][:, 0, :, :].rearrange("q h t -> q (h t)"), bank[4][:, :], ACT.Copy).then_inc(probT_act, 1)

                for m, (kind, t, _, _) in enumerate(MAPS):
                    nk = P * (t + 1)
                    dst = sprob[m % 2]
                    if kind == "idx":
                        act.wait_ge(map_mm, len(MAPS) * L + m + 1)
                        if m >= 2:
                            act.wait_ge(idx_added, NIDX * L + m - 1)
                        for b in range(2):
                            mm = nc.scalar.activation(dst[:, b:NHEAD:2, 0:nk],
                                                      bank[2 * (m % 2) + b][:, :].rearrange("q (h k) -> q h k", h=2)[:, :, 0:nk],
                                                      ACT.Relu, scale=SCALE)
                        mm.then_inc(relu_done, 1)
                        continue
                    act.wait_ge(masked, SOFT * L + m - NIDX + 1)
                    for h in range(NHEAD):
                        mm = nc.scalar.activation(dst[:, h, 0:nk], dst[:, h, 0:nk], ACT.Exp, bias=nb[:, m % 2, h:h + 1],
                                                  scale=SCALE, accum_out=den[:, m % 2, h:h + 1])
                    mm.then_inc(exp_done, 1)
                    if m in UNIT_OF:
                        probabilities_out(m)
                    if kind == "C2":
                        act.wait_ge(oss_ready, 2 * L + t + 1)
                        nc.scalar.activation(ort[:, :], oss[:, :], ACT.Sqrt, bias=eps[:, 0:1], scale=1.0 / CV).then_inc(ort_ready, 1)

                for t in range(NT):
                    act.wait_ge(oT_mm, 4 * L + 2 * t + 1)
                    nc.scalar.activation(oT[:, 0:4, P * t:P * t + P], bank[4 + 2 * t][:, :].rearrange("q (j s) -> q j s", j=4), ACT.Copy).then_inc(oT_act, 1)

                act.wait_ge(x_mixed, 4 * L + 4)
                norm(1)
                act.wait_ge(gsub_ready, L + 1)
                nc.scalar.activation(gexp[:, :, :], gsub[:, :, :], ACT.Exp).then_inc(gexp_ready, 1)
                act.wait_ge(edif_ready, L + 1)
                nc.scalar.activation(eexp[:, :], edif[:, :], ACT.Exp).then_inc(eexp_ready, 1)

                wait_apart(act, routed, L + 1)
                n_pass = act.value_load(npass[0:1, 0:1], min_val=1, max_val=4)
                with act.Fori(0, n_pass) as ps:
                    with act.Fori(0, PAIRS) as i:
                        pairs = act.snap((p0 + ps) * PAIRS + i)
                        act.wait_ge(slab_credit, 6 * (r0 + MIX_ROUNDS + ps * PAIRS + i) + RING + 2)
                        nc.scalar.activation(sg, bank[4][:, :], ACT.Silu).then_inc(silu_done, 1)
                        act.wait_ge(pickwT_mm, pairs + 1)
                        nc.scalar.activation(pickwT.rearrange("q t s -> q (t s)"), bank[6][:, 0:T], ACT.Copy).then_inc(pickwT_ready, 1)
                        act.wait_ge(hidT_mm, 2 * pairs + 1)
                        nc.scalar.activation(hidT[:, 0:2, :].rearrange("q c s -> q (c s)"), bank[4][:, 0:2 * P], ACT.Copy).then_inc(hidT_act, 1)
                        act.wait_ge(down_mm, pairs + 1)
                        nc.scalar.activation(ysb[:, 0:W], bank[7][:, :], ACT.Copy).then_inc(y_act, 1)
                act.wait_ge(combined, (p0 + n_pass) * PAIRS)
                nc.scalar.activation(xres[:, 0, 0:W], bank[0][:, :], ACT.Copy)
                nc.scalar.activation(xres[:, 0, W:D], bank[1][:, :], ACT.Copy).then_inc(x_act, 1)
                act.wait_ge(x_act, L + 1)
                count_on(act, rounds, passes, n_pass)

        @block.vector
        def _(dve):
            v = nc.vector
            dve.sem_inc(smalls_free, 1)
            v.memset(eps[:, :], EPS)
            v.memset(gpad[:, :, :], NEG)
            v.memset(rank[:, :, :], -1.0)
            v.memset(wt[:, :, :], 0.0)
            dve.drain()
            dve.wait_ge(consts_in, 96)
            dve.sem_inc(x_dve, 1)
            rounds, passes = counters(dve, "dve")

            with dve.Fori(0, DEPTH) as L:
                r0, p0 = counts(dve, rounds, passes)
                dve.wait_ge(smalls_in, 16 * SMALLS * (L + 1))

                def norm(n, gain):
                    dve.wait_ge(rooted, NORMS * L + n + 1)
                    v.reciprocal(rstd[:, :], rt[:, :]).then_inc(rstd_ready, 1)
                    dve.drain()
                    v.tensor_scalar(xs[:, 1, :, :].rearrange("q c p -> q p c"), xres[:, 1, :].rearrange("q (p c) -> q p c", c=KD),
                                    rstd[:, 1:2], None, ALU.mult).then_inc(xs_dve, 1)
                    for t in range(NT):
                        for h in range(2):
                            dve.wait_ge(hT_mm, 4 * (NORMS * L + n) + 2 * t + h + 1)
                            v.tensor_tensor(hT[:, 4 * h:4 * h + 4, P * t:P * t + P],
                                            bank[4 + 2 * t + h][:, :].rearrange("q (c s) -> q c s", c=4),
                                            gain[:, 4 * h:4 * h + 4].unsqueeze(2).broadcast_to([P, 4, P]), ALU.mult).then_inc(hT_ready, 1)

                norm(0, g_attn)

                H = HD // 2
                for t in range(NT):
                    v.tensor_tensor(gcos[:, t, 0:7, :], gain_b[:, :, :], rope[:, 0, t, :].unsqueeze(1).broadcast_to([P, 7, HD]), ALU.mult)
                    for a, b in ((0, H), (H, 0)):
                        v.tensor_tensor(gsin[:, t, 0:7, a:a + H], gain_b[:, :, b:b + H],
                                        rope[:, 1, t, a:a + H].unsqueeze(1).broadcast_to([P, 7, H]), ALU.mult)
                    v.tensor_copy(gcos[:, t, 7, :], rope[:, 0, t, :])
                    v.tensor_copy(gsin[:, t, 7, :], rope[:, 1, t, :])
                for n in range(2):
                    v.tensor_tensor_reduce(xs_flat[:, n, 0:HD], dlam[:, 2 * n, :], dlam[:, 2 * n + 1, :], 1.0, 0.0, ALU.mult, ALU.add,
                                           ldot[:, n:n + 1])
                dve.drain()
                dve.sem_inc(ldot_ready, 1)

                n = 0
                for col, sets, per, set0, h0, last in GROUPS:
                    nh = sets * per
                    wait_apart(dve, in_evac, NT * ((FULL + 1) * L + last + 1) + 2 * NT)
                    if h0 is not None:
                        for t in range(NT):
                            dve.drain()
                            v.tensor_tensor(xs_flat[:, t, 0:HD * nh], qkv[:, t, col:col + HD * nh], qkv[:, t, col:col + HD * nh], ALU.mult)
                        dve.drain()
                        for t in range(NT):
                            v.tensor_reduce(hss[:, t, h0:h0 + nh], xs_flat[:, t, 0:HD * nh].rearrange("q (h d) -> q h d", h=nh), AX.X, ALU.add)
                        dve.drain()
                        dve.sem_inc(sums_ready, 1)
                        dve.wait_ge(roots_ready, 4 * L + n + 1)
                        n += 1
                        v.reciprocal(hrs[:, :, h0:h0 + nh], hrt[:, :, h0:h0 + nh])
                        dve.drain()
                        for t in range(NT):
                            q = qkv[:, t, col:col + HD * nh].rearrange("q (h d) -> q h d", h=nh)
                            v.tensor_tensor(q, q, hrs[:, t, h0:h0 + nh].unsqueeze(2).broadcast_to([P, nh, HD]), ALU.mult)
                    for t in range(NT):
                        dve.drain()
                        q = qkv[:, t, col:col + HD * nh].rearrange("q (g h d) -> q g h d", g=sets, h=per)
                        a = xs_flat[:, 0, 0:HD * nh].rearrange("q (g h d) -> q g h d", g=sets, h=per)
                        b = xs_flat[:, 1, 0:HD * nh].rearrange("q (g h d) -> q g h d", g=sets, h=per)
                        v.tensor_tensor(a, q, gcos[:, t, set0:set0 + sets, :].unsqueeze(2).broadcast_to([P, sets, per, HD]), ALU.mult)
                        for d0, d1 in ((0, H), (H, 0)):
                            v.tensor_tensor(b[:, :, :, d0:d0 + H], q[:, :, :, d1:d1 + H],
                                            gsin[:, t, set0:set0 + sets, d0:d0 + H].unsqueeze(2).broadcast_to([P, sets, per, H]), ALU.mult)
                        dve.drain()
                        if col == KI:
                            for b2 in range(2):
                                v.tensor_tensor(ki2[:, t, HD * b2:HD * b2 + HD], xs_flat[:, 0, 0:HD], xs_flat[:, 1, 0:HD], ALU.add)
                        else:
                            v.tensor_tensor(qkv[:, t, col:col + HD * nh], xs_flat[:, 0, 0:HD * nh], xs_flat[:, 1, 0:HD * nh], ALU.add)
                for t in range(NT):
                    v.tensor_scalar(wis[:, t, :], qkv[:, t, WI:WI + IDX_HEADS], IDX_HEADS ** -0.5, None, ALU.mult)
                dve.drain()
                dve.sem_inc(rotated, 1)

                for n, (t, b) in enumerate(T_BATCHES):
                    if n % 2 == 1:
                        dve.wait_ge(qkT_mm, 12 * L + n + 1)
                        k = len(T_CHUNKS[T_BATCH * b:T_BATCH * b + T_BATCH])
                        v.tensor_copy(qkT[:, T_BATCH * b:T_BATCH * b + k, P * t:P * t + P],
                                      bank[4 + n % 4][:, 0:P * k].rearrange("q (j s) -> q j s", j=k)).then_inc(qkT_dve, 1)

                dve.wait_ge(lexp_ready, L + 1)
                v.tensor_tensor(nlam[:, :], lexp[:, 1:2], lexp[:, 0:1], ALU.subtract)
                dve.drain()
                v.tensor_tensor(nlam[:, :], nlam[:, :], lamc[:, bass.ds(L, 1), 0:1].rearrange("q a b -> q (a b)"), ALU.subtract)
                v.tensor_tensor(subln[:, :], subln[:, :], lamc[:, bass.ds(L, 1), 1:2].rearrange("q a b -> q (a b)").broadcast_to([P, CV]), ALU.mult)
                dve.drain()

                for m in range(NIDX):
                    _, t, _, _ = MAPS[m]
                    nk = P * (t + 1)
                    dve.wait_ge(relu_done, NIDX * L + m + 1)
                    for h in range(NHEAD):
                        wcol = wis[:, t, NHEAD * (m % 2) + h:NHEAD * (m % 2) + h + 1]
                        if m % 2 == 0 and h == 0:
                            v.tensor_scalar(score[t][:, 0:nk], sprob[m % 2][:, h, 0:nk], wcol, None, ALU.mult)
                        else:
                            v.scalar_tensor_tensor(out=score[t][:, 0:nk], in0=sprob[m % 2][:, h, 0:nk], scalar=wcol, in1=score[t][:, 0:nk],
                                                   op0=ALU.mult, op1=ALU.add)
                        dve.drain()
                    dve.sem_inc(idx_added, 1)

                def select(t):
                    nk = P * (t + 1)
                    v.tensor_tensor(left[t][:, 0:nk], score[t][:, 0:nk], causal[:, t, 0:nk], ALU.add)
                    dve.drain()
                    for _ in range(TOPK // 8):
                        v.max(m8[:, :], left[t][:, 0:nk])
                        dve.drain()
                        v.match_replace(left[t][:, 0:nk], m8[:, :], left[t][:, 0:nk], TAKEN)
                        dve.drain()
                    v.tensor_scalar(picked[t][:, 0:nk], left[t][:, 0:nk], 2 * NEG, NEG, ALU.is_gt, ALU.mult)
                    dve.drain()
                    v.tensor_tensor(picked[t][:, 0:nk], picked[t][:, 0:nk], causal[:, t, 0:nk], ALU.add)
                    dve.drain()

                def mask(m):
                    kind, t, _, _ = MAPS[m]
                    nk = P * (t + 1)
                    add = picked[t] if kind == "B" else causal[:, t, :]
                    dve.wait_ge(map_mm, len(MAPS) * L + m + 1)
                    if m >= 2 and MAPS[m - 1][0] == "C2":
                        u = UNIT_OF[m - 1]
                        dve.wait_ge(probT_mm, 9 * L + (3 * (u + 1)) // 2)
                    dve.sem_inc(past_wait, 1)
                    for h in range(NHEAD):
                        v.tensor_tensor_reduce(sprob[m % 2][:, h, 0:nk], bank[2 * (m % 2) + h % 2][:, T * (h // 2):T * (h // 2) + nk],
                                               add[:, 0:nk], 1.0, NEG, ALU.add, ALU.max, mx[:, m % 2, h:h + 1])
                    dve.drain()
                    v.tensor_scalar(nb[:, m % 2, :], mx[:, m % 2, :], -SCALE, None, ALU.mult).then_inc(masked, 1)

                def probabilities_out(m):
                    u = UNIT_OF[m]
                    if MAPS[m][1] == 1:
                        dve.wait_ge(probT_mm, 9 * L + (3 * (u + 1)) // 2)
                        v.tensor_copy(probT[u % 2][:, 1, :, :].rearrange("q h t -> q (h t)"), bank[5][:, :]).then_inc(probT_dve, 1)

                def finish(m):
                    kind, t, _, _ = MAPS[m]
                    u = UNIT_OF[m]
                    dve.wait_ge(pv_mm, UNITS * L + u + 1)
                    dst = xs_flat[:, t, O_OF[kind]:O_OF[kind] + (512 if kind == "C2" else 256)].rearrange("q (h d) -> q h d", h=NHEAD)
                    if kind != "C2":
                        v.tensor_tensor(dst, bank[6 + u % 2][:, 0:NHEAD * HD].rearrange("q (h d) -> q h d", h=NHEAD),
                                        rden[:, m % 2, :].unsqueeze(2).broadcast_to([P, NHEAD, HD]), ALU.mult).then_inc(o_ready, 1)
                        return
                    v.tensor_copy(dst, bank[6 + u % 2][:, :].rearrange("q (h d) -> q h d", h=NHEAD))
                    dve.drain()
                    sq = sprob[m % 2][:, :, 0:CV]
                    v.tensor_tensor(sq, dst, dst, ALU.mult)
                    dve.drain()
                    v.tensor_reduce(oss[:, :], sq, AX.X, ALU.add).then_inc(oss_ready, 1)
                    dve.wait_ge(ort_ready, 2 * L + t + 1)
                    v.reciprocal(ors[:, :], ort[:, :])
                    dve.drain()
                    v.tensor_tensor(dst, dst, ors[:, :].unsqueeze(2).broadcast_to([P, NHEAD, CV]), ALU.mult)
                    dve.drain()
                    v.tensor_tensor(dst, dst, subln[:, :].unsqueeze(1).broadcast_to([P, NHEAD, CV]), ALU.mult).then_inc(o_ready, 1)

                for t in range(NT):
                    select(t)
                mask(NIDX)
                for m in range(NIDX, len(MAPS)):
                    kind, t, _, _ = MAPS[m]
                    nk = P * (t + 1)
                    if m + 1 < len(MAPS) and kind != "C2":
                        mask(m + 1)
                    dve.wait_ge(exp_done, SOFT * L + m - NIDX + 1)
                    v.reciprocal(rden[:, m % 2, :], den[:, m % 2, :])
                    dve.drain()
                    if kind == "C2":
                        one, two = (m - 1) % 2, m % 2
                        v.tensor_scalar(rden[:, two, :], rden[:, two, :], nlam[:, 0:1], None, ALU.mult)
                        dve.drain()
                        for h in range(NHEAD):
                            v.tensor_scalar(sprob[two][:, h, 0:nk], sprob[two][:, h, 0:nk], rden[:, two, h:h + 1], None, ALU.mult)
                        dve.drain()
                        for h in range(NHEAD):
                            last = v.scalar_tensor_tensor(out=sprob[one][:, h, 0:nk], in0=sprob[one][:, h, 0:nk], scalar=rden[:, one, h:h + 1],
                                                          in1=sprob[two][:, h, 0:nk], op0=ALU.mult, op1=ALU.add)
                        last.then_inc(prob_ready, 1)
                    if m in UNIT_OF:
                        probabilities_out(m)
                        finish(m)
                    if kind == "C2":
                        dve.drain()
                        mask(m + 1)

                for t in range(NT):
                    dve.wait_ge(oT_mm, 4 * L + 2 * t + 2)
                    v.tensor_copy(oT[:, 4:8, P * t:P * t + P], bank[5 + 2 * t][:, :].rearrange("q (j s) -> q j s", j=4)).then_inc(oT_dve, 1)

                for n in range(4):
                    h, t = n // 2, n % 2
                    if t == 0:
                        dve.wait_ge(branch_mm, 2 * L + h + 1)
                    else:
                        dve.wait_ge(slab_credit, 6 * (r0 + 2) + RING + 3 + h)
                    dst = merged[:, t, W * h:W * h + W]
                    gate = [gates[:, t, D * b + W * h:D * b + W * h + W] for b in range(3)]
                    v.tensor_tensor(dst, bank[3 * (n % 2)][:, :], gate[0], ALU.mult)
                    for b in (1, 2):
                        dve.drain()
                        v.tensor_tensor(branch, bank[3 * (n % 2) + b][:, :], gate[b], ALU.mult)
                        dve.drain()
                        last = v.tensor_tensor(dst, dst, branch, ALU.add)
                    last.then_inc(merged_ready, 1)
                for n in range(4):
                    h, t = n // 2, n % 2
                    dve.wait_ge(mT_mm, 4 * L + n + 1)
                    v.tensor_copy(hT[:, 4 * h:4 * h + 4, P * t:P * t + P], bank[6 + n % 2][:, :].rearrange("q (j s) -> q j s", j=4)).then_inc(mT_ready, 1)
                for n in range(4):
                    h, t = n // 2, n % 2
                    if t == 0:
                        dve.wait_ge(out_mm, 2 * L + h + 1)
                    else:
                        dve.wait_ge(slab_credit, 6 * (r0 + 2) + RING + 5 + h)
                    v.tensor_tensor(xres[:, t, W * h:W * h + W], xres[:, t, W * h:W * h + W], bank[n][:, :], ALU.add).then_inc(x_mixed, 1)
                dve.drain()
                norm(1, g_ffn)

                dve.wait_ge(route_mm, L + 1)
                v.tensor_tensor(lg[:, :, :], bank[4][:, 0:NT * NR].rearrange("q (t n) -> q t n", t=NT),
                                b_route[:, :].unsqueeze(1).broadcast_to([P, NT, NR]), ALU.add)
                dve.drain()
                v.tensor_copy(gpad[:, :, 0:NG], lg[:, :, 0:NG])
                dve.drain()
                for t in range(NT):
                    v.max(gm8[:, t, :], gpad[:, t, :])
                dve.drain()
                for t in range(NT):
                    v.max_index(gi8[:, t, :], gm8[:, t, :], gpad[:, t, :])
                v.tensor_tensor(gsub[:, :, :], lg[:, :, 0:NG], gm8[:, :, 0:1].broadcast_to([P, NT, NG]), ALU.subtract).then_inc(gsub_ready, 1)
                dve.drain()
                v.tensor_copy(gif[:, :], gi8[:, :, 0])
                dve.drain()
                v.tensor_tensor(goh[:, :, :], iota64[:, 0:NG].unsqueeze(1).broadcast_to([P, NT, NG]),
                                gif[:, :].unsqueeze(2).broadcast_to([P, NT, NG]), ALU.is_equal)
                dve.drain()
                v.tensor_scalar(goh[:, :, :], goh[:, :, :], 1.0, -NEG, ALU.subtract, ALU.mult)
                dve.drain()
                v.tensor_tensor(elm[:, :, :].rearrange("q t (g e) -> q t g e", g=NG), lg[:, :, NG:NR].rearrange("q t (g e) -> q t g e", g=NG),
                                goh[:, :, :].unsqueeze(3).broadcast_to([P, NT, NG, EPG]), ALU.add)
                dve.drain()
                for t in range(NT):
                    v.max(e8[:, t, :], elm[:, t, :])
                dve.drain()
                for t in range(NT):
                    v.max_index(ei8[:, t, :], e8[:, t, :], elm[:, t, :])
                v.tensor_tensor(edif[:, :], e8[:, :, 1], e8[:, :, 0], ALU.subtract).then_inc(edif_ready, 1)
                dve.drain()
                v.tensor_copy(eif[:, :, :], ei8[:, :, 0:2])
                dve.drain()
                for oh, k in ((oh1, 0), (oh2, 1)):
                    v.tensor_tensor(oh[:, :, :], iota64[:, 0:NE].unsqueeze(1).broadcast_to([P, NT, NE]),
                                    eif[:, :, k:k + 1].broadcast_to([P, NT, NE]), ALU.is_equal)
                dve.drain()
                v.tensor_tensor(chosen[:, :, :], oh1[:, :, :], oh2[:, :, :], ALU.add).then_inc(chosen_ready, 1)
                dve.wait_ge(gexp_ready, L + 1)
                v.tensor_reduce(gsum[:, :], gexp[:, :, :], AX.X, ALU.add)
                dve.wait_ge(eexp_ready, L + 1)
                v.tensor_scalar(edif[:, :], eexp[:, :], 1.0, None, ALU.add)
                dve.drain()
                v.tensor_tensor(gsum[:, :], gsum[:, :], edif[:, :], ALU.mult)
                dve.drain()
                v.reciprocal(ew[:, :, 0], gsum[:, :])
                dve.drain()
                v.tensor_tensor(ew[:, :, 1], ew[:, :, 0], eexp[:, :], ALU.mult)
                dve.drain()
                for oh, k in ((oh1, 0), (oh2, 1)):
                    v.tensor_tensor(oh[:, :, :], oh[:, :, :], ew[:, :, k:k + 1].broadcast_to([P, NT, NE]), ALU.mult)
                dve.drain()
                v.tensor_tensor(wt[:, :, 0:NE], oh1[:, :, :], oh2[:, :, :], ALU.add)
                dve.wait_ge(rank_mm, L + 1)
                v.tensor_scalar(rank[:, :, 0:NE], bank[5][:, 0:NT * NE].rearrange("q (t e) -> q t e", t=NT), 1.0, None, ALU.add)
                v.tensor_reduce(cmax[:, :], bank[5][:, 2 * NE:3 * NE], AX.X, ALU.max)
                dve.drain()
                v.tensor_tensor(rank[:, :, 0:NE], rank[:, :, 0:NE], chosen[:, :, :], ALU.mult)
                v.tensor_tensor(over[:, :], limits, cmax[:, 0:1].broadcast_to([P, 3]), ALU.is_lt)
                dve.drain()
                v.tensor_scalar(rank[:, :, 0:NE], rank[:, :, 0:NE], 1.0, None, ALU.subtract)
                v.tensor_reduce(npf[:, :], over[:, :], AX.X, ALU.add)
                dve.drain()
                v.tensor_scalar(npass[:, :], npf[:, :], 1.0, None, ALU.add).then_inc(routed, 1)
                wait_apart(dve, routed, L + 1)
                n_pass = dve.value_load(npass[0:1, 0:1], min_val=1, max_val=4)

                def one_hot(e):
                    shape = [P, NT, 2, SLOTS]
                    v.tensor_tensor(pick.rearrange("q t (e s) -> q t e s", e=2), iota64.unsqueeze(1).unsqueeze(1).broadcast_to(shape),
                                    rank[:, :, bass.ds(e, 2)].unsqueeze(3).broadcast_to(shape), ALU.is_equal)
                    dve.drain()
                    v.tensor_tensor(pickw.rearrange("q t (e s) -> q t e s", e=2), pick.rearrange("q t (e s) -> q t e s", e=2),
                                    wt[:, :, bass.ds(e, 2)].unsqueeze(3).broadcast_to(shape), ALU.mult).then_inc(pick_ready, 1)

                with dve.Fori(0, n_pass) as ps:
                    one_hot(0)
                    with dve.Fori(0, PAIRS) as i:
                        pairs = dve.snap((p0 + ps) * PAIRS + i)
                        for h in range(2):
                            dve.wait_ge(gather_mm, 2 * pairs + h + 1)
                            v.tensor_tensor(xgT[:, 4 * h:4 * h + 4, :], bank[6 + h][:, :].rearrange("q (c s) -> q c s", c=4),
                                            g_ffn[:, 4 * h:4 * h + 4].unsqueeze(2).broadcast_to([P, 4, P]), ALU.mult).then_inc(xgT_ready, 1)
                        dve.wait_ge(slab_credit, 6 * (r0 + MIX_ROUNDS + ps * PAIRS + i) + RING + 4)
                        dve.wait_ge(silu_done, pairs + 1)
                        v.tensor_tensor(hid.rearrange("q c p -> q p c"), sg.rearrange("q (p c) -> q p c", c=KF),
                                        bank[5][:, :].rearrange("q (p c) -> q p c", c=KF), ALU.mult).then_inc(hid_ready, 1)
                        dve.wait_ge(hidT_mm, 2 * pairs + 2)
                        v.tensor_copy(hidT[:, 2:4, :].rearrange("q c s -> q (c s)"), bank[5][:, 0:2 * P]).then_inc(hidT_dve, 1)
                        dve.wait_ge(pickwT_mm, pairs + 1)
                        one_hot(2 * i + 2)
                        dve.wait_ge(slab_credit, 6 * (r0 + MIX_ROUNDS + ps * PAIRS + i) + RING + 6)
                        v.tensor_copy(ysb[:, W:D], bank[6][:, :]).then_inc(y_dve, 1)
                    dve.drain()
                    v.tensor_scalar(rank[:, :, 0:NE], rank[:, :, 0:NE], float(SLOTS), None, ALU.subtract)
                    dve.drain()
                dve.sem_inc(smalls_free, 1)
                dve.wait_ge(combined, (p0 + n_pass) * PAIRS)
                v.tensor_copy(xres[:, 1, 0:W], bank[2][:, :])
                v.tensor_copy(xres[:, 1, W:D], bank[3][:, :])
                dve.drain()
                dve.sem_inc(x_dve, 1)
                count_on(dve, rounds, passes, n_pass)


_INS = ["x", "norm_attn", "w_in", "qk_gain", "idx_k_gain", "diff_lambda", "diff_subln_gain", "w_proj_a",
        "w_proj_b", "w_proj_c", "w_out", "norm_ffn", "w_group", "b_group", "w_router", "b_router",
        "w_e_gate", "w_e_up", "w_e_down"]


def _constants():
    import math

    import numpy as np

    f = np.float32
    inv = (1.0 / (f(10000.0) ** (np.arange(0, HD, 2, dtype=f) / f(HD)))).astype(f)
    ang = np.arange(T, dtype=f)[:, None] * inv[None, :]
    cos, sin = np.cos(ang), np.sin(ang)
    rope = np.stack([np.concatenate([cos, cos], 1), np.concatenate([-sin, sin], 1)])
    rope = rope.reshape(2, NT, P, HD).transpose(2, 0, 1, 3)
    pos = np.arange(T).reshape(NT, P).T
    causal = np.where(np.arange(T)[None, None, :] <= pos[:, :, None], 0.0, NEG)
    i = np.arange(P)
    square = np.stack([np.eye(P), i[:, None] < i[None, :], np.ones((P, P))], 1)
    row = np.zeros((P, 72))
    row[:, 0:64] = np.arange(64)
    row[:, 64:67] = SLOTS * np.arange(1, 4)
    init = [0.8 - 0.6 * math.exp(-0.3 * layer) for layer in range(DEPTH)]
    lam = np.broadcast_to(np.array([[v, 1.0 - v] for v in init]), (P, DEPTH, 2))
    return {"c_square": square, "c_rope": rope, "c_causal": causal, "c_row": row, "c_lam": lam}


def kernel(**inputs):
    import numpy as _np
    import concourse.bacc as _bacc
    from concourse import mybir as _mybir
    from concourse.bass_utils import run_bass_kernel_spmd as _run

    nc = _bacc.Bacc("TRN2", target_bir_lowering=False, num_devices=1)
    arrays, args = {}, []
    for name in _INS:
        arrays[name] = _np.ascontiguousarray(inputs[name])
    for name, a in _constants().items():
        arrays[name] = _np.ascontiguousarray(a.astype(_np.float32))
    for name, a in arrays.items():
        args.append(nc.dram_tensor(name, a.shape, _mybir.dt.from_np(a.dtype), kind="ExternalInput").ap())
    args.append(nc.dram_tensor("out", (1, T, D), _mybir.dt.float32, kind="ExternalOutput").ap())
    trunk(nc, *args)
    r = _run(nc, [arrays], core_ids=[0])
    return r.results[0]["out"]
```

```python
from contextlib import ExitStack

import concourse.bass as bass
from concourse import mybir

P = 128
T = 256
NT = T // P
D = 1024
KD = D // P
DEPTH = 2
HD = 64
EPS = 1e-6
SCALE = HD ** -0.5
NHEAD = 4
IDX_HEADS = 8
TOPK = min(256, T // 4)
CV = 2 * HD
NG = 4
EPG = 8
NE = NG * EPG
FE = 512
KF = FE // P
NR = NG + NE
D_IN = 6728
GATES = D_IN - 3 * D
RING = 10
W = 512
FULL = D_IN // W
TAIL = D_IN - FULL * W
QKV = GATES // W
MIX_RING = 4
MIX_SLABS = FULL + 1 + 4
QUARTERS = 4 * MIX_SLABS
QW = KD * W // 4
QBUFS = 4
LEAD = QBUFS - 1
BRANCH0 = 4 * (FULL + 1)
OUT0 = BRANCH0 + 8
PAIRS = NE // 2
PAIR_SLABS = 6
PASS_SLABS = PAIRS * PAIR_SLABS
BODY = 5
BODIES = PAIRS // BODY
REST = PAIRS - BODY * BODIES
ROUNDS = BODY * PAIR_SLABS // RING
PASS_LOADS = [len(range(k, PASS_SLABS, RING)) for k in range(RING)]
SLOTS = 64
NEG = -1e30
TAKEN = -3e38

QA, VA, QB, VB, QI, KI, WI, Q1, K1, VC = 0, 512, 768, 1280, 1536, 2048, 2112, 2120, 2632, 3144
GROUPS = [
    (QA, 2, 4, 0, 0, 0),
    (QB, 2, 4, 2, 8, 2),
    (QI, 1, 8, 7, None, 3),
    (KI, 1, 1, 6, 16, 4),
    (Q1, 1, 8, 4, 17, 5),
    (K1, 1, 8, 5, 25, 6),
]
NGROUPS = len(GROUPS)
ROOTS = [0, 1, 3, 4]
NSUM = 33
NSETS = 8
T_QA, T_KA, T_QB, T_KB, T_QI, T_KI, T_Q1, T_Q2, T_K1, T_K2 = 0, 2, 4, 6, 8, 12, 0, 2, 4, 6
T_CHUNKS = 13
T_GROUP = [(0, 4), (4, 4), (8, 4), (12, 1), (0, 4), (4, 4)]

MAPS = [("idx", t, T_QI + 2 * g, None) for t in range(NT) for g in range(2)]
MAPS += [("A", t, T_QA, T_KA) for t in range(NT)]
MAPS += [("B", t, T_QB, T_KB) for t in range(NT)]
MAPS += [(c, t, q, k) for t in range(NT) for c, q, k in (("C1", T_Q1, T_K1), ("C2", T_Q2, T_K2))]
NIDX = 4
SOFT = len(MAPS) - NIDX
UNIT_OF = {}
for _m, _map in enumerate(MAPS):
    if _map[0] in ("A", "B", "C2"):
        UNIT_OF[_m] = len(UNIT_OF)
UNITS = len(UNIT_OF)
V_OF = {"A": VA, "B": VB, "C2": VC}
O_OF = {"A": 0, "B": 256, "C2": 512}

def _order():
    steps = []

    def piece(*chunks):
        steps.extend(("quarter", 4 * s + 2 * half + i) for s, half in chunks for i in range(2))

    def step(*names):
        steps.extend(names)

    piece((0, 0), (0, 1), (1, 0))
    step(("roots", 0))
    piece((1, 1), (2, 0), (2, 1))
    step(("turn", 0), ("roots", 1))
    piece((3, 0), (3, 1))
    step(("turn", 1))
    piece((4, 0), (4, 1))
    step(("turn", 2), ("roots", 3))
    piece((5, 0))
    step(("turn", 3), ("scores", 0), ("scores", 1), ("scores", 2), ("scores", 3))
    piece((5, 1))
    step(("lambda",), ("scores", 4))
    piece((6, 0))
    step(("values", 4), ("scores", 5))
    piece((6, 1), (7, 0))
    step(("values", 5), ("scores", 6))
    piece((7, 1))
    step(("values", 6), ("scores", 7))
    piece((8, 0))
    step(("values", 7))
    piece((8, 1))
    step(("roots", 4))
    piece((9, 0))
    step(("turn", 4))
    piece((9, 1))
    step(("turn", 5), ("scores", 8))
    piece((10, 0))
    step(("scores", 9))
    piece((10, 1))
    step(("values", 9), ("scores", 10))
    piece((11, 0))
    step(("scores", 11))
    piece((11, 1))
    step(("values", 11))
    piece((12, 0), (12, 1))
    step(("heads",))
    piece((13, 0), (13, 1))
    return steps


ORDER = _order()


def trunk(nc, x, norm_attn, w_in, qk_gain, idx_k_gain, diff_lambda, diff_subln_gain, w_proj_a,
          w_proj_b, w_proj_c, w_out, norm_ffn, w_group, b_group, w_router, b_router,
          w_e_gate, w_e_up, w_e_down, c_square, c_rope, c_causal, c_row, c_lam, out):
    F = mybir.dt.float32
    FR = mybir.dt.float32r
    I32 = mybir.dt.int32
    U32 = mybir.dt.uint32
    ALU = mybir.AluOpType
    ACT = mybir.ActivationFunctionType
    AX = mybir.AxisListType

    ctx = ExitStack()
    with ctx:
        def sb(name, shape, dt=F):
            return ctx.enter_context(nc.sbuf_tensor(name, shape, dt))

        def sem(name):
            return ctx.enter_context(nc.semaphore(name))

        ring = [sb(f"ring{k}", [P, KD * W]) for k in range(MIX_RING)]
        w_hi = nc.alloc_sbuf_tensor_at("w_hi", [P, QBUFS, QW], FR, offset=nc.sbuf_base)
        ring.append(sb("ring4", [P, KD * W]))
        w_lo = nc.alloc_sbuf_tensor_at("w_lo", [P, QBUFS, QW], FR, offset=nc.sbuf_base)
        ring.append(sb("ring5", [P, KD * W]))
        ring.append(nc.alloc_sbuf_tensor_at("ring6", [P, KD * W], F, offset=nc.sbuf_base))
        h_hi = sb("h_hi", [P, KD, T], FR)
        h_lo = sb("h_lo", [P, KD, T], FR)
        BETWEEN = NT * GATES + NT * 3 * D + T_CHUNKS * T - KD * W
        ring.append(nc.alloc_sbuf_tensor_at("ring7", [P, KD * W], F, offset=nc.sbuf_base + 4 * KD * W))
        ring.append(nc.alloc_sbuf_tensor_at("ring8", [P, KD * W], F, offset=nc.sbuf_base + 4 * BETWEEN))
        ring.append(nc.alloc_sbuf_tensor_at("ring9", [P, KD * W], F, offset=nc.sbuf_base))
        qkv = sb("qkv", [P, NT, GATES])
        gates = sb("gates", [P, NT, 3 * D])
        m_hi = nc.alloc_sbuf_tensor_at("m_hi", [P, NT, KD, P], FR, offset=nc.sbuf_base)
        qkT = sb("qkT", [P, T_CHUNKS, T])
        xres = sb("xres", [P, NT, D])
        m_lo = nc.alloc_sbuf_tensor_at("m_lo", [P, NT, KD, P], FR, offset=nc.sbuf_base)
        xs = sb("xs", [P, NT, KD, P])
        xs_flat = xs[:, :, :, :].rearrange("q t c p -> q t (c p)")
        gcos = gates[:, :, 2048:2560].rearrange("q t (g d) -> q t g d", g=NSETS)
        gsin = gates[:, :, 2560:3072].rearrange("q t (g d) -> q t g d", g=NSETS)
        gain_b = gates[:, 1, 1600:1600 + 7 * HD].rearrange("q (g d) -> q g d", g=7)
        qkv_flat = qkv[:, :, :].rearrange("q t n -> q (t n)")
        merged = qkv_flat[:, 0:2 * D].rearrange("q (t n) -> q t n", t=NT)
        branch = qkv_flat[:, 2 * D:2 * D + 2 * W].rearrange("q (t n) -> q t n", t=NT)

        square = sb("square", [P, 3, P])
        ident, tri, ones = square[:, 0, :], square[:, 1, :], square[:, 2, :]
        rope = sb("rope", [P, 2, NT, HD])
        causal = sb("causal", [P, NT, T])
        row = sb("row", [P, 72])
        iota64, limits = row[:, 0:64], row[:, 64:67]
        lamc = sb("lamc", [P, DEPTH, 2])
        ki2 = sb("ki2", [P, NT, 2 * HD])
        g_attn = sb("g_attn", [P, KD])
        g_ffn = sb("g_ffn", [P, KD])
        w_route = sb("w_route", [P, KD, NR])
        b_route = sb("b_route", [P, NR])
        dlam = sb("dlam", [P, 4, HD])
        subln = sb("subln", [P, CV])
        eps = sb("eps", [P, 1])
        ssq = sb("ssq", [P, NT])
        rt = sb("rt", [P, NT])
        rstd = sb("rstd", [P, NT])
        hss = sb("hss", [P, NT, NSUM])
        hrt = sb("hrt", [P, NT, NSUM])
        hrs = sb("hrs", [P, NT, NSUM])
        wis = sb("wis", [P, NT, IDX_HEADS])
        m8 = sb("m8", [P, 8])
        mx = sb("mx", [P, 2, NHEAD])
        nb = sb("nb", [P, 2, NHEAD])
        den = sb("den", [P, 2, NHEAD])
        rden = sb("rden", [P, 2, NHEAD])
        oss = sb("oss", [P, NT, NHEAD])
        ort = sb("ort", [P, NT, NHEAD])
        ors = sb("ors", [P, NT, NHEAD])
        ldot = sb("ldot", [P, 2])
        lexp = sb("lexp", [P, 2])
        nlam = sb("nlam", [P, 1])
        lg = sb("lg", [P, NT, NR])
        gpad = sb("gpad", [P, NT, 8])
        gm8 = sb("gm8", [P, NT, 8])
        gi8 = sb("gi8", [P, NT, 8], U32)
        e8 = sb("e8", [P, NT, 8])
        ei8 = sb("ei8", [P, NT, 8], U32)
        gsub = sb("gsub", [P, NT, NG])
        gexp = sb("gexp", [P, NT, NG])
        gsum = sb("gsum", [P, NT])
        gw = sb("gw", [P, NT])
        gif = sb("gif", [P, NT])
        goh = sb("goh", [P, NT, NG])
        elm = sb("elm", [P, NT, NE])
        eif = sb("eif", [P, NT, 2])
        edif = sb("edif", [P, NT])
        eexp = sb("eexp", [P, NT])
        ew = sb("ew", [P, NT, 2])
        oh1 = sb("oh1", [P, NT, NE])
        oh2 = sb("oh2", [P, NT, NE])
        chosen = sb("chosen", [P, NT, NE])
        rank = sb("rank", [P, NT, NE + 2])
        wt = sb("wt", [P, NT, NE + 2])
        cmax = sb("cmax", [P, 1])
        over = sb("over", [P, 3])
        npf = sb("npf", [P, 1])
        npass = sb("npass", [P, 1], I32)

        pairs_of_heads = [qkv[:, b, 0:2 * QB].rearrange("q (g n) -> q g n", g=2)[:, :, 0:2 * T] for b in range(2)]
        sprob = [[pairs_of_heads[b][:, h // 2, T * (h % 2):T * (h % 2) + T] for h in range(NHEAD)] for b in range(2)]
        score = [qkv[:, t, QI:QI + T] for t in range(NT)]
        left = [qkv[:, t, QI + T:QI + 2 * T] for t in range(NT)]
        picked = left
        probT = [(gates[:, u % 2, 1024:2048] if u < 4 else qkv[:, u % 2, Q1:Q1 + 1024]).rearrange("q (k h t) -> q k h t", k=NT, h=NHEAD)
                 for u in range(UNITS)]
        arena = gates[:, :, :].rearrange("q t n -> q (t n)")[:, 2 * KD * W - NT * GATES:BETWEEN - NT * GATES]
        xgT = arena[:, 0:1024].rearrange("q (c s) -> q c s", c=KD)
        hid = arena[:, 1024:1536].rearrange("q (c p) -> q c p", c=KF)
        sg = arena[:, 1536:2048]
        hidT = arena[:, 1536:2048].rearrange("q (c s) -> q c s", c=KF)
        ysb = arena[:, 2048:3072]
        pick = arena[:, 3072:3328].rearrange("q (t s) -> q t s", t=NT)
        pickw = arena[:, 3328:3584].rearrange("q (t s) -> q t s", t=NT)
        pickwT = arena[:, 4240:4496].rearrange("q (t s) -> q t s", t=NT)
        hnT = arena[:, 0:KD * T].rearrange("q (c t) -> q c t", c=KD)

        bank = [ctx.enter_context(nc.psum_tensor(f"bank{b}", [P, 512], F)) for b in range(8)]

        consts_in = sem("consts_in")
        smalls_in = sem("smalls_in")
        smalls_free = sem("smalls_free")
        slab_loaded = [sem(f"slab_loaded{k}") for k in range(RING)]
        slab_credit = sem("slab_credit")
        NORMS = 2
        squared = sem("squared")
        rooted = sem("rooted")
        rstd_ready = sem("rstd_ready")
        xs_act = sem("xs_act")
        xs_dve = sem("xs_dve")
        hT_mm = sem("hT_mm")
        hT_ready = sem("hT_ready")
        hi_done = sem("hi_done")
        lo_done = sem("lo_done")
        quarter_mm = sem("quarter_mm")
        in_mm = sem("in_mm")
        in_evac = sem("in_evac")
        sums_ready = sem("sums_ready")
        roots_ready = sem("roots_ready")
        rotated = sem("rotated")
        qkT_mm = sem("qkT_mm")
        qkT_act = sem("qkT_act")
        map_mm = sem("map_mm")
        relu_done = sem("relu_done")
        idx_added = sem("idx_added")
        masked = sem("masked")
        exp_done = sem("exp_done")
        prob_ready = sem("prob_ready")
        probT_mm = sem("probT_mm")
        probT_act = sem("probT_act")
        probT_dve = sem("probT_dve")
        pv_mm = sem("pv_mm")
        o_ready = sem("o_ready")
        oss_ready = sem("oss_ready")
        heads_ready = sem("heads_ready")
        ort_ready = sem("ort_ready")
        ldot_ready = sem("ldot_ready")
        lexp_ready = sem("lexp_ready")
        oT_mm = sem("oT_mm")
        oT_hi = sem("oT_hi")
        oT_lo = sem("oT_lo")
        branch_used = sem("branch_used")
        mT_mm = sem("mT_mm")
        mT_hi = sem("mT_hi")
        mT_lo = sem("mT_lo")
        out_mm = sem("out_mm")
        x_mixed = sem("x_mixed")
        route_mm = sem("route_mm")
        gsub_ready = sem("gsub_ready")
        gexp_ready = sem("gexp_ready")
        edif_ready = sem("edif_ready")
        eexp_ready = sem("eexp_ready")
        chosen_ready = sem("chosen_ready")
        rank_mm = sem("rank_mm")
        routed = sem("routed")
        pick_ready = sem("pick_ready")
        gather_mm = sem("gather_mm")
        xgT_ready = sem("xgT_ready")
        silu_done = sem("silu_done")
        hid_ready = sem("hid_ready")
        pickwT_mm = sem("pickwT_mm")
        pickwT_ready = sem("pickwT_ready")
        hidT_mm = sem("hidT_mm")
        hidT_act = sem("hidT_act")
        hidT_dve = sem("hidT_dve")
        down_mm = sem("down_mm")
        y_act = sem("y_act")
        y_dve = sem("y_dve")
        combined = sem("combined")
        x_act = sem("x_act")
        x_dve = sem("x_dve")
        stored = sem("stored")
        past_wait = sem("past_wait")
        SMALLS = 10

        x_view = x.rearrange("b (t p) d -> p (b t) d", p=P)
        out_view = out.rearrange("b (t p) d -> p (b t) d", p=P)

        def counter(eng, tag):
            passes = eng.alloc_register(f"passes_{tag}")
            eng.reg_mov(passes, 0)
            return passes

        def count_of(eng, passes):
            return eng.snap(passes, min_val=0, max_val=4 * DEPTH)

        def wait_apart(eng, signal, value):
            eng.wait_ge(signal, value)
            eng.sem_inc(past_wait, 1)

        MIX_LOADS = (5, 5, 6, 6, 0, 0, 0, 0, 0, 0)

        def slot_of(n):
            return n % MIX_RING

        def place_free(eng, passes, b, n):
            eng.wait_ge(slab_credit, PASS_SLABS * passes + BODY * PAIR_SLABS * b + n + 1)

        def pass_begins(eng, passes, k):
            eng.wait_ge(slab_credit, PASS_SLABS * passes + k + 1 + RING * PASS_LOADS[k] - PASS_SLABS)

        def pair_slab(j, k):
            return (PAIR_SLABS * j + k) % RING, (PAIR_SLABS * j + k) // RING

        def wait_mix_slab(eng, n, L, p0):
            eng.wait_ge(slab_loaded[slot_of(n)],
                        16 * (MIX_LOADS[slot_of(n)] * L + PASS_LOADS[slot_of(n)] * p0 + n // MIX_RING + 1 + (2 if n // 2 == (FULL + 1) // 2 else 0)))

        def score_bank(m):
            return 6 if m in (1, 3) else 2

        block = ctx.enter_context(nc.Block())

        @block.sync
        def _(sp):
            sp.dma_start(xres[:, :, :], x_view).then_inc(consts_in, 16)
            sp.dma_start(square[:, :, :], c_square).then_inc(consts_in, 16)
            sp.dma_start(rope[:, :, :, :], c_rope).then_inc(consts_in, 16)
            sp.dma_start(causal[:, :, :], c_causal).then_inc(consts_in, 16)
            sp.dma_start(row[:, :], c_row).then_inc(consts_in, 16)
            sp.dma_start(lamc[:, :, :], c_lam).then_inc(consts_in, 16)
            passes = counter(sp, "sp")

            with sp.Fori(0, DEPTH) as L:
                p0 = count_of(sp, passes)
                sp.wait_ge(smalls_free, L + 1)
                sp.dma_start(g_attn[:, :], norm_attn[L, :].rearrange("(p c) -> p c", c=KD)).then_inc(smalls_in, 16)
                sp.dma_start(g_ffn[:, :], norm_ffn[L, :].rearrange("(p c) -> p c", c=KD)).then_inc(smalls_in, 16)
                sp.dma_start(gain_b[:, 0:6, :].rearrange("q g d -> q (g d)"),
                             qk_gain[L, :, :].rearrange("g d -> (g d)").partition_broadcast(P)).then_inc(smalls_in, 16)
                sp.dma_start(gain_b[:, 6, :], idx_k_gain[L, :].partition_broadcast(P)).then_inc(smalls_in, 16)
                sp.dma_start(dlam[:, :, :].rearrange("q g d -> q (g d)"),
                             diff_lambda[L, :, :].rearrange("g d -> (g d)").partition_broadcast(P)).then_inc(smalls_in, 16)
                sp.dma_start(subln[:, :], diff_subln_gain[L, :].partition_broadcast(P)).then_inc(smalls_in, 16)
                sp.dma_start(w_route[:, :, 0:NG], w_group[L, :, :].rearrange("(p c) n -> p c n", c=KD)).then_inc(smalls_in, 16)
                sp.dma_start(w_route[:, :, NG:NR], w_router[L, :, :].rearrange("(p c) n -> p c n", c=KD)).then_inc(smalls_in, 16)
                sp.dma_start(b_route[:, 0:NG], b_group[L, :].partition_broadcast(P)).then_inc(smalls_in, 16)
                sp.dma_start(b_route[:, NG:NR], b_router[L, :].partition_broadcast(P)).then_inc(smalls_in, 16)

                w_in_v = w_in[L, :, :].rearrange("(p c) n -> p c n", c=KD)
                for n in range(MIX_SLABS):
                    k = slot_of(n)
                    if n < MIX_RING:
                        pass_begins(sp, p0, k)
                    else:
                        sp.wait_ge(lo_done, QUARTERS * L + 4 * (n - MIX_RING + 1))
                    slab = ring[k][:, :].rearrange("q (c n) -> q c n", c=KD)
                    if n < FULL:
                        sp.dma_start(slab, w_in_v[:, :, W * n:W * n + W]).then_inc(slab_loaded[k], 16)
                    elif n == FULL:
                        sp.dma_start(ring[k][:, 0:KD * TAIL].rearrange("q (c n) -> q c n", c=KD),
                                     w_in_v[:, :, FULL * W:D_IN]).then_inc(slab_loaded[k], 16)
                    elif n < FULL + 3:
                        h = n - FULL - 1
                        for w, a, b in ((w_proj_a, 0, 2), (w_proj_b, 2, 4), (w_proj_c, 4, 8)):
                            sp.dma_start(slab[:, a:b, :],
                                         w[L, :, :].rearrange("(c p) n -> p c n", p=P)[:, :, h * W:h * W + W]).then_inc(slab_loaded[k], 16)
                    else:
                        h = n - FULL - 3
                        sp.dma_start(ring[k][:, :].rearrange("q (c n) -> q c n", c=4),
                                     w_out[L, D // 2 * h:D // 2 * h + D // 2, :].rearrange("(c p) n -> p c n", p=P)).then_inc(slab_loaded[k], 16)

                def load_expert(pair, j, k):
                    w = (w_e_gate, w_e_up, w_e_down)[k // 2]
                    slot = pair_slab(j, k)[0]
                    sp.dma_start(ring[slot][:, :], w[L, 2 * pair + k % 2, :, :].rearrange("(p c) n -> p (c n)", p=P)).then_inc(slab_loaded[slot], 16)

                def load_pairs(passes, b, count, first=0):
                    for n in range(first, count * PAIR_SLABS):
                        place_free(sp, passes, b, n)
                        load_expert(BODY * b + n // PAIR_SLABS, n // PAIR_SLABS, n % PAIR_SLABS)

                def load_pass(passes):
                    load_pairs(passes, 0, BODY, RING)
                    with sp.Fori(1, BODIES) as b:
                        load_pairs(passes, b, BODY)
                    load_pairs(passes, BODIES, REST)

                for slot, signal, value in ((2, lo_done, QUARTERS * L + OUT0 - 4),
                                            (7, branch_used, 6 * L + 4),
                                            (3, lo_done, QUARTERS * L + OUT0),
                                            (6, quarter_mm, QUARTERS * L + OUT0),
                                            (0, lo_done, QUARTERS * L + OUT0 + 4),
                                            (9, mT_mm, 4 * (L + 1)),
                                            (1, lo_done, QUARTERS * (L + 1)),
                                            (4, quarter_mm, QUARTERS * (L + 1)),
                                            (5, quarter_mm, QUARTERS * (L + 1)),
                                            (8, quarter_mm, QUARTERS * (L + 1))):
                    wait_apart(sp, signal, value)
                    load_expert(slot // PAIR_SLABS, slot // PAIR_SLABS, slot % PAIR_SLABS)
                load_pass(p0)
                wait_apart(sp, routed, L + 1)
                n = sp.value_load(npass[0:1, 0:1], min_val=1, max_val=4)
                with sp.If(n > 1):
                    with sp.Fori(1, n) as more:
                        for k in range(RING):
                            pass_begins(sp, p0 + more, k)
                            load_expert(k // PAIR_SLABS, k // PAIR_SLABS, k % PAIR_SLABS)
                        load_pass(p0 + more)
                sp.reg_add(passes, passes, n)

            sp.wait_ge(x_act, DEPTH)
            sp.wait_ge(x_dve, DEPTH + 1)
            sp.dma_start(out_view, xres[:, :, :]).then_inc(stored, 16)
            sp.wait_ge(stored, 16)

        @block.tensor
        def _(pe):
            pe.sem_inc(slab_credit, RING)
            pe.wait_ge(consts_in, 96)
            passes = counter(pe, "pe")

            with pe.Fori(0, DEPTH) as L:
                p0 = count_of(pe, passes)

                def transpose_x(n):
                    for t in range(NT):
                        pe.wait_ge((xs_act, xs_dve)[t], NORMS * L + n + 1)
                        for h in range(2):
                            for c in range(4):
                                mm = nc.tensor.transpose(bank[4 + 2 * t + h][:, P * c:P * c + P], xs[:, t, 4 * h + c, :], ident)
                            mm.then_inc(hT_mm, 1)

                transpose_x(0)

                def parts(out, n, lhs_hi, lhs_lo, col, w, start, stop):
                    hi, lo = w_hi[:, n % QBUFS, col:col + w], w_lo[:, n % QBUFS, col:col + w]
                    nc.tensor.matmul(out, lhs_hi, hi, start=start, stop=False)
                    nc.tensor.matmul(out, lhs_hi, lo, start=False, stop=False)
                    return nc.tensor.matmul(out, lhs_lo, hi, start=False, stop=stop)

                def quarter(n):
                    s, qc = n // 4, n % 4
                    w = W if s < FULL else TAIL
                    pe.wait_ge(lo_done, QUARTERS * L + n + 1)
                    for t in range(NT):
                        if n == 0:
                            pe.wait_ge(hT_ready, 4 * NORMS * L + 2 * t + 2)
                        if qc == 0:
                            pe.wait_ge(in_evac, NT * ((FULL + 1) * L + s) + t + 1)
                        for c in range(2):
                            k = 2 * qc + c
                            mm = parts(bank[t][:, 0:w], n, h_hi[:, k, P * t:P * t + P], h_lo[:, k, P * t:P * t + P],
                                       w * c, w, k == 0, k == KD - 1)
                        if t == 0 and qc == 3:
                            mm.then_inc(in_mm, 1)
                    mm.then_inc(quarter_mm, 1)

                def heads():
                    for t in range(NT):
                        pe.wait_ge(heads_ready, NT * L + t + 1)
                        for h in range(2):
                            for j in range(4):
                                mm = nc.tensor.transpose(bank[4 + 2 * t + h][:, P * j:P * j + P], xs[:, t, 4 * h + j, :], ident)
                            mm.then_inc(oT_mm, 1)

                turned = [0]

                def turn(g):
                    pe.wait_ge(rotated, NGROUPS * L + g + 1)
                    k0, nk = T_GROUP[g]
                    if turned[0]:
                        pe.wait_ge(qkT_act, (NGROUPS * NT) * L + turned[0])
                    for t in range(NT):
                        for j in range(nk):
                            col = GROUPS[g][0] + P * j
                            src = ki2[:, t, :] if g == 3 else qkv[:, t, col:col + P]
                            mm = nc.tensor.transpose(bank[4 + t][:, P * j:P * j + P], src, ident)
                        mm.then_inc(qkT_mm, 1)
                    turned[0] += NT

                def scores(m):
                    kind, t, tq, tk = MAPS[m]
                    pe.wait_ge(qkT_act, NGROUPS * NT * L + turned[0])
                    if 2 <= m < NIDX:
                        pe.wait_ge(relu_done, NIDX * L + m - 1)
                    elif m == NIDX:
                        pe.wait_ge(relu_done, NIDX * L + NIDX)
                    elif m > NIDX:
                        pe.wait_ge(masked, SOFT * L + m - NIDX)
                    nk = P * (t + 1)
                    for h in range(NHEAD):
                        a = HD * (h % 2)
                        k = T_KI if tk is None else tk + h // 2
                        mm = nc.tensor.matmul(bank[score_bank(m) + h % 2][:, T * (h // 2):T * (h // 2) + nk],
                                              qkT[a:a + HD, tq + h // 2, P * t:P * t + P], qkT[a:a + HD, k, 0:nk],
                                              start=True, stop=True)
                    mm.then_inc(map_mm, 1)

                def values(m):
                    kind, t, _, _ = MAPS[m]
                    u = UNIT_OF[m]
                    src = sprob[(m - 1) % 2 if kind == "C2" else m % 2]
                    if kind == "C2":
                        pe.wait_ge(prob_ready, 2 * L + t + 1)
                    else:
                        pe.wait_ge(exp_done, SOFT * L + m - NIDX + 1)
                    for b in range(t + 1):
                        for h in range(NHEAD):
                            mm = nc.tensor.transpose(bank[4 + b][:, P * h:P * h + P], src[h][:, P * b:P * b + P], ident)
                        mm.then_inc(probT_mm, 1)
                    pe.wait_ge(probT_act, UNITS * L + u + 1)
                    if t == 1:
                        pe.wait_ge(probT_dve, 3 * L + u // 2 + 1)
                    if u >= 2:
                        pe.wait_ge(o_ready, UNITS * L + u - 1)
                    dv = CV if kind == "C2" else HD
                    for h in range(NHEAD):
                        for b in range(t + 1):
                            mm = nc.tensor.matmul(bank[6 + u % 2][:, dv * h:dv * h + dv], probT[u][:, b, h, :],
                                                  qkv[:, b, V_OF[kind] + dv * h:V_OF[kind] + dv * h + dv],
                                                  start=b == 0, stop=b == t)
                    mm.then_inc(pv_mm, 1)

                for what, *which in ORDER:
                    if what == "quarter":
                        quarter(*which)
                    elif what == "heads":
                        heads()
                    elif what == "turn":
                        turn(*which)
                    elif what == "scores":
                        scores(*which)
                    elif what == "values":
                        values(*which)

                def branch_quarter(n):
                    h, qc = (n - BRANCH0) // 4, n % 4
                    r = 3 * h + min(qc, 2)
                    pe.wait_ge(lo_done, QUARTERS * L + n + 1)
                    if r >= 2 and qc < 3:
                        pe.wait_ge(branch_used, 6 * L + r - 1)
                    for t in range(NT):
                        if n == BRANCH0:
                            pe.wait_ge(oT_lo, 4 * L + 2 * t + 2)
                        for c in range(2):
                            k = 2 * qc + c
                            mm = parts(bank[2 * (r % 2) + t][:, :], n, h_hi[:, k, P * t:P * t + P], h_lo[:, k, P * t:P * t + P],
                                       W * c, W, c == 0 and qc < 3, c == 1 and qc != 2)
                    mm.then_inc(quarter_mm, 1)

                def turn_merged(h):
                    pe.wait_ge(branch_used, 6 * L + 3 * h + 3)
                    for t in range(NT):
                        for j in range(4):
                            mm = nc.tensor.transpose(bank[(6, 0)[h] + t][:, P * j:P * j + P],
                                                     merged[:, t, W * h + P * j:W * h + P * j + P], ident)
                        mm.then_inc(mT_mm, 1)

                def out_quarter(n):
                    k = n - OUT0
                    pe.wait_ge(lo_done, QUARTERS * L + n + 1)
                    if k % 4 == 0:
                        pe.wait_ge(mT_lo, 4 * L + k // 2 + 2)
                    for t in range(NT):
                        for h in range(2):
                            mm = parts(bank[4 + 2 * t + h][:, :], n, m_hi[:, t, k, :], m_lo[:, t, k, :], W * h, W, k == 0, k == KD - 1)
                        if t == 0 and k == KD - 1:
                            mm.then_inc(out_mm, 1)
                    mm.then_inc(quarter_mm, 1)

                pe.wait_ge(in_evac, NT * ((FULL + 1) * (L + 1)) + NT)
                for n in range(BRANCH0, BRANCH0 + 6):
                    branch_quarter(n)
                turn_merged(0)
                for n in range(BRANCH0 + 6, OUT0):
                    branch_quarter(n)
                out_quarter(OUT0)
                out_quarter(OUT0 + 1)
                turn_merged(1)
                for n in range(OUT0 + 2, QUARTERS):
                    out_quarter(n)

                transpose_x(1)
                pe.wait_ge(hT_ready, 4 * (NORMS * L + 2))
                for t in range(NT):
                    for c in range(KD):
                        mm = nc.tensor.matmul(bank[4][:, NR * t:NR * t + NR], hnT[:, c, P * t:P * t + P], w_route[:, c, :],
                                              start=c == 0, stop=c == KD - 1)
                mm.then_inc(route_mm, 1)
                pe.wait_ge(x_mixed, 4 * L + 4)
                for t in range(NT):
                    for h in range(2):
                        nc.tensor.matmul(bank[2 * t + h][:, :], ident, xres[:, t, W * h:W * h + W], start=True, stop=True)
                pe.wait_ge(chosen_ready, L + 1)
                nc.tensor.matmul(bank[5][:, 0:NE], tri, chosen[:, 0, :], start=True, stop=True)
                nc.tensor.matmul(bank[5][:, NE:2 * NE], ones, chosen[:, 0, :], start=True, stop=False)
                nc.tensor.matmul(bank[5][:, NE:2 * NE], tri, chosen[:, 1, :], start=False, stop=True)
                nc.tensor.matmul(bank[5][:, 2 * NE:3 * NE], ones, chosen[:, 0, :], start=True, stop=False)
                nc.tensor.matmul(bank[5][:, 2 * NE:3 * NE], ones, chosen[:, 1, :], start=False, stop=True).then_inc(rank_mm, 1)

                wait_apart(pe, routed, L + 1)
                n_pass = pe.value_load(npass[0:1, 0:1], min_val=1, max_val=4)
                def pair_steps(ps, b, j, pairs):
                        def loaded(k):
                            slot, times = pair_slab(j, k)
                            pe.wait_ge(slab_loaded[slot], 16 * (MIX_LOADS[slot] * (L + 1) + PASS_LOADS[slot] * (p0 + ps) + ROUNDS * b + times + 1))

                        def slab(k):
                            return ring[pair_slab(j, k)[0]]

                        pe.wait_ge(pick_ready, (p0 + ps) * (PAIRS + 1) + BODY * b + j + 1)
                        for c in range(KD):
                            for t in range(NT):
                                mm = nc.tensor.matmul(bank[6 + c // 4][:, P * (c % 4):P * (c % 4) + P], xs[:, t, c, :], pick[:, t, :],
                                                      start=t == 0, stop=t == NT - 1)
                            if c % 4 == 3:
                                mm.then_inc(gather_mm, 1)
                        for m in range(2):
                            for k in (2 * m, 2 * m + 1):
                                loaded(k)
                            for c in range(KD):
                                if m == 0 and c % 4 == 0:
                                    pe.wait_ge(xgT_ready, 2 * pairs + c // 4 + 1)
                                for e in range(2):
                                    mm = nc.tensor.matmul(bank[4 + m][SLOTS * e:SLOTS * e + SLOTS, :], xgT[:, c, SLOTS * e:SLOTS * e + SLOTS],
                                                          slab(2 * m + e)[:, W * c:W * c + W], start=c == 0, stop=c == KD - 1)
                                    if c == KD - 1:
                                        mm.then_inc(slab_credit, 1)
                        for t in range(NT):
                            mm = nc.tensor.transpose(bank[6][:, P * t:P * t + P], pickw[:, t, :], ident)
                        mm.then_inc(pickwT_mm, 1)
                        pe.wait_ge(hid_ready, pairs + 1)
                        for c in range(KF):
                            mm = nc.tensor.transpose(bank[4 + c // 2][:, P * (c % 2):P * (c % 2) + P], hid[:, c, :], ident)
                            if c % 2 == 1:
                                mm.then_inc(hidT_mm, 1)
                        for k in (4, 5):
                            loaded(k)
                        pe.wait_ge(hidT_act, pairs + 1)
                        for h in range(2):
                            if h == 1:
                                pe.wait_ge(pickwT_ready, pairs + 1)
                            for c in range(KF):
                                if h == 0 and c == 2:
                                    pe.wait_ge(hidT_dve, pairs + 1)
                                for e in range(2):
                                    mm = nc.tensor.matmul(bank[7 - h][SLOTS * e:SLOTS * e + SLOTS, :], hidT[:, c, SLOTS * e:SLOTS * e + SLOTS],
                                                          slab(4 + e)[:, D * c + W * h:D * c + W * h + W], start=c == 0, stop=c == KF - 1)
                                    if c == KF - 1 and h == 0 and e == 1:
                                        mm.then_inc(down_mm, 1)
                                    if c == KF - 1 and h == 1:
                                        mm.then_inc(slab_credit, 1)
                        for h in range(2):
                            pe.wait_ge((y_act, y_dve)[h], pairs + 1)
                            for t in range(NT):
                                mm = nc.tensor.matmul(bank[2 * t + h][:, :], pickwT[:, t, :], ysb[:, W * h:W * h + W],
                                                      start=False, stop=True, skip_group_check=True)
                        mm.then_inc(combined, 1)

                with pe.Fori(0, n_pass) as ps:
                    with pe.Fori(0, BODIES) as b:
                        for j in range(BODY):
                            pair_steps(ps, b, j, pe.snap((p0 + ps) * PAIRS + BODY * b + j))
                    for j in range(REST):
                        pair_steps(ps, BODIES, j, pe.snap((p0 + ps) * PAIRS + BODY * BODIES + j))
                pe.reg_add(passes, passes, n_pass)

        @block.scalar
        def _(act):
            act.sem_inc(in_evac, NT)
            act.wait_ge(consts_in, 96)
            passes = counter(act, "act")

            with act.Fori(0, DEPTH) as L:
                p0 = count_of(act, passes)

                def norm(n):
                    for t in range(NT):
                        if n == 1:
                            act.wait_ge(x_mixed, 4 * L + 2 * t + 2)
                        nc.scalar.activation(xs_flat[:, t, :], xres[:, t, :], ACT.Square, accum_out=ssq[:, t:t + 1]).then_inc(squared, 1)
                        act.wait_ge(squared, NT * (NORMS * L + n) + t + 1)
                        nc.scalar.activation(rt[:, t:t + 1], ssq[:, t:t + 1], ACT.Sqrt, bias=eps[:, 0:1], scale=1.0 / D).then_inc(rooted, 1)
                    act.wait_ge(rstd_ready, NORMS * L + n + 1)
                    nc.scalar.activation(xs[:, 0, :, :].rearrange("q c p -> q p c"), xres[:, 0, :].rearrange("q (p c) -> q p c", c=KD),
                                         ACT.Copy, scale=rstd[:, 0:1]).then_inc(xs_act, 1)

                def split_hi(n):
                    wait_mix_slab(act, n // 4, L, p0)
                    if n >= QBUFS:
                        act.wait_ge(quarter_mm, QUARTERS * L + n - QBUFS + 1)
                    w = QW if n // 4 != FULL else 2 * TAIL
                    nc.scalar.activation(w_hi[:, n % QBUFS, 0:w], ring[slot_of(n // 4)][:, w * (n % 4):w * (n % 4) + w], ACT.Copy).then_inc(hi_done, 1)

                act.wait_ge(x_dve, L + 1)
                norm(0)
                for n in range(LEAD):
                    split_hi(n)

                def quarter(n):
                    if n + LEAD < QUARTERS:
                        split_hi(n + LEAD)
                    if n % 4 == 3:
                        chunk_out(n // 4, 0)
                        chunk_out(n // 4, 1)

                def chunk_out(s, t):
                    w = W if s < FULL else TAIL
                    if t == 0:
                        act.wait_ge(in_mm, (FULL + 1) * L + s + 1)
                    else:
                        act.wait_ge(quarter_mm, QUARTERS * L + 4 * s + 4)
                    src = bank[t]
                    if (s, t) == (11, 0):
                        wait_apart(act, rotated, NGROUPS * (L + 1))
                    if s < QKV:
                        nc.scalar.activation(qkv[:, t, W * s:W * s + w], src[:, 0:w], ACT.Copy).then_inc(in_evac, 1)
                    elif s == QKV:
                        v = GATES - QKV * W
                        nc.scalar.activation(qkv[:, t, W * s:GATES], src[:, 0:v], ACT.Copy)
                        nc.scalar.activation(gates[:, t, 0:W - v], src[:, v:W], ACT.Tanh, scale=0.5).then_inc(in_evac, 1)
                    else:
                        nc.scalar.activation(gates[:, t, W * s - GATES:W * s - GATES + w], src[:, 0:w], ACT.Tanh, scale=0.5).then_inc(in_evac, 1)

                def roots(g):
                    _, sets, per, _, h0, _ = GROUPS[g]
                    nh = sets * per if g < 4 else NSUM - h0
                    act.wait_ge(sums_ready, len(ROOTS) * L + ROOTS.index(g) + 1)
                    nc.scalar.activation(hrt[:, :, h0:h0 + nh], hss[:, :, h0:h0 + nh], ACT.Sqrt,
                                         bias=eps[:, 0:1], scale=1.0 / HD).then_inc(roots_ready, 1)

                turned = [0]

                def turn(g):
                    k0, nk = T_GROUP[g]
                    for t in range(NT):
                        turned[0] += 1
                        act.wait_ge(qkT_mm, NGROUPS * NT * L + turned[0])
                        nc.scalar.activation(qkT[:, k0:k0 + nk, P * t:P * t + P],
                                             bank[4 + t][:, 0:P * nk].rearrange("q (j s) -> q j s", j=nk), ACT.Copy).then_inc(qkT_act, 1)

                def scores(m):
                    kind, t, _, _ = MAPS[m]
                    nk = P * (t + 1)
                    if kind == "idx":
                        act.wait_ge(map_mm, len(MAPS) * L + m + 1)
                        if m >= 2:
                            act.wait_ge(idx_added, NIDX * L + m - 1)
                        for b in range(2):
                            mm = nc.scalar.activation(pairs_of_heads[m % 2][:, :, T * b:T * b + nk],
                                                      bank[score_bank(m) + b][:, :].rearrange("q (h k) -> q h k", h=2)[:, :, 0:nk],
                                                      ACT.Relu, scale=SCALE)
                        mm.then_inc(relu_done, 1)
                        return
                    act.wait_ge(masked, SOFT * L + m - NIDX + 1)
                    for h in range(NHEAD):
                        p = sprob[m % 2][h][:, 0:nk]
                        mm = nc.scalar.activation(p, p, ACT.Exp, bias=nb[:, m % 2, h:h + 1],
                                                  scale=SCALE, accum_out=den[:, m % 2, h:h + 1])
                    mm.then_inc(exp_done, 1)

                def values(m):
                    kind, t, _, _ = MAPS[m]
                    u = UNIT_OF[m]
                    act.wait_ge(probT_mm, 9 * L + (3 * u) // 2 + 1)
                    nc.scalar.activation(probT[u][:, 0, :, :].rearrange("q h t -> q (h t)"), bank[4][:, :], ACT.Copy).then_inc(probT_act, 1)
                    if (kind, t) == ("C2", NT - 1):
                        act.wait_ge(oss_ready, NT * (L + 1))
                        nc.scalar.activation(ort[:, :, :], oss[:, :, :], ACT.Sqrt, bias=eps[:, 0:1], scale=1.0 / CV).then_inc(ort_ready, 1)

                def heads():
                    pass

                def exp_lambda():
                    act.wait_ge(ldot_ready, L + 1)
                    nc.scalar.activation(lexp[:, :], ldot[:, :], ACT.Exp).then_inc(lexp_ready, 1)

                for what, *which in ORDER:
                    {"quarter": quarter, "roots": roots, "turn": turn, "scores": scores, "values": values, "lambda": exp_lambda, "heads": heads}[what](*which)

                def out_hi(signal_in, value, dst, src, scale, signal_out):
                    act.wait_ge(signal_in, value)
                    nc.scalar.activation(dst, src[:, :].rearrange("q (j s) -> q j s", j=4), ACT.Copy, scale=scale).then_inc(signal_out, 1)

                for t in range(NT):
                    if t == 1:
                        split_hi(BRANCH0 + LEAD)
                    for h in range(2):
                        out_hi(oT_mm, 4 * L + 2 * t + h + 1, h_hi[:, 4 * h:4 * h + 4, P * t:P * t + P], bank[4 + 2 * t + h], 1.0, oT_hi)
                for n in range(BRANCH0, QUARTERS):
                    if BRANCH0 < n < QUARTERS - LEAD:
                        split_hi(n + LEAD)
                    if n in (BRANCH0 + 5, OUT0 + 1):
                        h = (n - BRANCH0) // 8
                        for t in range(NT):
                            out_hi(mT_mm, 4 * L + 2 * h + t + 1, m_hi[:, t, 4 * h:4 * h + 4, :], bank[(6, 0)[h] + t], 0.5, mT_hi)

                norm(1)
                act.wait_ge(gsub_ready, L + 1)
                nc.scalar.activation(gexp[:, :, :], gsub[:, :, :], ACT.Exp).then_inc(gexp_ready, 1)
                act.wait_ge(edif_ready, L + 1)
                nc.scalar.activation(eexp[:, :], edif[:, :], ACT.Exp).then_inc(eexp_ready, 1)

                wait_apart(act, routed, L + 1)
                n_pass = act.value_load(npass[0:1, 0:1], min_val=1, max_val=4)
                with act.Fori(0, n_pass) as ps:
                    with act.Fori(0, PAIRS) as i:
                        pairs = act.snap((p0 + ps) * PAIRS + i)
                        act.wait_ge(slab_credit, PAIR_SLABS * pairs + RING + 2)
                        nc.scalar.activation(sg, bank[4][:, :], ACT.Silu).then_inc(silu_done, 1)
                        act.wait_ge(pickwT_mm, pairs + 1)
                        nc.scalar.activation(pickwT.rearrange("q t s -> q (t s)"), bank[6][:, 0:T], ACT.Copy).then_inc(pickwT_ready, 1)
                        act.wait_ge(hidT_mm, 2 * pairs + 1)
                        nc.scalar.activation(hidT[:, 0:2, :].rearrange("q c s -> q (c s)"), bank[4][:, 0:2 * P], ACT.Copy).then_inc(hidT_act, 1)
                        act.wait_ge(down_mm, pairs + 1)
                        nc.scalar.activation(ysb[:, 0:W], bank[7][:, :], ACT.Copy).then_inc(y_act, 1)
                act.wait_ge(combined, (p0 + n_pass) * PAIRS)
                nc.scalar.activation(xres[:, 0, 0:W], bank[0][:, :], ACT.Copy)
                nc.scalar.activation(xres[:, 0, W:D], bank[1][:, :], ACT.Copy).then_inc(x_act, 1)
                act.wait_ge(x_act, L + 1)
                act.reg_add(passes, passes, n_pass)

        @block.gpsimd
        def _(pool):
            with pool.Fori(0, DEPTH) as L:
                for n in range(QUARTERS):
                    pool.wait_ge(hi_done, QUARTERS * L + n + 1)
                    w = QW if n // 4 != FULL else 2 * TAIL
                    nc.gpsimd.tensor_tensor(w_lo[:, n % QBUFS, 0:w], ring[slot_of(n // 4)][:, w * (n % 4):w * (n % 4) + w],
                                            w_hi[:, n % QBUFS, 0:w].bitcast(F), ALU.subtract).then_inc(lo_done, 1)

        @block.vector
        def _(dve):
            v = nc.vector
            dve.sem_inc(smalls_free, 1)
            v.memset(eps[:, :], EPS)
            v.memset(gpad[:, :, :], NEG)
            v.memset(rank[:, :, :], -1.0)
            v.memset(wt[:, :, :], 0.0)
            dve.drain()
            dve.wait_ge(consts_in, 96)
            dve.sem_inc(x_dve, 1)
            passes = counter(dve, "dve")

            with dve.Fori(0, DEPTH) as L:
                p0 = count_of(dve, passes)
                dve.wait_ge(smalls_in, 16 * SMALLS * (L + 1))

                def norm(n, gain):
                    for t in range(NT):
                        dve.wait_ge(rooted, NT * (NORMS * L + n) + t + 1)
                        last = v.reciprocal(rstd[:, t:t + 1], rt[:, t:t + 1])
                    last.then_inc(rstd_ready, 1)
                    dve.drain()
                    v.tensor_scalar(xs[:, 1, :, :].rearrange("q c p -> q p c"), xres[:, 1, :].rearrange("q (p c) -> q p c", c=KD),
                                    rstd[:, 1:2], None, ALU.mult).then_inc(xs_dve, 1)
                    for t in range(NT):
                        for h in range(2):
                            dve.wait_ge(hT_mm, 4 * (NORMS * L + n) + 2 * t + h + 1)
                            src = bank[4 + 2 * t + h][:, :].rearrange("q (c s) -> q c s", c=4)
                            dst = (h_hi, hnT)[n][:, 4 * h:4 * h + 4, P * t:P * t + P]
                            last = v.tensor_tensor(dst, src, gain[:, 4 * h:4 * h + 4].unsqueeze(2).broadcast_to([P, 4, P]), ALU.mult)
                            if n == 0:
                                dve.drain()
                                for c in range(4):
                                    k = 4 * h + c
                                    last = v.scalar_tensor_tensor(out=h_lo[:, k, P * t:P * t + P], in0=src[:, c, :], scalar=gain[:, k:k + 1],
                                                                  in1=h_hi[:, k, P * t:P * t + P].bitcast(F), op0=ALU.mult, op1=ALU.subtract)
                            last.then_inc(hT_ready, 1)

                norm(0, g_attn)

                H = HD // 2
                for t in range(NT):
                    v.tensor_tensor(gcos[:, t, 0:7, :], gain_b[:, :, :], rope[:, 0, t, :].unsqueeze(1).broadcast_to([P, 7, HD]), ALU.mult)
                    for a, b in ((0, H), (H, 0)):
                        v.tensor_tensor(gsin[:, t, 0:7, a:a + H], gain_b[:, :, b:b + H],
                                        rope[:, 1, t, a:a + H].unsqueeze(1).broadcast_to([P, 7, H]), ALU.mult)
                    v.tensor_copy(gcos[:, t, 7, :], rope[:, 0, t, :])
                    v.tensor_copy(gsin[:, t, 7, :], rope[:, 1, t, :])
                for n in range(2):
                    v.tensor_tensor_reduce(xs_flat[:, n, 0:HD], dlam[:, 2 * n, :], dlam[:, 2 * n + 1, :], 1.0, 0.0, ALU.mult, ALU.add,
                                           ldot[:, n:n + 1])
                dve.drain()
                dve.sem_inc(ldot_ready, 1)

                def sum_squares(g):
                    col, sets, per, _, h0, _ = GROUPS[g]
                    nh = sets * per
                    w = HD * nh
                    for t in range(NT):
                        v.tensor_tensor(xs_flat[:, t, W:W + w], qkv[:, t, col:col + w], qkv[:, t, col:col + w], ALU.mult)
                    dve.drain()
                    for t in range(NT):
                        v.tensor_reduce(hss[:, t, h0:h0 + nh], xs_flat[:, t, W:W + w].rearrange("q (h d) -> q h d", h=nh), AX.X, ALU.add)
                    dve.drain()

                def rotate(g):
                    col, sets, per, set0, h0, last = GROUPS[g]
                    nh = sets * per
                    w = HD * nh
                    wait_apart(dve, in_evac, NT * ((FULL + 1) * L + last + 1) + NT)
                    if h0 is not None:
                        if g != 5:
                            sum_squares(g)
                            if g == 4:
                                wait_apart(dve, in_evac, NT * ((FULL + 1) * L + GROUPS[5][5] + 1) + NT)
                                sum_squares(5)
                            dve.sem_inc(sums_ready, 1)
                            nr = nh if g < 4 else NSUM - h0
                            dve.wait_ge(roots_ready, len(ROOTS) * L + ROOTS.index(g) + 1)
                            v.reciprocal(hrs[:, :, h0:h0 + nr], hrt[:, :, h0:h0 + nr])
                            dve.drain()
                        for t in range(NT):
                            q = qkv[:, t, col:col + w].rearrange("q (h d) -> q h d", h=nh)
                            v.tensor_tensor(q, q, hrs[:, t, h0:h0 + nh].unsqueeze(2).broadcast_to([P, nh, HD]), ALU.mult)
                    for t in range(NT):
                        dve.drain()
                        q = qkv[:, t, col:col + w].rearrange("q (g h d) -> q g h d", g=sets, h=per)
                        a = xs_flat[:, 0, W:W + w].rearrange("q (g h d) -> q g h d", g=sets, h=per)
                        b = xs_flat[:, 1, W:W + w].rearrange("q (g h d) -> q g h d", g=sets, h=per)
                        v.tensor_tensor(a, q, gcos[:, t, set0:set0 + sets, :].unsqueeze(2).broadcast_to([P, sets, per, HD]), ALU.mult)
                        for d0, d1 in ((0, H), (H, 0)):
                            v.tensor_tensor(b[:, :, :, d0:d0 + H], q[:, :, :, d1:d1 + H],
                                            gsin[:, t, set0:set0 + sets, d0:d0 + H].unsqueeze(2).broadcast_to([P, sets, per, H]), ALU.mult)
                        dve.drain()
                        if col == KI:
                            for b2 in range(2):
                                v.tensor_tensor(ki2[:, t, HD * b2:HD * b2 + HD], xs_flat[:, 0, W:W + w], xs_flat[:, 1, W:W + w], ALU.add)
                        else:
                            v.tensor_tensor(qkv[:, t, col:col + w], xs_flat[:, 0, W:W + w], xs_flat[:, 1, W:W + w], ALU.add)
                    dve.drain()
                    dve.sem_inc(rotated, 1)

                for g in range(4):
                    rotate(g)
                for t in range(NT):
                    v.tensor_scalar(wis[:, t, :], qkv[:, t, WI:WI + IDX_HEADS], IDX_HEADS ** -0.5, None, ALU.mult)
                dve.drain()

                for m in range(NIDX):
                    _, t, _, _ = MAPS[m]
                    nk = P * (t + 1)
                    dve.wait_ge(relu_done, NIDX * L + m + 1)
                    for h in range(NHEAD):
                        wcol = wis[:, t, NHEAD * (m % 2) + h:NHEAD * (m % 2) + h + 1]
                        if m % 2 == 0 and h == 0:
                            v.tensor_scalar(score[t][:, 0:nk], sprob[m % 2][h][:, 0:nk], wcol, None, ALU.mult)
                        else:
                            v.scalar_tensor_tensor(out=score[t][:, 0:nk], in0=sprob[m % 2][h][:, 0:nk], scalar=wcol, in1=score[t][:, 0:nk],
                                                   op0=ALU.mult, op1=ALU.add)
                        dve.drain()
                    dve.sem_inc(idx_added, 1)

                def select(t):
                    nk = P * (t + 1)
                    v.tensor_tensor(left[t][:, 0:nk], score[t][:, 0:nk], causal[:, t, 0:nk], ALU.add)
                    dve.drain()
                    for _ in range(TOPK // 8):
                        v.max(m8[:, :], left[t][:, 0:nk])
                        dve.drain()
                        v.match_replace(left[t][:, 0:nk], m8[:, :], left[t][:, 0:nk], TAKEN)
                        dve.drain()
                    v.tensor_scalar(picked[t][:, 0:nk], left[t][:, 0:nk], 2 * NEG, NEG, ALU.is_gt, ALU.mult)
                    dve.drain()
                    v.tensor_tensor(picked[t][:, 0:nk], picked[t][:, 0:nk], causal[:, t, 0:nk], ALU.add)
                    dve.drain()

                def mask(m):
                    kind, t, _, _ = MAPS[m]
                    nk = P * (t + 1)
                    add = picked[t] if kind == "B" else causal[:, t, :]
                    dve.wait_ge(map_mm, len(MAPS) * L + m + 1)
                    if m >= 2 and MAPS[m - 1][0] == "C2":
                        u = UNIT_OF[m - 1]
                        dve.wait_ge(probT_mm, 9 * L + (3 * (u + 1)) // 2)
                    dve.sem_inc(past_wait, 1)
                    for h in range(NHEAD):
                        v.tensor_tensor_reduce(sprob[m % 2][h][:, 0:nk], bank[2 + h % 2][:, T * (h // 2):T * (h // 2) + nk],
                                               add[:, 0:nk], 1.0, NEG, ALU.add, ALU.max, mx[:, m % 2, h:h + 1])
                    dve.drain()
                    v.tensor_scalar(nb[:, m % 2, :], mx[:, m % 2, :], -SCALE, None, ALU.mult).then_inc(masked, 1)

                def probabilities_out(m):
                    u = UNIT_OF[m]
                    if MAPS[m][1] == 1:
                        dve.wait_ge(probT_mm, 9 * L + (3 * (u + 1)) // 2)
                        v.tensor_copy(probT[u][:, 1, :, :].rearrange("q h t -> q (h t)"), bank[5][:, :]).then_inc(probT_dve, 1)

                def finish(m):
                    kind, t, _, _ = MAPS[m]
                    u = UNIT_OF[m]
                    dve.wait_ge(pv_mm, UNITS * L + u + 1)
                    dst = xs_flat[:, t, O_OF[kind]:O_OF[kind] + (512 if kind == "C2" else 256)].rearrange("q (h d) -> q h d", h=NHEAD)
                    if kind != "C2":
                        v.tensor_tensor(dst, bank[6 + u % 2][:, 0:NHEAD * HD].rearrange("q (h d) -> q h d", h=NHEAD),
                                        rden[:, m % 2, :].unsqueeze(2).broadcast_to([P, NHEAD, HD]), ALU.mult).then_inc(o_ready, 1)
                        return
                    v.tensor_copy(dst, bank[6 + u % 2][:, :].rearrange("q (h d) -> q h d", h=NHEAD))
                    dve.drain()
                    sq = pairs_of_heads[m % 2].rearrange("q g (h k) -> q g h k", h=2)[:, :, :, 0:CV]
                    dst4 = dst.rearrange("q (g h) d -> q g h d", g=2)
                    v.tensor_tensor(sq, dst4, dst4, ALU.mult)
                    dve.drain()
                    v.tensor_reduce(oss[:, t, :].rearrange("q (g h) -> q g h", g=2), sq, AX.X, ALU.add).then_inc(oss_ready, 1)
                    v.tensor_tensor(dst, dst, subln[:, :].unsqueeze(1).broadcast_to([P, NHEAD, CV]), ALU.mult).then_inc(o_ready, 1)
                    if t == NT - 1:
                        dve.wait_ge(ort_ready, L + 1)
                        v.reciprocal(ors[:, :, :], ort[:, :, :])
                        dve.drain()
                        for t2 in range(NT):
                            dst = xs_flat[:, t2, 512:1024].rearrange("q (h d) -> q h d", h=NHEAD)
                            v.tensor_tensor(dst, dst, ors[:, t2, :].unsqueeze(2).broadcast_to([P, NHEAD, CV]), ALU.mult).then_inc(heads_ready, 1)

                mask(NIDX)
                for m in range(NIDX, len(MAPS)):
                    kind, t, _, _ = MAPS[m]
                    nk = P * (t + 1)
                    if kind == "A":
                        select(t)
                    dve.wait_ge(exp_done, SOFT * L + m - NIDX + 1)
                    v.reciprocal(rden[:, m % 2, :], den[:, m % 2, :])
                    dve.drain()
                    if kind == "C2":
                        one, two = (m - 1) % 2, m % 2
                        v.tensor_scalar(rden[:, two, :], rden[:, two, :], nlam[:, 0:1], None, ALU.mult)
                        dve.drain()
                        for h in range(NHEAD):
                            p = sprob[two][h][:, 0:nk]
                            v.tensor_scalar(p, p, rden[:, two, h:h + 1], None, ALU.mult)
                        dve.drain()
                        for h in range(NHEAD):
                            p = sprob[one][h][:, 0:nk]
                            last = v.scalar_tensor_tensor(out=p, in0=p, scalar=rden[:, one, h:h + 1],
                                                          in1=sprob[two][h][:, 0:nk], op0=ALU.mult, op1=ALU.add)
                        last.then_inc(prob_ready, 1)
                    if m in UNIT_OF:
                        probabilities_out(m)
                        finish(m)
                    if m + 1 < len(MAPS):
                        dve.drain()
                        if MAPS[m + 1][0] == "C1" and MAPS[m][0] == "B":
                            dve.wait_ge(lexp_ready, L + 1)
                            v.tensor_tensor(nlam[:, :], lexp[:, 1:2], lexp[:, 0:1], ALU.subtract)
                            dve.drain()
                            v.tensor_tensor(nlam[:, :], nlam[:, :], lamc[:, bass.ds(L, 1), 0:1].rearrange("q a b -> q (a b)"), ALU.subtract)
                            v.tensor_tensor(subln[:, :], subln[:, :], lamc[:, bass.ds(L, 1), 1:2].rearrange("q a b -> q (a b)").broadcast_to([P, CV]), ALU.mult)
                            dve.drain()
                            rotate(4)
                            rotate(5)
                        mask(m + 1)

                def out_lo(signal_in, value, dst, hi, src, scale, signal_out):
                    dve.wait_ge(signal_in, value)
                    v.scalar_tensor_tensor(out=dst, in0=src[:, :].rearrange("q (j s) -> q j s", j=4), scalar=scale, in1=hi.bitcast(F),
                                           op0=ALU.mult, op1=ALU.subtract).then_inc(signal_out, 1)

                for t in range(NT):
                    for h in range(2):
                        out_lo(oT_hi, 4 * L + 2 * t + h + 1, h_lo[:, 4 * h:4 * h + 4, P * t:P * t + P],
                               h_hi[:, 4 * h:4 * h + 4, P * t:P * t + P], bank[4 + 2 * t + h], 1.0, oT_lo)

                for r in range(6):
                    h, b = r // 3, r % 3
                    dve.wait_ge(quarter_mm, QUARTERS * L + BRANCH0 + 4 * h + (1, 2, 4)[b])
                    for t in range(NT):
                        gate = gates[:, t, D * b + W * h:D * b + W * h + W]
                        last = v.scalar_tensor_tensor(out=merged[:, t, W * h:W * h + W] if b == 0 else branch[:, t, :],
                                                      in0=gate, scalar=1.0, in1=bank[2 * (r % 2) + t][:, :], op0=ALU.add, op1=ALU.mult)
                    if b > 0:
                        dve.drain()
                        for t in range(NT):
                            m = merged[:, t, W * h:W * h + W]
                            last = v.tensor_tensor(m, m, branch[:, t, :], ALU.add)
                    last.then_inc(branch_used, 1)
                    dve.drain()
                    if r == 3:
                        for t in range(NT):
                            out_lo(mT_hi, 4 * L + t + 1, m_lo[:, t, 0:4, :], m_hi[:, t, 0:4, :], bank[6 + t], 0.5, mT_lo)
                for t in range(NT):
                    out_lo(mT_hi, 4 * L + 2 + t + 1, m_lo[:, t, 4:8, :], m_hi[:, t, 4:8, :], bank[t], 0.5, mT_lo)
                for t in range(NT):
                    if t == 0:
                        dve.wait_ge(out_mm, L + 1)
                    else:
                        dve.wait_ge(quarter_mm, QUARTERS * (L + 1))
                    for h in range(2):
                        x = xres[:, t, W * h:W * h + W]
                        v.tensor_tensor(x, x, bank[4 + 2 * t + h][:, :], ALU.add).then_inc(x_mixed, 1)
                dve.drain()
                norm(1, g_ffn)

                dve.wait_ge(route_mm, L + 1)
                v.tensor_tensor(lg[:, :, :], bank[4][:, 0:NT * NR].rearrange("q (t n) -> q t n", t=NT),
                                b_route[:, :].unsqueeze(1).broadcast_to([P, NT, NR]), ALU.add)
                dve.drain()
                v.tensor_copy(gpad[:, :, 0:NG], lg[:, :, 0:NG])
                dve.drain()
                for t in range(NT):
                    v.max(gm8[:, t, :], gpad[:, t, :])
                dve.drain()
                for t in range(NT):
                    v.max_index(gi8[:, t, :], gm8[:, t, :], gpad[:, t, :])
                v.tensor_tensor(gsub[:, :, :], lg[:, :, 0:NG], gm8[:, :, 0:1].broadcast_to([P, NT, NG]), ALU.subtract).then_inc(gsub_ready, 1)
                dve.drain()
                v.tensor_copy(gif[:, :], gi8[:, :, 0])
                dve.drain()
                v.tensor_tensor(goh[:, :, :], iota64[:, 0:NG].unsqueeze(1).broadcast_to([P, NT, NG]),
                                gif[:, :].unsqueeze(2).broadcast_to([P, NT, NG]), ALU.is_equal)
                dve.drain()
                v.tensor_scalar(goh[:, :, :], goh[:, :, :], 1.0, -NEG, ALU.subtract, ALU.mult)
                dve.drain()
                v.tensor_tensor(elm[:, :, :].rearrange("q t (g e) -> q t g e", g=NG), lg[:, :, NG:NR].rearrange("q t (g e) -> q t g e", g=NG),
                                goh[:, :, :].unsqueeze(3).broadcast_to([P, NT, NG, EPG]), ALU.add)
                dve.drain()
                for t in range(NT):
                    v.max(e8[:, t, :], elm[:, t, :])
                dve.drain()
                for t in range(NT):
                    v.max_index(ei8[:, t, :], e8[:, t, :], elm[:, t, :])
                v.tensor_tensor(edif[:, :], e8[:, :, 1], e8[:, :, 0], ALU.subtract).then_inc(edif_ready, 1)
                dve.drain()
                v.tensor_copy(eif[:, :, :], ei8[:, :, 0:2])
                dve.drain()
                for oh, k in ((oh1, 0), (oh2, 1)):
                    v.tensor_tensor(oh[:, :, :], iota64[:, 0:NE].unsqueeze(1).broadcast_to([P, NT, NE]),
                                    eif[:, :, k:k + 1].broadcast_to([P, NT, NE]), ALU.is_equal)
                dve.drain()
                v.tensor_tensor(chosen[:, :, :], oh1[:, :, :], oh2[:, :, :], ALU.add).then_inc(chosen_ready, 1)
                dve.wait_ge(gexp_ready, L + 1)
                v.tensor_reduce(gsum[:, :], gexp[:, :, :], AX.X, ALU.add)
                dve.wait_ge(eexp_ready, L + 1)
                v.tensor_scalar(edif[:, :], eexp[:, :], 1.0, None, ALU.add)
                dve.drain()
                v.tensor_tensor(gsum[:, :], gsum[:, :], edif[:, :], ALU.mult)
                dve.drain()
                v.reciprocal(ew[:, :, 0], gsum[:, :])
                dve.drain()
                v.tensor_tensor(ew[:, :, 1], ew[:, :, 0], eexp[:, :], ALU.mult)
                dve.drain()
                for oh, k in ((oh1, 0), (oh2, 1)):
                    v.tensor_tensor(oh[:, :, :], oh[:, :, :], ew[:, :, k:k + 1].broadcast_to([P, NT, NE]), ALU.mult)
                dve.drain()
                v.tensor_tensor(wt[:, :, 0:NE], oh1[:, :, :], oh2[:, :, :], ALU.add)
                dve.wait_ge(rank_mm, L + 1)
                v.tensor_scalar(rank[:, :, 0:NE], bank[5][:, 0:NT * NE].rearrange("q (t e) -> q t e", t=NT), 1.0, None, ALU.add)
                v.tensor_reduce(cmax[:, :], bank[5][:, 2 * NE:3 * NE], AX.X, ALU.max)
                dve.drain()
                v.tensor_tensor(rank[:, :, 0:NE], rank[:, :, 0:NE], chosen[:, :, :], ALU.mult)
                v.tensor_tensor(over[:, :], limits, cmax[:, 0:1].broadcast_to([P, 3]), ALU.is_lt)
                dve.drain()
                v.tensor_scalar(rank[:, :, 0:NE], rank[:, :, 0:NE], 1.0, None, ALU.subtract)
                v.tensor_reduce(npf[:, :], over[:, :], AX.X, ALU.add)
                dve.drain()
                v.tensor_scalar(npass[:, :], npf[:, :], 1.0, None, ALU.add).then_inc(routed, 1)
                wait_apart(dve, routed, L + 1)
                n_pass = dve.value_load(npass[0:1, 0:1], min_val=1, max_val=4)

                def one_hot(e):
                    shape = [P, NT, 2, SLOTS]
                    v.tensor_tensor(pick.rearrange("q t (e s) -> q t e s", e=2), iota64.unsqueeze(1).unsqueeze(1).broadcast_to(shape),
                                    rank[:, :, bass.ds(e, 2)].unsqueeze(3).broadcast_to(shape), ALU.is_equal)
                    dve.drain()
                    v.tensor_tensor(pickw.rearrange("q t (e s) -> q t e s", e=2), pick.rearrange("q t (e s) -> q t e s", e=2),
                                    wt[:, :, bass.ds(e, 2)].unsqueeze(3).broadcast_to(shape), ALU.mult).then_inc(pick_ready, 1)

                with dve.Fori(0, n_pass) as ps:
                    one_hot(0)
                    with dve.Fori(0, PAIRS) as i:
                        pairs = dve.snap((p0 + ps) * PAIRS + i)
                        for h in range(2):
                            dve.wait_ge(gather_mm, 2 * pairs + h + 1)
                            v.tensor_tensor(xgT[:, 4 * h:4 * h + 4, :], bank[6 + h][:, :].rearrange("q (c s) -> q c s", c=4),
                                            g_ffn[:, 4 * h:4 * h + 4].unsqueeze(2).broadcast_to([P, 4, P]), ALU.mult).then_inc(xgT_ready, 1)
                        dve.wait_ge(slab_credit, PAIR_SLABS * pairs + RING + 4)
                        dve.wait_ge(silu_done, pairs + 1)
                        v.tensor_tensor(hid.rearrange("q c p -> q p c"), sg.rearrange("q (p c) -> q p c", c=KF),
                                        bank[5][:, :].rearrange("q (p c) -> q p c", c=KF), ALU.mult).then_inc(hid_ready, 1)
                        dve.wait_ge(hidT_mm, 2 * pairs + 2)
                        v.tensor_copy(hidT[:, 2:4, :].rearrange("q c s -> q (c s)"), bank[5][:, 0:2 * P]).then_inc(hidT_dve, 1)
                        dve.wait_ge(pickwT_mm, pairs + 1)
                        one_hot(2 * i + 2)
                        dve.wait_ge(slab_credit, PAIR_SLABS * pairs + RING + 6)
                        v.tensor_copy(ysb[:, W:D], bank[6][:, :]).then_inc(y_dve, 1)
                    dve.drain()
                    v.tensor_scalar(rank[:, :, 0:NE], rank[:, :, 0:NE], float(SLOTS), None, ALU.subtract)
                    dve.drain()
                dve.sem_inc(smalls_free, 1)
                dve.wait_ge(combined, (p0 + n_pass) * PAIRS)
                v.tensor_copy(xres[:, 1, 0:W], bank[2][:, :])
                v.tensor_copy(xres[:, 1, W:D], bank[3][:, :])
                dve.drain()
                dve.sem_inc(x_dve, 1)
                dve.reg_add(passes, passes, n_pass)


_INS = ["x", "norm_attn", "w_in", "qk_gain", "idx_k_gain", "diff_lambda", "diff_subln_gain", "w_proj_a",
        "w_proj_b", "w_proj_c", "w_out", "norm_ffn", "w_group", "b_group", "w_router", "b_router",
        "w_e_gate", "w_e_up", "w_e_down"]


def _constants():
    import math

    import numpy as np

    f = np.float32
    inv = (1.0 / (f(10000.0) ** (np.arange(0, HD, 2, dtype=f) / f(HD)))).astype(f)
    ang = np.arange(T, dtype=f)[:, None] * inv[None, :]
    cos, sin = np.cos(ang), np.sin(ang)
    rope = np.stack([np.concatenate([cos, cos], 1), np.concatenate([-sin, sin], 1)])
    rope = rope.reshape(2, NT, P, HD).transpose(2, 0, 1, 3)
    pos = np.arange(T).reshape(NT, P).T
    causal = np.where(np.arange(T)[None, None, :] <= pos[:, :, None], 0.0, NEG)
    i = np.arange(P)
    square = np.stack([np.eye(P), i[:, None] < i[None, :], np.ones((P, P))], 1)
    row = np.zeros((P, 72))
    row[:, 0:64] = np.arange(64)
    row[:, 64:67] = SLOTS * np.arange(1, 4)
    init = [0.8 - 0.6 * math.exp(-0.3 * layer) for layer in range(DEPTH)]
    lam = np.broadcast_to(np.array([[v, 1.0 - v] for v in init]), (P, DEPTH, 2))
    return {"c_square": square, "c_rope": rope, "c_causal": causal, "c_row": row, "c_lam": lam}


def kernel(**inputs):
    import numpy as _np
    import concourse.bacc as _bacc
    from concourse import mybir as _mybir
    from concourse.bass_utils import run_bass_kernel_spmd as _run

    nc = _bacc.Bacc("TRN2", target_bir_lowering=False, num_devices=1)
    arrays, args = {}, []
    for name in _INS:
        arrays[name] = _np.ascontiguousarray(inputs[name])
    for name, a in _constants().items():
        arrays[name] = _np.ascontiguousarray(a.astype(_np.float32))
    for name, a in arrays.items():
        args.append(nc.dram_tensor(name, a.shape, _mybir.dt.from_np(a.dtype), kind="ExternalInput").ap())
    args.append(nc.dram_tensor("out", (1, T, D), _mybir.dt.float32, kind="ExternalOutput").ap())
    trunk(nc, *args)
    r = _run(nc, [arrays], core_ids=[0])
    return r.results[0]["out"]
```

```python
from contextlib import ExitStack

import concourse.bass as bass
from concourse import mybir

P = 128
T = 256
NT = T // P
D = 1024
KD = D // P
DEPTH = 2
HD = 64
EPS = 1e-6
SCALE = HD ** -0.5
NHEAD = 4
IDX_HEADS = 8
TOPK = min(256, T // 4)
CV = 2 * HD
NG = 4
EPG = 8
NE = NG * EPG
FE = 512
KF = FE // P
NR = NG + NE
D_IN = 6728
GATES = D_IN - 3 * D
RING = 10
W = 512
FULL = D_IN // W
TAIL = D_IN - FULL * W
QKV = GATES // W
MIX_RING = 2
MIX_SLABS = FULL + 1 + 4
QUARTERS = 4 * MIX_SLABS
QW = KD * W // 4
QBUFS = 4
LEAD = QBUFS - 1
BRANCH0 = 4 * (FULL + 1)
OUT0 = BRANCH0 + 8
PAIRS = NE // 2
PAIR_SLABS = 6
PASS_SLABS = PAIRS * PAIR_SLABS
BODY = 5
BODIES = PAIRS // BODY
REST = PAIRS - BODY * BODIES
ROUNDS = BODY * PAIR_SLABS // RING
PASS_LOADS = [len(range(k, PASS_SLABS, RING)) for k in range(RING)]
SLOTS = 64
NEG = -1e30
TAKEN = -3e38

QA, VA, QB, VB, QI, KI, WI, Q1, K1, VC = 0, 512, 768, 1280, 1536, 2048, 2112, 2120, 2632, 3144
GROUPS = [
    (QA, 2, 4, 0, 0, 0),
    (QB, 2, 4, 2, 8, 2),
    (QI, 1, 8, 7, None, 3),
    (KI, 1, 1, 6, 16, 4),
    (Q1, 1, 8, 4, 17, 5),
    (K1, 1, 8, 5, 25, 6),
]
NGROUPS = len(GROUPS)
ROOTS = [0, 1, 3, 4]
NSUM = 33
NSETS = 8
T_QA, T_KA, T_QB, T_KB, T_QI, T_KI, T_Q1, T_Q2, T_K1, T_K2 = 0, 2, 4, 6, 8, 12, 0, 2, 4, 6
T_CHUNKS = 13
T_GROUP = [(0, 4), (4, 4), (8, 4), (12, 1), (0, 4), (4, 4)]

MAPS = [("idx", t, T_QI + 2 * g, None) for t in range(NT) for g in range(2)]
MAPS += [("A", t, T_QA, T_KA) for t in range(NT)]
MAPS += [("B", t, T_QB, T_KB) for t in range(NT)]
MAPS += [(c, t, q, k) for t in range(NT) for c, q, k in (("C1", T_Q1, T_K1), ("C2", T_Q2, T_K2))]
NIDX = 4
SOFT = len(MAPS) - NIDX
UNIT_OF = {}
for _m, _map in enumerate(MAPS):
    if _map[0] in ("A", "B", "C2"):
        UNIT_OF[_m] = len(UNIT_OF)
UNITS = len(UNIT_OF)
V_OF = {"A": VA, "B": VB, "C2": VC}
O_OF = {"A": 0, "B": 256, "C2": 512}

def _order():
    steps = []

    def piece(*chunks):
        steps.extend(("quarter", 4 * s + 2 * half + i) for s, half in chunks for i in range(2))

    def step(*names):
        steps.extend(names)

    piece((0, 0), (0, 1), (1, 0))
    step(("roots", 0))
    piece((1, 1), (2, 0), (2, 1))
    step(("turn", 0), ("roots", 1))
    piece((3, 0), (3, 1))
    step(("turn", 1))
    piece((4, 0), (4, 1))
    step(("turn", 2), ("roots", 3))
    piece((5, 0))
    step(("turn", 3), ("scores", 0), ("scores", 1), ("scores", 2), ("scores", 3))
    piece((5, 1))
    step(("lambda",), ("scores", 4))
    piece((6, 0))
    step(("probs", 4), ("scores", 5), ("values", 4))
    piece((6, 1), (7, 0))
    step(("probs", 5), ("scores", 6), ("values", 5))
    piece((7, 1))
    step(("probs", 6), ("scores", 7), ("values", 6))
    piece((8, 0))
    step(("probs", 7), ("quarter", 34), ("values", 7), ("roots", 4), ("quarter", 35))
    piece((9, 0))
    step(("turn", 4))
    piece((9, 1))
    step(("turn", 5), ("quarter", 40), ("scores", 8), ("quarter", 41))
    step(("scores", 9))
    piece((10, 1))
    step(("probs", 9), ("scores", 10), ("values", 9))
    piece((11, 0))
    step(("scores", 11))
    piece((11, 1))
    step(("quarter", 48), ("probs", 11), ("quarter", 49), ("values", 11))
    piece((12, 1))
    step(("heads",))
    piece((13, 0), (13, 1))
    return steps


ORDER = _order()


def trunk(nc, x, norm_attn, w_in, qk_gain, idx_k_gain, diff_lambda, diff_subln_gain, w_proj_a,
          w_proj_b, w_proj_c, w_out, norm_ffn, w_group, b_group, w_router, b_router,
          w_e_gate, w_e_up, w_e_down, c_square, c_rope, c_causal, c_row, c_lam, out):
    F = mybir.dt.float32
    FR = mybir.dt.float32r
    I32 = mybir.dt.int32
    U32 = mybir.dt.uint32
    ALU = mybir.AluOpType
    ACT = mybir.ActivationFunctionType
    AX = mybir.AxisListType

    ctx = ExitStack()
    with ctx:
        def sb(name, shape, dt=F):
            return ctx.enter_context(nc.sbuf_tensor(name, shape, dt))

        def sem(name):
            return ctx.enter_context(nc.semaphore(name))

        ring = [sb(f"ring{k}", [P, KD * W]) for k in range(3)]
        ring.append(nc.alloc_sbuf_tensor_at("ring3", [P, KD * W], F, offset=nc.sbuf_base))
        o_hi = sb("o_hi", [P, KD, T], FR)
        o_lo = sb("o_lo", [P, KD, T], FR)
        w_hi = nc.alloc_sbuf_tensor_at("w_hi", [P, QBUFS, QW], FR, offset=nc.sbuf_base)
        slot8 = sb("ring8", [P, KD * W])
        w_lo = nc.alloc_sbuf_tensor_at("w_lo", [P, QBUFS, QW], FR, offset=nc.sbuf_base)
        slot9 = sb("ring9", [P, KD * W])
        slot6 = nc.alloc_sbuf_tensor_at("ring6", [P, KD * W], F, offset=nc.sbuf_base)
        h_hi = sb("h_hi", [P, KD, T], FR)
        h_lo = sb("h_lo", [P, KD, T], FR)
        QKV_LEFT = NT * GATES - KD * W
        GATES_LEFT = NT * 3 * D + T_CHUNKS * T - 2 * KD * W
        slot7 = nc.alloc_sbuf_tensor_at("ring7", [P, KD * W], F, offset=nc.sbuf_base + 4 * QKV_LEFT)
        slot4 = nc.alloc_sbuf_tensor_at("ring4", [P, KD * W], F, offset=nc.sbuf_base + 4 * (NT * GATES + KD * W + GATES_LEFT))
        slot5 = nc.alloc_sbuf_tensor_at("ring5", [P, KD * W], F, offset=nc.sbuf_base + 4 * NT * GATES)
        ring += [slot4, slot5, slot6, slot7, slot8, slot9]
        qkv = sb("qkv", [P, NT, GATES])
        gates = sb("gates", [P, NT, 3 * D])
        m_hi = nc.alloc_sbuf_tensor_at("m_hi", [P, NT, KD, P], FR, offset=nc.sbuf_base)
        qkT = sb("qkT", [P, T_CHUNKS, T])
        xres = sb("xres", [P, NT, D])
        m_lo = nc.alloc_sbuf_tensor_at("m_lo", [P, NT, KD, P], FR, offset=nc.sbuf_base)
        xs = sb("xs", [P, NT, KD, P])
        xs_flat = xs[:, :, :, :].rearrange("q t c p -> q t (c p)")
        gcos = gates[:, :, 2048:2560].rearrange("q t (g d) -> q t g d", g=NSETS)
        gsin = gates[:, :, 2560:3072].rearrange("q t (g d) -> q t g d", g=NSETS)
        gain_b = gates[:, 1, 1600:1600 + 7 * HD].rearrange("q (g d) -> q g d", g=7)
        qkv_flat = qkv[:, :, :].rearrange("q t n -> q (t n)")
        merged = qkv_flat[:, 0:2 * D].rearrange("q (t n) -> q t n", t=NT)
        branch = qkv_flat[:, 2 * D:2 * D + 2 * W].rearrange("q (t n) -> q t n", t=NT)

        square = sb("square", [P, 3, P])
        ident, tri, ones = square[:, 0, :], square[:, 1, :], square[:, 2, :]
        rope = sb("rope", [P, 2, NT, HD])
        causal = sb("causal", [P, NT, T])
        row = sb("row", [P, 72])
        iota64, limits = row[:, 0:64], row[:, 64:67]
        lamc = sb("lamc", [P, DEPTH, 2])
        ki2 = sb("ki2", [P, NT, 2 * HD])
        g_attn = sb("g_attn", [P, KD])
        g_ffn = sb("g_ffn", [P, KD])
        w_route = sb("w_route", [P, KD, NR])
        b_route = sb("b_route", [P, NR])
        dlam = sb("dlam", [P, 4, HD])
        subln = sb("subln", [P, CV])
        eps = sb("eps", [P, 1])
        unread = sb("unread", [P, 1])
        ssq = sb("ssq", [P, NT])
        rt = sb("rt", [P, NT])
        rstd = sb("rstd", [P, NT])
        half_rstd = sb("half_rstd", [P, NT])
        hss = sb("hss", [P, NT, NSUM])
        hrt = sb("hrt", [P, NT, NSUM])
        hrs = sb("hrs", [P, NT, NSUM])
        wis = sb("wis", [P, NT, IDX_HEADS])
        m8 = sb("m8", [P, 8])
        mx = sb("mx", [P, 2, NHEAD])
        nb = sb("nb", [P, 2, NHEAD])
        den = sb("den", [P, 2, NHEAD])
        rden = sb("rden", [P, 2, NHEAD])
        oss = sb("oss", [P, NT, NHEAD])
        ort = sb("ort", [P, NT, NHEAD])
        ors = sb("ors", [P, NT, NHEAD])
        ldot = sb("ldot", [P, 2])
        lexp = sb("lexp", [P, 2])
        nlam = sb("nlam", [P, 1])
        lg = sb("lg", [P, NT, NR])
        gpad = sb("gpad", [P, NT, 8])
        gm8 = sb("gm8", [P, NT, 8])
        gi8 = sb("gi8", [P, NT, 8], U32)
        e8 = sb("e8", [P, NT, 8])
        ei8 = sb("ei8", [P, NT, 8], U32)
        gsub = sb("gsub", [P, NT, NG])
        gexp = sb("gexp", [P, NT, NG])
        gsum = sb("gsum", [P, NT])
        gw = sb("gw", [P, NT])
        gif = sb("gif", [P, NT])
        goh = sb("goh", [P, NT, NG])
        elm = sb("elm", [P, NT, NE])
        eif = sb("eif", [P, NT, 2])
        edif = sb("edif", [P, NT])
        eexp = sb("eexp", [P, NT])
        ew = sb("ew", [P, NT, 2])
        oh1 = sb("oh1", [P, NT, NE])
        oh2 = sb("oh2", [P, NT, NE])
        chosen = sb("chosen", [P, NT, NE])
        rank = sb("rank", [P, NT, NE + 2])
        wt = sb("wt", [P, NT, NE + 2])
        count = sb("count", [P, NE])
        cmax = sb("cmax", [P, 1])
        over = sb("over", [P, 3])
        npf = sb("npf", [P, 1])
        npass = sb("npass", [P, 1], I32)

        pairs_of_heads = [qkv[:, b, 0:2 * QB].rearrange("q (g n) -> q g n", g=2)[:, :, 0:2 * T] for b in range(2)]
        sprob = [[pairs_of_heads[b][:, h // 2, T * (h % 2):T * (h % 2) + T] for h in range(NHEAD)] for b in range(2)]
        score = [qkv[:, t, QI:QI + T] for t in range(NT)]
        left = [qkv[:, t, QI + T:QI + 2 * T] for t in range(NT)]
        picked = left
        probT = [(gates[:, u % 2, 1024:2048] if u < 4 else qkv[:, u % 2, Q1:Q1 + 1024]).rearrange("q (k h t) -> q k h t", k=NT, h=NHEAD)
                 for u in range(UNITS)]
        experts = qkv_flat[:, 0:QKV_LEFT]
        xgT = experts[:, 0:1024].rearrange("q (c s) -> q c s", c=KD)
        hid = experts[:, 1024:1536].rearrange("q (c p) -> q c p", c=KF)
        sg = experts[:, 1536:2048]
        hidT = experts[:, 1536:2048].rearrange("q (c s) -> q c s", c=KF)
        ysb = experts[:, 2048:3072]
        hnT = experts[:, 0:KD * T].rearrange("q (c t) -> q c t", c=KD)
        one_hots = gates[:, :, :].rearrange("q t n -> q (t n)")[:, KD * W:KD * W + GATES_LEFT]
        pick = one_hots[:, 0:256].rearrange("q (t s) -> q t s", t=NT)
        pickw = one_hots[:, 256:512].rearrange("q (t s) -> q t s", t=NT)
        pickwT = one_hots[:, 1024:1280].rearrange("q (t s) -> q t s", t=NT)

        bank = [ctx.enter_context(nc.psum_tensor(f"bank{b}", [P, 512], F)) for b in range(8)]

        x_in = sem("x_in")
        square_in = sem("square_in")
        consts_in = sem("consts_in")
        smalls_in = sem("smalls_in")
        smalls_free = sem("smalls_free")
        first_gain_in = sem("first_gain_in")
        gain_in = sem("gain_in")
        gain_free = sem("gain_free")
        slab_loaded = [sem(f"slab_loaded{k}") for k in range(RING)]
        last_part_in = sem("last_part_in")
        slab_credit = sem("slab_credit")
        NORMS = 2
        squared = sem("squared")
        rooted = sem("rooted")
        rstd_ready = sem("rstd_ready")
        xs_act = sem("xs_act")
        xs_dve = sem("xs_dve")
        xs_mixed = sem("xs_mixed")
        xs_scaled = sem("xs_scaled")
        hT_mm = sem("hT_mm")
        hT_ready = sem("hT_ready")
        hi_done = sem("hi_done")
        lo_done = sem("lo_done")
        quarter_mm = sem("quarter_mm")
        in_mm = sem("in_mm")
        in_evac = sem("in_evac")
        sums_ready = sem("sums_ready")
        roots_ready = sem("roots_ready")
        rotated = sem("rotated")
        qkT_mm = sem("qkT_mm")
        qkT_act = sem("qkT_act")
        map_mm = sem("map_mm")
        relu_done = sem("relu_done")
        idx_added = sem("idx_added")
        masked = sem("masked")
        exp_done = sem("exp_done")
        prob_ready = sem("prob_ready")
        probT_mm = sem("probT_mm")
        probT_act = sem("probT_act")
        probT_dve = sem("probT_dve")
        pv_mm = sem("pv_mm")
        o_ready = sem("o_ready")
        oss_ready = sem("oss_ready")
        heads_ready = sem("heads_ready")
        ort_ready = sem("ort_ready")
        ldot_ready = sem("ldot_ready")
        lexp_ready = sem("lexp_ready")
        oT_mm = sem("oT_mm")
        oT_hi = sem("oT_hi")
        oT_lo = sem("oT_lo")
        branch_used = sem("branch_used")
        mT_mm = sem("mT_mm")
        mT_hi = sem("mT_hi")
        mT_lo = sem("mT_lo")
        out_mm = sem("out_mm")
        x_mixed = sem("x_mixed")
        route_mm = sem("route_mm")
        logits_read = sem("logits_read")
        gsub_ready = sem("gsub_ready")
        gexp_ready = sem("gexp_ready")
        edif_ready = sem("edif_ready")
        eexp_ready = sem("eexp_ready")
        chosen_ready = sem("chosen_ready")
        rank_mm = sem("rank_mm")
        routed = sem("routed")
        pick_ready = sem("pick_ready")
        pickw_ready = sem("pickw_ready")
        gather_mm = sem("gather_mm")
        xgT_ready = sem("xgT_ready")
        silu_done = sem("silu_done")
        hid_ready = sem("hid_ready")
        pickwT_mm = sem("pickwT_mm")
        pickwT_ready = sem("pickwT_ready")
        hidT_mm = sem("hidT_mm")
        hidT_act = sem("hidT_act")
        hidT_dve = sem("hidT_dve")
        down_mm = sem("down_mm")
        y_act = sem("y_act")
        y_dve = sem("y_dve")
        combined = sem("combined")
        x_act = sem("x_act")
        eps_set = sem("eps_set")
        stored = sem("stored")
        past_wait = sem("past_wait")
        SMALLS = 8

        x_view = x.rearrange("b (t p) d -> p (b t) d", p=P)
        out_view = out.rearrange("b (t p) d -> p (b t) d", p=P)

        def counter(eng, tag):
            passes = eng.alloc_register(f"passes_{tag}")
            eng.reg_mov(passes, 0)
            return passes

        def count_of(eng, passes):
            return eng.snap(passes, min_val=0, max_val=4 * DEPTH)

        def wait_apart(eng, signal, value):
            eng.wait_ge(signal, value)
            eng.sem_inc(past_wait, 1)

        def loads_up_to(slot, n):
            return sum(3 if m in (FULL + 1, FULL + 2) else 1 for m in range(n + 1) if m % MIX_RING == slot)

        MIX_LOADS = [loads_up_to(slot, MIX_SLABS - 1) for slot in range(RING)]

        def slot_of(n):
            return n % MIX_RING

        HT_ORDER = ([(t, h) for h in range(2) for t in range(NT)], [(t, h) for t in range(NT) for h in range(2)])

        def chunked(tile):
            return tile.rearrange("q c p -> q p c")

        def place_free(eng, passes, b, n):
            eng.wait_ge(slab_credit, PASS_SLABS * passes + BODY * PAIR_SLABS * b + n + 1)

        def pass_begins(eng, passes, k):
            eng.wait_ge(slab_credit, PASS_SLABS * passes + k + 1 + RING * PASS_LOADS[k] - PASS_SLABS)

        def pair_slab(j, k):
            return (PAIR_SLABS * j + k) % RING, (PAIR_SLABS * j + k) // RING

        def wait_mix_slab(eng, n, L, p0):
            eng.wait_ge(slab_loaded[slot_of(n)],
                        16 * (MIX_LOADS[slot_of(n)] * L + PASS_LOADS[slot_of(n)] * p0 + loads_up_to(slot_of(n), n)))

        EARLY = {11: 2}

        def score_bank(m):
            return 6 if m in (1, 3) else 2

        block = ctx.enter_context(nc.Block())

        @block.sync
        def _(sp):
            sp.dma_start(xres[:, :, :], x_view).then_inc(x_in, 16)
            passes = counter(sp, "sp")

            with sp.Fori(0, DEPTH) as L:
                p0 = count_of(sp, passes)
                def load_expert(pair, j, k, last=False):
                    w = (w_e_gate, w_e_up, w_e_down)[k // 2]
                    slot = pair_slab(j, k)[0]
                    source = w[L, 2 * pair + k % 2, :, :].rearrange("(p c) n -> p (c n)", p=P)
                    if last:
                        sp.dma_start(ring[slot][:, 0:KD * W // 2], source[:, 0:KD * W // 2]).then_inc(slab_loaded[slot], 16)
                        sp.dma_start(ring[slot][:, KD * W // 2:KD * W], source[:, KD * W // 2:KD * W]).then_inc(last_part_in, 16)
                    else:
                        sp.dma_start(ring[slot][:, :], source).then_inc(slab_loaded[slot], 16)

                w_in_v = w_in[L, :, :].rearrange("(p c) n -> p c n", c=KD)
                sp.wait_ge(smalls_free, L + 1)
                sp.dma_start(g_attn[:, :], norm_attn[L, :].rearrange("(p c) -> p c", c=KD)).then_inc(first_gain_in, 16)
                pass_begins(sp, p0, 0)
                sp.dma_start(ring[0][:, :].rearrange("q (c n) -> q c n", c=KD), w_in_v[:, :, 0:W]).then_inc(slab_loaded[0], 16)
                sp.dma_start(gain_b[:, 0:6, :].rearrange("q g d -> q (g d)"),
                             qk_gain[L, :, :].rearrange("g d -> (g d)").partition_broadcast(P)).then_inc(smalls_in, 16)
                sp.dma_start(gain_b[:, 6, :], idx_k_gain[L, :].partition_broadcast(P)).then_inc(smalls_in, 16)
                sp.dma_start(dlam[:, :, :].rearrange("q g d -> q (g d)"),
                             diff_lambda[L, :, :].rearrange("g d -> (g d)").partition_broadcast(P)).then_inc(smalls_in, 16)
                sp.dma_start(subln[:, :], diff_subln_gain[L, :].partition_broadcast(P)).then_inc(smalls_in, 16)
                sp.dma_start(w_route[:, :, 0:NG], w_group[L, :, :].rearrange("(p c) n -> p c n", c=KD)).then_inc(smalls_in, 16)
                sp.dma_start(w_route[:, :, NG:NR], w_router[L, :, :].rearrange("(p c) n -> p c n", c=KD)).then_inc(smalls_in, 16)
                sp.dma_start(b_route[:, 0:NG], b_group[L, :].partition_broadcast(P)).then_inc(smalls_in, 16)
                sp.dma_start(b_route[:, NG:NR], b_router[L, :].partition_broadcast(P)).then_inc(smalls_in, 16)

                for n in range(1, MIX_SLABS):
                    if n == FULL + 3:
                        wait_apart(sp, oT_mm, 4 * (L + 1))
                        load_expert(7 // PAIR_SLABS, 7 // PAIR_SLABS, 7 % PAIR_SLABS)
                    if n == FULL + 4:
                        wait_apart(sp, quarter_mm, QUARTERS * L + BRANCH0)
                        load_expert(6 // PAIR_SLABS, 6 // PAIR_SLABS, 6 % PAIR_SLABS)
                    if n in EARLY:
                        pass_begins(sp, p0, EARLY[n])
                        sp.sem_inc(past_wait, 1)
                        load_expert(0, 0, EARLY[n])
                    k = slot_of(n)
                    if n < MIX_RING:
                        pass_begins(sp, p0, k)
                    else:
                        sp.wait_ge(lo_done, QUARTERS * L + 4 * (n - MIX_RING + 1))
                    if n == 4:
                        sp.wait_ge(gain_free, L + 1)
                        sp.dma_start(g_ffn[:, :], norm_ffn[L, :].rearrange("(p c) -> p c", c=KD)).then_inc(gain_in, 16)
                    slab = ring[k][:, :].rearrange("q (c n) -> q c n", c=KD)
                    if n < FULL:
                        sp.dma_start(slab, w_in_v[:, :, W * n:W * n + W]).then_inc(slab_loaded[k], 16)
                    elif n == FULL:
                        sp.dma_start(ring[k][:, 0:KD * TAIL].rearrange("q (c n) -> q c n", c=KD),
                                     w_in_v[:, :, FULL * W:D_IN]).then_inc(slab_loaded[k], 16)
                    elif n < FULL + 3:
                        h = n - FULL - 1
                        for w, a, b in ((w_proj_a, 0, 2), (w_proj_b, 2, 4), (w_proj_c, 4, 8)):
                            sp.dma_start(slab[:, a:b, :],
                                         w[L, :, :].rearrange("(c p) n -> p c n", p=P)[:, :, h * W:h * W + W]).then_inc(slab_loaded[k], 16)
                    else:
                        h = n - FULL - 3
                        sp.dma_start(ring[k][:, :].rearrange("q (c n) -> q c n", c=4),
                                     w_out[L, D // 2 * h:D // 2 * h + D // 2, :].rearrange("(c p) n -> p c n", p=P)).then_inc(slab_loaded[k], 16)

                def load_pairs(passes, b, count, first=0, last=False):
                    for n in range(first, count * PAIR_SLABS):
                        place_free(sp, passes, b, n)
                        load_expert(BODY * b + n // PAIR_SLABS, n // PAIR_SLABS, n % PAIR_SLABS,
                                    last=last and n == count * PAIR_SLABS - 1)

                def load_pass(passes):
                    load_pairs(passes, 0, BODY, RING)
                    with sp.Fori(1, BODIES) as b:
                        load_pairs(passes, b, BODY)
                    load_pairs(passes, BODIES, REST, last=True)

                for slot, signal, value in ((3, quarter_mm, QUARTERS * L + OUT0),
                                            (0, lo_done, QUARTERS * L + OUT0 + 4),
                                            (5, branch_used, 6 * (L + 1)),
                                            (1, lo_done, QUARTERS * (L + 1)),
                                            (4, quarter_mm, QUARTERS * (L + 1)),
                                            (8, quarter_mm, QUARTERS * (L + 1)),
                                            (9, quarter_mm, QUARTERS * (L + 1))):
                    wait_apart(sp, signal, value)
                    load_expert(slot // PAIR_SLABS, slot // PAIR_SLABS, slot % PAIR_SLABS)
                load_pass(p0)
                wait_apart(sp, routed, L + 1)
                n = sp.value_load(npass[0:1, 0:1], min_val=1, max_val=4)
                with sp.If(n > 1):
                    with sp.Fori(1, n) as more:
                        for k in range(RING):
                            pass_begins(sp, p0 + more, k)
                            load_expert(k // PAIR_SLABS, k // PAIR_SLABS, k % PAIR_SLABS)
                        load_pass(p0 + more)
                sp.reg_add(passes, passes, n)

            sp.wait_ge(x_act, NT * (DEPTH + 1))
            sp.dma_start(out_view, xres[:, :, :]).then_inc(stored, 16)
            sp.wait_ge(stored, 16)

        @block.tensor
        def _(pe):
            pe.sem_inc(slab_credit, RING)
            pe.wait_ge(square_in, 16)
            passes = counter(pe, "pe")

            pe.wait_ge(x_in, 16)
            for t in range(NT):
                for h in range(2):
                    mm = nc.tensor.matmul(bank[2 * t + h][:, :], ident, xres[:, t, W * h:W * h + W], start=True, stop=True)
            mm.then_inc(combined, 1)

            with pe.Fori(0, DEPTH) as L:
                p0 = count_of(pe, passes)

                def transpose_x(n):
                    for t, h in HT_ORDER[n]:
                            if h == 0 and n == 0:
                                pe.wait_ge((xs_act, xs_dve)[t], L + 1)
                            elif h == 0:
                                pe.wait_ge(xs_mixed, NT * L + t + 1)
                            for c in range(4):
                                mm = nc.tensor.transpose(bank[4 + 2 * t + h][:, P * c:P * c + P], xs[:, t, 4 * h + c, :], ident)
                            mm.then_inc(hT_mm, 1)

                transpose_x(0)

                def parts(out, n, lhs_hi, lhs_lo, col, w, start, stop):
                    hi, lo = w_hi[:, n % QBUFS, col:col + w], w_lo[:, n % QBUFS, col:col + w]
                    nc.tensor.matmul(out, lhs_hi, hi, start=start, stop=False)
                    nc.tensor.matmul(out, lhs_hi, lo, start=False, stop=False)
                    return nc.tensor.matmul(out, lhs_lo, hi, start=False, stop=stop)

                def quarter(n):
                    s, qc = n // 4, n % 4
                    w = W if s < FULL else TAIL
                    pe.wait_ge(lo_done, QUARTERS * L + n + 1)
                    for t in range(NT):
                        if n == 0 and t == 0:
                            pe.wait_ge(x_act, NT * L + 1)
                        if n in (0, 2):
                            pe.wait_ge(hT_ready, 4 * NORMS * L + n + t + 1)
                        if qc == 0:
                            pe.wait_ge(in_evac, NT * ((FULL + 1) * L + s) + t + 1)
                        for c in range(2):
                            k = 2 * qc + c
                            mm = parts(bank[t][:, 0:w], n, h_hi[:, k, P * t:P * t + P], h_lo[:, k, P * t:P * t + P],
                                       w * c, w, k == 0, k == KD - 1)
                        if t == 0 and qc == 3:
                            mm.then_inc(in_mm, 1)
                    mm.then_inc(quarter_mm, 1)

                def heads():
                    for t in range(NT):
                        pe.wait_ge(heads_ready, NT * L + t + 1)
                        for h in range(2):
                            for j in range(4):
                                mm = nc.tensor.transpose(bank[4 + 2 * t + h][:, P * j:P * j + P], xs[:, t, 4 * h + j, :], ident)
                            mm.then_inc(oT_mm, 1)

                turned = [0]

                def turn(g):
                    pe.wait_ge(rotated, NGROUPS * L + g + 1)
                    k0, nk = T_GROUP[g]
                    if turned[0]:
                        pe.wait_ge(qkT_act, (NGROUPS * NT) * L + turned[0])
                    for t in range(NT):
                        for j in range(nk):
                            col = GROUPS[g][0] + P * j
                            src = ki2[:, t, :] if g == 3 else qkv[:, t, col:col + P]
                            mm = nc.tensor.transpose(bank[4 + t][:, P * j:P * j + P], src, ident)
                        mm.then_inc(qkT_mm, 1)
                    turned[0] += NT

                def scores(m):
                    kind, t, tq, tk = MAPS[m]
                    pe.wait_ge(qkT_act, NGROUPS * NT * L + turned[0])
                    if 2 <= m < NIDX:
                        pe.wait_ge(relu_done, NIDX * L + m - 1)
                    elif m == NIDX:
                        pe.wait_ge(relu_done, NIDX * L + NIDX)
                    elif m > NIDX:
                        pe.wait_ge(masked, SOFT * L + m - NIDX)
                    nk = P * (t + 1)
                    for h in range(NHEAD):
                        a = HD * (h % 2)
                        k = T_KI if tk is None else tk + h // 2
                        mm = nc.tensor.matmul(bank[score_bank(m) + h % 2][:, T * (h // 2):T * (h // 2) + nk],
                                              qkT[a:a + HD, tq + h // 2, P * t:P * t + P], qkT[a:a + HD, k, 0:nk],
                                              start=True, stop=True)
                    mm.then_inc(map_mm, 1)

                def probs(m):
                    kind, t, _, _ = MAPS[m]
                    u = UNIT_OF[m]
                    src = sprob[(m - 1) % 2 if kind == "C2" else m % 2]
                    if kind == "C2":
                        pe.wait_ge(prob_ready, 2 * L + t + 1)
                    else:
                        pe.wait_ge(exp_done, SOFT * L + m - NIDX + 1)
                    for b in range(t + 1):
                        for h in range(NHEAD):
                            mm = nc.tensor.transpose(bank[4 + b][:, P * h:P * h + P], src[h][:, P * b:P * b + P], ident)
                        mm.then_inc(probT_mm, 1)

                def values(m):
                    kind, t, _, _ = MAPS[m]
                    u = UNIT_OF[m]
                    pe.wait_ge(probT_act, UNITS * L + u + 1)
                    if t == 1:
                        pe.wait_ge(probT_dve, 3 * L + u // 2 + 1)
                    if u >= 2:
                        pe.wait_ge(o_ready, UNITS * L + u - 1)
                    dv = CV if kind == "C2" else HD
                    for h in range(NHEAD):
                        for b in range(t + 1):
                            mm = nc.tensor.matmul(bank[6 + u % 2][:, dv * h:dv * h + dv], probT[u][:, b, h, :],
                                                  qkv[:, b, V_OF[kind] + dv * h:V_OF[kind] + dv * h + dv],
                                                  start=b == 0, stop=b == t)
                    mm.then_inc(pv_mm, 1)

                for what, *which in ORDER:
                    if what == "quarter":
                        quarter(*which)
                    elif what == "heads":
                        heads()
                    elif what == "turn":
                        turn(*which)
                    elif what == "scores":
                        scores(*which)
                    elif what == "probs":
                        probs(*which)
                    elif what == "values":
                        values(*which)

                def branch_quarter(n):
                    h, qc = (n - BRANCH0) // 4, n % 4
                    r = 3 * h + min(qc, 2)
                    pe.wait_ge(lo_done, QUARTERS * L + n + 1)
                    if r >= 2 and qc < 3:
                        pe.wait_ge(branch_used, 6 * L + r - 1)
                    for t in range(NT):
                        if n == BRANCH0:
                            pe.wait_ge(oT_lo, 4 * L + 2 * t + 2)
                        for c in range(2):
                            k = 2 * qc + c
                            mm = parts(bank[2 * (r % 2) + t][:, :], n, o_hi[:, k, P * t:P * t + P], o_lo[:, k, P * t:P * t + P],
                                       W * c, W, c == 0 and qc < 3, c == 1 and qc != 2)
                    mm.then_inc(quarter_mm, 1)

                def turn_merged(h):
                    pe.wait_ge(branch_used, 6 * L + 3 * h + 3)
                    for t in range(NT):
                        for j in range(4):
                            mm = nc.tensor.transpose(bank[(6, 0)[h] + t][:, P * j:P * j + P],
                                                     merged[:, t, W * h + P * j:W * h + P * j + P], ident)
                        mm.then_inc(mT_mm, 1)

                def out_quarter(n):
                    k = n - OUT0
                    pe.wait_ge(lo_done, QUARTERS * L + n + 1)
                    if k % 4 == 0:
                        pe.wait_ge(mT_lo, 4 * L + k // 2 + 2)
                    for t in range(NT):
                        for h in range(2):
                            mm = parts(bank[4 + 2 * t + h][:, :], n, m_hi[:, t, k, :], m_lo[:, t, k, :], W * h, W, k == 0, k == KD - 1)
                        if t == 0 and k == KD - 1:
                            mm.then_inc(out_mm, 1)
                    mm.then_inc(quarter_mm, 1)

                pe.wait_ge(in_evac, NT * ((FULL + 1) * (L + 1)) + NT)
                for n in range(BRANCH0, BRANCH0 + 6):
                    branch_quarter(n)
                turn_merged(0)
                for n in range(BRANCH0 + 6, OUT0):
                    branch_quarter(n)
                out_quarter(OUT0)
                out_quarter(OUT0 + 1)
                turn_merged(1)
                for n in range(OUT0 + 2, QUARTERS):
                    out_quarter(n)

                transpose_x(1)
                for t in range(NT):
                    for c in range(KD):
                        if c % 4 == 0:
                            pe.wait_ge(hT_ready, 4 * (NORMS * L + 1) + 2 * t + c // 4 + 1)
                        mm = nc.tensor.matmul(bank[2][:, NR * t:NR * t + NR], hnT[:, c, P * t:P * t + P], w_route[:, c, :],
                                              start=c == 0, stop=c == KD - 1)
                mm.then_inc(route_mm, 1)
                pe.wait_ge(x_mixed, L + 1)
                for t in range(NT):
                    for h in range(2):
                        if (t, h) == (1, 0):
                            pe.wait_ge(logits_read, L + 1)
                        nc.tensor.matmul(bank[2 * t + h][:, :], ident, xres[:, t, W * h:W * h + W], start=True, stop=True)
                pe.wait_ge(chosen_ready, L + 1)
                both = chosen[:, :, :].rearrange("q t e -> q (t e)")
                nc.tensor.matmul(bank[5][:, 2 * NE:4 * NE], ones, both, start=True, stop=True)
                nc.tensor.matmul(bank[5][:, 0:2 * NE], tri, both, start=True, stop=True)
                nc.tensor.matmul(bank[5][:, NE:2 * NE], ones, chosen[:, 0, :], start=False, stop=True,
                                 skip_group_check=True).then_inc(rank_mm, 1)

                wait_apart(pe, xs_scaled, L + 1)
                def pair_steps(ps, b, j, pairs, last=False):
                        def loaded(k):
                            slot, times = pair_slab(j, k)
                            pe.wait_ge(slab_loaded[slot], 16 * (MIX_LOADS[slot] * (L + 1) + PASS_LOADS[slot] * (p0 + ps) + ROUNDS * b + times + 1))

                        def slab(k):
                            return ring[pair_slab(j, k)[0]]

                        pe.wait_ge(pick_ready, L + (p0 + ps) * (PAIRS + 1) + BODY * b + j + 1)
                        for c in range(KD):
                            for t in range(NT):
                                mm = nc.tensor.matmul(bank[6 + c // 4][:, P * (c % 4):P * (c % 4) + P], xs[:, t, c, :], pick[:, t, :],
                                                      start=t == 0, stop=t == NT - 1)
                            if c % 4 == 3:
                                mm.then_inc(gather_mm, 1)
                        for m in range(2):
                            for k in (2 * m, 2 * m + 1):
                                loaded(k)
                            for c in range(KD):
                                if m == 0 and c % 4 == 0:
                                    pe.wait_ge(xgT_ready, 2 * pairs + c // 4 + 1)
                                for e in range(2):
                                    mm = nc.tensor.matmul(bank[4 + m][SLOTS * e:SLOTS * e + SLOTS, :], xgT[:, c, SLOTS * e:SLOTS * e + SLOTS],
                                                          slab(2 * m + e)[:, W * c:W * c + W], start=c == 0, stop=c == KD - 1)
                                    if c == KD - 1:
                                        mm.then_inc(slab_credit, 1)
                        pe.wait_ge(pickw_ready, L + (p0 + ps) * (PAIRS + 1) + BODY * b + j + 1)
                        for t in range(NT):
                            mm = nc.tensor.transpose(bank[6][:, P * t:P * t + P], pickw[:, t, :], ident)
                        mm.then_inc(pickwT_mm, 1)
                        pe.wait_ge(hid_ready, pairs + 1)
                        for c in range(KF):
                            mm = nc.tensor.transpose(bank[4 + c // 2][:, P * (c % 2):P * (c % 2) + P], hid[:, c, :], ident)
                            if c % 2 == 1:
                                mm.then_inc(hidT_mm, 1)
                        for k in (4, 5):
                            loaded(k)
                        pe.wait_ge(hidT_act, pairs + 1)
                        for c0 in (0, 2):
                            for h in range(2):
                                if c0 == 0 and h == 1:
                                    pe.wait_ge(pickwT_ready, pairs + 1)
                                elif c0 == 2 and h == 0:
                                    pe.wait_ge(hidT_dve, pairs + 1)
                                    if last:
                                        pe.wait_ge(last_part_in, 16 * (p0 + ps + 1))
                                for c in (c0, c0 + 1):
                                    for e in range(2):
                                        mm = nc.tensor.matmul(bank[7 - h][SLOTS * e:SLOTS * e + SLOTS, :], hidT[:, c, SLOTS * e:SLOTS * e + SLOTS],
                                                              slab(4 + e)[:, D * c + W * h:D * c + W * h + W], start=c == 0, stop=c == KF - 1)
                                        if c == KF - 1 and h == 0 and e == 1:
                                            mm.then_inc(down_mm, 1)
                                        if c == KF - 1 and h == 1:
                                            mm.then_inc(slab_credit, 1)
                        for h in range(2):
                            pe.wait_ge((y_act, y_dve)[h], pairs + 1)
                            for t in range(NT):
                                mm = nc.tensor.matmul(bank[2 * t + h][:, :], pickwT[:, t, :], ysb[:, W * h:W * h + W],
                                                      start=False, stop=True, skip_group_check=True)
                        mm.then_inc(combined, 1)

                def one_pass(ps):
                    with pe.Fori(0, BODIES) as b:
                        for j in range(BODY):
                            pair_steps(ps, b, j, pe.snap((p0 + ps) * PAIRS + BODY * b + j))
                    for j in range(REST):
                        pair_steps(ps, BODIES, j, pe.snap((p0 + ps) * PAIRS + BODY * BODIES + j), last=j == REST - 1)

                one_pass(0)
                wait_apart(pe, routed, L + 1)
                n_pass = pe.value_load(npass[0:1, 0:1], min_val=1, max_val=4)
                with pe.If(n_pass > 1):
                    with pe.Fori(1, n_pass) as ps:
                        one_pass(ps)
                pe.reg_add(passes, passes, n_pass)

        @block.scalar
        def _(act):
            act.sem_inc(in_evac, NT)
            act.dma_start(square[:, :, :], c_square).then_inc(square_in, 16)
            act.dma_start(rope[:, :, :, :], c_rope).then_inc(consts_in, 16)
            act.dma_start(causal[:, :, :], c_causal).then_inc(consts_in, 16)
            act.dma_start(row[:, :], c_row).then_inc(consts_in, 16)
            act.dma_start(lamc[:, :, :], c_lam).then_inc(consts_in, 16)
            act.wait_ge(eps_set, 1)
            passes = counter(act, "act")

            def root_table():
                nc.scalar.activation(unread[:, :], eps[:, :], ACT.Sqrt)

            def x_out(t):
                for h in range(2):
                    last = nc.scalar.activation(xres[:, t, W * h:W * h + W], bank[2 * t + h][:, :], ACT.Copy)
                last.then_inc(x_act, 1)

            with act.Fori(0, DEPTH) as L:
                p0 = count_of(act, passes)

                def roots_of_squares(n, scratch):
                    for t in range(NT):
                        nc.scalar.activation(scratch, xres[:, t, :], ACT.Square, accum_out=ssq[:, t:t + 1]).then_inc(squared, 1)
                        act.wait_ge(squared, NT * (NORMS * L + n) + t + 1)
                    nc.scalar.activation(rt[:, :], ssq[:, :], ACT.Sqrt, bias=eps[:, 0:1], scale=1.0 / D).then_inc(rooted, 1)

                def split_hi(n):
                    wait_mix_slab(act, n // 4, L, p0)
                    if n >= QBUFS:
                        act.wait_ge(quarter_mm, QUARTERS * L + n - QBUFS + 1)
                    w = QW if n // 4 != FULL else 2 * TAIL
                    nc.scalar.activation(w_hi[:, n % QBUFS, 0:w], ring[slot_of(n // 4)][:, w * (n % 4):w * (n % 4) + w], ACT.Copy).then_inc(hi_done, 1)

                pass_begins(act, p0, 8)
                pass_begins(act, p0, 9)
                for n in range(LEAD):
                    split_hi(n)
                act.wait_ge(combined, p0 * PAIRS + 1)
                for h in range(2):
                    last = nc.scalar.activation(chunked(xs[:, 0, :, P // 2 * h:P // 2 * h + P // 2]),
                                                bank[h][:, :].rearrange("q (p c) -> q p c", c=KD), ACT.Copy)
                last.then_inc(xs_act, 1)
                x_out(0)
                act.wait_ge(xs_dve, L + 1)
                x_out(1)
                act.wait_ge(x_act, NT * (L + 1))
                roots_of_squares(0, qkv_flat[:, 0:D])

                def quarter(n):
                    if n % 4 == 3:
                        chunk_out(n // 4, 0)
                        chunk_out(n // 4, 1)
                    if n + LEAD < QUARTERS:
                        split_hi(n + LEAD)

                def chunk_out(s, t):
                    w = W if s < FULL else TAIL
                    if t == 0:
                        act.wait_ge(in_mm, (FULL + 1) * L + s + 1)
                    else:
                        act.wait_ge(quarter_mm, QUARTERS * L + 4 * s + 4)
                    if (s, t) == (0, 0):
                        act.wait_ge(rstd_ready, NORMS * L + 1)
                    src = bank[t]
                    if (s, t) == (11, 0):
                        wait_apart(act, rotated, NGROUPS * (L + 1))
                    if s < QKV:
                        nc.scalar.activation(qkv[:, t, W * s:W * s + w], src[:, 0:w], ACT.Copy, scale=rstd[:, t:t + 1]).then_inc(in_evac, 1)
                    elif s == QKV:
                        v = GATES - QKV * W
                        nc.scalar.activation(qkv[:, t, W * s:GATES], src[:, 0:v], ACT.Copy, scale=rstd[:, t:t + 1])
                        nc.scalar.activation(gates[:, t, 0:W - v], src[:, v:W], ACT.Tanh, scale=half_rstd[:, t:t + 1]).then_inc(in_evac, 1)
                    else:
                        nc.scalar.activation(gates[:, t, W * s - GATES:W * s - GATES + w], src[:, 0:w], ACT.Tanh, scale=half_rstd[:, t:t + 1]).then_inc(in_evac, 1)

                def roots(g):
                    _, sets, per, _, h0, _ = GROUPS[g]
                    nh = sets * per if g < 4 else NSUM - h0
                    act.wait_ge(sums_ready, len(ROOTS) * L + ROOTS.index(g) + 1)
                    nc.scalar.activation(hrt[:, :, h0:h0 + nh], hss[:, :, h0:h0 + nh], ACT.Sqrt,
                                         bias=eps[:, 0:1], scale=1.0 / HD).then_inc(roots_ready, 1)

                turned = [0]

                def turn(g):
                    k0, nk = T_GROUP[g]
                    for t in range(NT):
                        turned[0] += 1
                        act.wait_ge(qkT_mm, NGROUPS * NT * L + turned[0])
                        nc.scalar.activation(qkT[:, k0:k0 + nk, P * t:P * t + P],
                                             bank[4 + t][:, 0:P * nk].rearrange("q (j s) -> q j s", j=nk), ACT.Copy).then_inc(qkT_act, 1)

                def scores(m):
                    kind, t, _, _ = MAPS[m]
                    nk = P * (t + 1)
                    if kind == "idx":
                        act.wait_ge(map_mm, len(MAPS) * L + m + 1)
                        if m >= 2:
                            act.wait_ge(idx_added, NIDX * L + m - 1)
                        for b in range(2):
                            mm = nc.scalar.activation(pairs_of_heads[m % 2][:, :, T * b:T * b + nk],
                                                      bank[score_bank(m) + b][:, :].rearrange("q (h k) -> q h k", h=2)[:, :, 0:nk],
                                                      ACT.Relu, scale=SCALE)
                        mm.then_inc(relu_done, 1)
                        return
                    act.wait_ge(masked, SOFT * L + m - NIDX + 1)
                    for h in range(NHEAD):
                        p = sprob[m % 2][h][:, 0:nk]
                        mm = nc.scalar.activation(p, p, ACT.Exp, bias=nb[:, m % 2, h:h + 1],
                                                  scale=SCALE, accum_out=den[:, m % 2, h:h + 1])
                    mm.then_inc(exp_done, 1)

                def probs(m):
                    u = UNIT_OF[m]
                    act.wait_ge(probT_mm, 9 * L + (3 * u) // 2 + 1)
                    nc.scalar.activation(probT[u][:, 0, :, :].rearrange("q h t -> q (h t)"), bank[4][:, :], ACT.Copy).then_inc(probT_act, 1)

                def values(m):
                    kind, t, _, _ = MAPS[m]
                    if (kind, t) == ("C2", NT - 1):
                        act.wait_ge(oss_ready, NT * (L + 1))
                        nc.scalar.activation(ort[:, :, :], oss[:, :, :], ACT.Sqrt, bias=eps[:, 0:1], scale=1.0 / CV).then_inc(ort_ready, 1)

                def out_hi(signal_in, value, dst, src, scale, signal_out):
                    act.wait_ge(signal_in, value)
                    nc.scalar.activation(dst, src[:, :].rearrange("q (j s) -> q j s", j=4), ACT.Copy, scale=scale).then_inc(signal_out, 1)

                def heads():
                    for t in range(NT):
                        for h in range(2):
                            out_hi(oT_mm, 4 * L + 2 * t + h + 1, o_hi[:, 4 * h:4 * h + 4, P * t:P * t + P], bank[4 + 2 * t + h], 1.0, oT_hi)

                def exp_lambda():
                    act.wait_ge(ldot_ready, L + 1)
                    nc.scalar.activation(lexp[:, :], ldot[:, :], ACT.Exp).then_inc(lexp_ready, 1)

                for what, *which in ORDER:
                    {"quarter": quarter, "roots": roots, "turn": turn, "scores": scores, "probs": probs, "values": values, "lambda": exp_lambda, "heads": heads}[what](*which)

                for n in range(BRANCH0, QUARTERS):
                    if n < QUARTERS - LEAD:
                        split_hi(n + LEAD)
                    if n in (BRANCH0 + 5, OUT0 + 1):
                        h = (n - BRANCH0) // 8
                        for t in range(NT):
                            out_hi(mT_mm, 4 * L + 2 * h + t + 1, m_hi[:, t, 4 * h:4 * h + 4, :], bank[(6, 0)[h] + t], 0.5, mT_hi)

                root_table()
                for t in range(NT):
                    act.wait_ge(xs_mixed, NT * L + t + 1)
                    last = nc.scalar.activation(xres[:, t, :].rearrange("q (p c) -> q p c", c=KD), chunked(xs[:, t, :, :]), ACT.Copy)
                last.then_inc(x_mixed, 1)
                act.wait_ge(x_mixed, L + 1)
                roots_of_squares(1, ysb)
                act.wait_ge(rstd_ready, NORMS * L + 2)
                act.wait_ge(hT_mm, 4 * (NORMS * L + 2))
                for t in range(NT):
                    last = nc.scalar.activation(xs_flat[:, t, :], xs_flat[:, t, :], ACT.Copy, scale=rstd[:, t:t + 1])
                last.then_inc(xs_scaled, 1)
                act.wait_ge(gsub_ready, L + 1)
                nc.scalar.activation(gexp[:, :, :], gsub[:, :, :], ACT.Exp).then_inc(gexp_ready, 1)
                act.wait_ge(edif_ready, L + 1)
                nc.scalar.activation(eexp[:, :], edif[:, :], ACT.Exp).then_inc(eexp_ready, 1)

                wait_apart(act, routed, L + 1)
                n_pass = act.value_load(npass[0:1, 0:1], min_val=1, max_val=4)
                with act.Fori(0, n_pass) as ps:
                    with act.Fori(0, PAIRS) as i:
                        pairs = act.snap((p0 + ps) * PAIRS + i)
                        act.wait_ge(slab_credit, PAIR_SLABS * pairs + RING + 2)
                        nc.scalar.activation(sg, bank[4][:, :], ACT.Silu).then_inc(silu_done, 1)
                        act.wait_ge(pickwT_mm, pairs + 1)
                        nc.scalar.activation(pickwT.rearrange("q t s -> q (t s)"), bank[6][:, 0:T], ACT.Copy).then_inc(pickwT_ready, 1)
                        act.wait_ge(hidT_mm, 2 * pairs + 1)
                        nc.scalar.activation(hidT[:, 0:2, :].rearrange("q c s -> q (c s)"), bank[4][:, 0:2 * P], ACT.Copy).then_inc(hidT_act, 1)
                        act.wait_ge(down_mm, pairs + 1)
                        nc.scalar.activation(ysb[:, 0:W], bank[7][:, :], ACT.Copy).then_inc(y_act, 1)
                act.reg_add(passes, passes, n_pass)

            act.wait_ge(combined, count_of(act, passes) * PAIRS + 1)
            for t in range(NT):
                x_out(t)

        @block.gpsimd
        def _(pool):
            with pool.Fori(0, DEPTH) as L:
                for n in range(QUARTERS):
                    pool.wait_ge(hi_done, QUARTERS * L + n + 1)
                    w = QW if n // 4 != FULL else 2 * TAIL
                    nc.gpsimd.tensor_tensor(w_lo[:, n % QBUFS, 0:w], ring[slot_of(n // 4)][:, w * (n % 4):w * (n % 4) + w],
                                            w_hi[:, n % QBUFS, 0:w].bitcast(F), ALU.subtract).then_inc(lo_done, 1)

        @block.vector
        def _(dve):
            v = nc.vector
            dve.sem_inc(smalls_free, 1)
            dve.sem_inc(gain_free, 1)
            v.memset(eps[:, :], EPS)
            v.memset(gpad[:, :, :], NEG)
            v.memset(rank[:, :, :], -1.0)
            v.memset(wt[:, :, :], 0.0)
            dve.drain()
            dve.sem_inc(eps_set, 1)
            passes = counter(dve, "dve")

            with dve.Fori(0, DEPTH) as L:
                p0 = count_of(dve, passes)

                def norm(n, gain):
                    if n == 0:
                        dve.wait_ge(first_gain_in, 16 * (L + 1))
                    else:
                        dve.wait_ge(gain_in, 16 * (L + 1))
                    for i, (t, h) in enumerate(HT_ORDER[n]):
                            dve.wait_ge(hT_mm, 4 * (NORMS * L + n) + i + 1)
                            src = bank[4 + 2 * t + h][:, :].rearrange("q (c s) -> q c s", c=4)
                            dst = (h_hi, hnT)[n][:, 4 * h:4 * h + 4, P * t:P * t + P]
                            last = v.tensor_tensor(dst, src, gain[:, 4 * h:4 * h + 4].unsqueeze(2).broadcast_to([P, 4, P]), ALU.mult)
                            if n == 0:
                                dve.drain()
                                for c in range(4):
                                    k = 4 * h + c
                                    last = v.scalar_tensor_tensor(out=h_lo[:, k, P * t:P * t + P], in0=src[:, c, :], scalar=gain[:, k:k + 1],
                                                                  in1=h_hi[:, k, P * t:P * t + P].bitcast(F), op0=ALU.mult, op1=ALU.subtract)
                            last.then_inc(hT_ready, 1)
                    dve.wait_ge(rooted, NORMS * L + n + 1)
                    v.reciprocal(rstd[:, :], rt[:, :])
                    dve.drain()
                    v.tensor_scalar(half_rstd[:, :], rstd[:, :], 0.5, None, ALU.mult).then_inc(rstd_ready, 1)

                dve.wait_ge(combined, p0 * PAIRS + 1)
                for h in range(2):
                    last = v.tensor_copy(chunked(xs[:, 1, :, P // 2 * h:P // 2 * h + P // 2]),
                                         bank[2 + h][:, :].rearrange("q (p c) -> q p c", c=KD))
                last.then_inc(xs_dve, 1)
                norm(0, g_attn)

                dve.wait_ge(consts_in, 64)
                dve.wait_ge(smalls_in, 16 * SMALLS * (L + 1))
                H = HD // 2
                for t in range(NT):
                    v.tensor_tensor(gcos[:, t, 0:7, :], gain_b[:, :, :], rope[:, 0, t, :].unsqueeze(1).broadcast_to([P, 7, HD]), ALU.mult)
                    for a, b in ((0, H), (H, 0)):
                        v.tensor_tensor(gsin[:, t, 0:7, a:a + H], gain_b[:, :, b:b + H],
                                        rope[:, 1, t, a:a + H].unsqueeze(1).broadcast_to([P, 7, H]), ALU.mult)
                    v.tensor_copy(gcos[:, t, 7, :], rope[:, 0, t, :])
                    v.tensor_copy(gsin[:, t, 7, :], rope[:, 1, t, :])
                for n in range(2):
                    v.tensor_tensor_reduce(xs_flat[:, n, 0:HD], dlam[:, 2 * n, :], dlam[:, 2 * n + 1, :], 1.0, 0.0, ALU.mult, ALU.add,
                                           ldot[:, n:n + 1])
                dve.drain()
                dve.sem_inc(ldot_ready, 1)

                def sum_squares(g):
                    col, sets, per, _, h0, _ = GROUPS[g]
                    nh = sets * per
                    w = HD * nh
                    for t in range(NT):
                        v.tensor_tensor(xs_flat[:, t, W:W + w], qkv[:, t, col:col + w], qkv[:, t, col:col + w], ALU.mult)
                    dve.drain()
                    for t in range(NT):
                        v.tensor_reduce(hss[:, t, h0:h0 + nh], xs_flat[:, t, W:W + w].rearrange("q (h d) -> q h d", h=nh), AX.X, ALU.add)
                    dve.drain()

                def rotate(g):
                    col, sets, per, set0, h0, last = GROUPS[g]
                    nh = sets * per
                    w = HD * nh
                    wait_apart(dve, in_evac, NT * ((FULL + 1) * L + last + 1) + NT)
                    if h0 is not None:
                        if g != 5:
                            if g < 4:
                                sum_squares(g)
                                dve.sem_inc(sums_ready, 1)
                            nr = nh if g < 4 else NSUM - h0
                            dve.wait_ge(roots_ready, len(ROOTS) * L + ROOTS.index(g) + 1)
                            v.reciprocal(hrs[:, :, h0:h0 + nr], hrt[:, :, h0:h0 + nr])
                            dve.drain()
                        for t in range(NT):
                            q = qkv[:, t, col:col + w].rearrange("q (h d) -> q h d", h=nh)
                            v.tensor_tensor(q, q, hrs[:, t, h0:h0 + nh].unsqueeze(2).broadcast_to([P, nh, HD]), ALU.mult)
                    for t in range(NT):
                        dve.drain()
                        q = qkv[:, t, col:col + w].rearrange("q (g h d) -> q g h d", g=sets, h=per)
                        a = xs_flat[:, 0, W:W + w].rearrange("q (g h d) -> q g h d", g=sets, h=per)
                        b = xs_flat[:, 1, W:W + w].rearrange("q (g h d) -> q g h d", g=sets, h=per)
                        v.tensor_tensor(a, q, gcos[:, t, set0:set0 + sets, :].unsqueeze(2).broadcast_to([P, sets, per, HD]), ALU.mult)
                        for d0, d1 in ((0, H), (H, 0)):
                            v.tensor_tensor(b[:, :, :, d0:d0 + H], q[:, :, :, d1:d1 + H],
                                            gsin[:, t, set0:set0 + sets, d0:d0 + H].unsqueeze(2).broadcast_to([P, sets, per, H]), ALU.mult)
                        dve.drain()
                        if col == KI:
                            for b2 in range(2):
                                v.tensor_tensor(ki2[:, t, HD * b2:HD * b2 + HD], xs_flat[:, 0, W:W + w], xs_flat[:, 1, W:W + w], ALU.add)
                        else:
                            v.tensor_tensor(qkv[:, t, col:col + w], xs_flat[:, 0, W:W + w], xs_flat[:, 1, W:W + w], ALU.add)
                    dve.drain()
                    dve.sem_inc(rotated, 1)

                for g in range(4):
                    rotate(g)
                for t in range(NT):
                    v.tensor_scalar(wis[:, t, :], qkv[:, t, WI:WI + IDX_HEADS], IDX_HEADS ** -0.5, None, ALU.mult)
                dve.drain()

                for m in range(NIDX):
                    _, t, _, _ = MAPS[m]
                    nk = P * (t + 1)
                    dve.wait_ge(relu_done, NIDX * L + m + 1)
                    for h in range(NHEAD):
                        wcol = wis[:, t, NHEAD * (m % 2) + h:NHEAD * (m % 2) + h + 1]
                        if m % 2 == 0 and h == 0:
                            v.tensor_scalar(score[t][:, 0:nk], sprob[m % 2][h][:, 0:nk], wcol, None, ALU.mult)
                        else:
                            v.scalar_tensor_tensor(out=score[t][:, 0:nk], in0=sprob[m % 2][h][:, 0:nk], scalar=wcol, in1=score[t][:, 0:nk],
                                                   op0=ALU.mult, op1=ALU.add)
                        dve.drain()
                    dve.sem_inc(idx_added, 1)

                def select(t):
                    nk = P * (t + 1)
                    v.tensor_tensor(left[t][:, 0:nk], score[t][:, 0:nk], causal[:, t, 0:nk], ALU.add)
                    dve.drain()
                    for _ in range(TOPK // 8):
                        v.max(m8[:, :], left[t][:, 0:nk])
                        dve.drain()
                        v.match_replace(left[t][:, 0:nk], m8[:, :], left[t][:, 0:nk], TAKEN)
                        dve.drain()
                    v.tensor_scalar(picked[t][:, 0:nk], left[t][:, 0:nk], 2 * NEG, NEG, ALU.is_gt, ALU.mult)
                    dve.drain()
                    v.tensor_tensor(picked[t][:, 0:nk], picked[t][:, 0:nk], causal[:, t, 0:nk], ALU.add)
                    dve.drain()

                def mask(m):
                    kind, t, _, _ = MAPS[m]
                    nk = P * (t + 1)
                    add = picked[t] if kind == "B" else causal[:, t, :]
                    dve.wait_ge(map_mm, len(MAPS) * L + m + 1)
                    if m >= 2 and MAPS[m - 1][0] == "C2":
                        u = UNIT_OF[m - 1]
                        dve.wait_ge(probT_mm, 9 * L + (3 * (u + 1)) // 2)
                    dve.sem_inc(past_wait, 1)
                    for h in range(NHEAD):
                        v.tensor_tensor_reduce(sprob[m % 2][h][:, 0:nk], bank[2 + h % 2][:, T * (h // 2):T * (h // 2) + nk],
                                               add[:, 0:nk], 1.0, NEG, ALU.add, ALU.max, mx[:, m % 2, h:h + 1])
                    dve.drain()
                    v.tensor_scalar(nb[:, m % 2, :], mx[:, m % 2, :], -SCALE, None, ALU.mult).then_inc(masked, 1)

                def probabilities_out(m):
                    u = UNIT_OF[m]
                    if MAPS[m][1] == 1:
                        dve.wait_ge(probT_mm, 9 * L + (3 * (u + 1)) // 2)
                        v.tensor_copy(probT[u][:, 1, :, :].rearrange("q h t -> q (h t)"), bank[5][:, :]).then_inc(probT_dve, 1)

                def finish(m):
                    kind, t, _, _ = MAPS[m]
                    u = UNIT_OF[m]
                    dve.wait_ge(pv_mm, UNITS * L + u + 1)
                    dst = xs_flat[:, t, O_OF[kind]:O_OF[kind] + (512 if kind == "C2" else 256)].rearrange("q (h d) -> q h d", h=NHEAD)
                    if kind != "C2":
                        v.tensor_tensor(dst, bank[6 + u % 2][:, 0:NHEAD * HD].rearrange("q (h d) -> q h d", h=NHEAD),
                                        rden[:, m % 2, :].unsqueeze(2).broadcast_to([P, NHEAD, HD]), ALU.mult).then_inc(o_ready, 1)
                        return
                    v.tensor_copy(dst, bank[6 + u % 2][:, :].rearrange("q (h d) -> q h d", h=NHEAD))
                    dve.drain()
                    sq = pairs_of_heads[m % 2].rearrange("q g (h k) -> q g h k", h=2)[:, :, :, 0:CV]
                    dst4 = dst.rearrange("q (g h) d -> q g h d", g=2)
                    v.tensor_tensor(sq, dst4, dst4, ALU.mult)
                    dve.drain()
                    v.tensor_reduce(oss[:, t, :].rearrange("q (g h) -> q g h", g=2), sq, AX.X, ALU.add).then_inc(oss_ready, 1)
                    v.tensor_tensor(dst, dst, subln[:, :].unsqueeze(1).broadcast_to([P, NHEAD, CV]), ALU.mult).then_inc(o_ready, 1)
                    if t == NT - 1:
                        dve.wait_ge(ort_ready, L + 1)
                        v.reciprocal(ors[:, :, :], ort[:, :, :])
                        dve.drain()
                        for t2 in range(NT):
                            dst = xs_flat[:, t2, 512:1024].rearrange("q (h d) -> q h d", h=NHEAD)
                            v.tensor_tensor(dst, dst, ors[:, t2, :].unsqueeze(2).broadcast_to([P, NHEAD, CV]), ALU.mult).then_inc(heads_ready, 1)

                mask(NIDX)
                for m in range(NIDX, len(MAPS)):
                    kind, t, _, _ = MAPS[m]
                    nk = P * (t + 1)
                    if kind == "A":
                        select(t)
                    if (kind, t) == ("B", 1):
                        sum_squares(5)
                        dve.sem_inc(sums_ready, 1)
                    dve.wait_ge(exp_done, SOFT * L + m - NIDX + 1)
                    v.reciprocal(rden[:, m % 2, :], den[:, m % 2, :])
                    dve.drain()
                    if kind == "C2":
                        one, two = (m - 1) % 2, m % 2
                        v.tensor_scalar(rden[:, two, :], rden[:, two, :], nlam[:, 0:1], None, ALU.mult)
                        dve.drain()
                        for h in range(NHEAD):
                            p = sprob[two][h][:, 0:nk]
                            v.tensor_scalar(p, p, rden[:, two, h:h + 1], None, ALU.mult)
                        dve.drain()
                        for h in range(NHEAD):
                            p = sprob[one][h][:, 0:nk]
                            last = v.scalar_tensor_tensor(out=p, in0=p, scalar=rden[:, one, h:h + 1],
                                                          in1=sprob[two][h][:, 0:nk], op0=ALU.mult, op1=ALU.add)
                        last.then_inc(prob_ready, 1)
                    if (kind, t) == ("B", 0):
                        wait_apart(dve, in_evac, NT * ((FULL + 1) * L + GROUPS[5][5] + 1) + NT)
                        sum_squares(4)
                    if m in UNIT_OF:
                        probabilities_out(m)
                        finish(m)
                    if m + 1 < len(MAPS):
                        dve.drain()
                        if MAPS[m + 1][0] == "C1" and MAPS[m][0] == "B":
                            dve.wait_ge(lexp_ready, L + 1)
                            v.tensor_tensor(nlam[:, :], lexp[:, 1:2], lexp[:, 0:1], ALU.subtract)
                            dve.drain()
                            v.tensor_tensor(nlam[:, :], nlam[:, :], lamc[:, bass.ds(L, 1), 0:1].rearrange("q a b -> q (a b)"), ALU.subtract)
                            v.tensor_tensor(subln[:, :], subln[:, :], lamc[:, bass.ds(L, 1), 1:2].rearrange("q a b -> q (a b)").broadcast_to([P, CV]), ALU.mult)
                            dve.drain()
                            rotate(4)
                            rotate(5)
                        mask(m + 1)

                def out_lo(signal_in, value, dst, hi, src, scale, signal_out):
                    dve.wait_ge(signal_in, value)
                    v.scalar_tensor_tensor(out=dst, in0=src[:, :].rearrange("q (j s) -> q j s", j=4), scalar=scale, in1=hi.bitcast(F),
                                           op0=ALU.mult, op1=ALU.subtract).then_inc(signal_out, 1)

                for t in range(NT):
                    for h in range(2):
                        out_lo(oT_hi, 4 * L + 2 * t + h + 1, o_lo[:, 4 * h:4 * h + 4, P * t:P * t + P],
                               o_hi[:, 4 * h:4 * h + 4, P * t:P * t + P], bank[4 + 2 * t + h], 1.0, oT_lo)

                for r in range(6):
                    h, b = r // 3, r % 3
                    dve.wait_ge(quarter_mm, QUARTERS * L + BRANCH0 + 4 * h + (1, 2, 4)[b])
                    for t in range(NT):
                        gate = gates[:, t, D * b + W * h:D * b + W * h + W]
                        last = v.scalar_tensor_tensor(out=merged[:, t, W * h:W * h + W] if b == 0 else branch[:, t, :],
                                                      in0=gate, scalar=1.0, in1=bank[2 * (r % 2) + t][:, :], op0=ALU.add, op1=ALU.mult)
                    if b > 0:
                        dve.drain()
                        for t in range(NT):
                            m = merged[:, t, W * h:W * h + W]
                            last = v.tensor_tensor(m, m, branch[:, t, :], ALU.add)
                    last.then_inc(branch_used, 1)
                    dve.drain()
                    if r == 3:
                        for t in range(NT):
                            out_lo(mT_hi, 4 * L + t + 1, m_lo[:, t, 0:4, :], m_hi[:, t, 0:4, :], bank[6 + t], 0.5, mT_lo)
                for t in range(NT):
                    out_lo(mT_hi, 4 * L + 2 + t + 1, m_lo[:, t, 4:8, :], m_hi[:, t, 4:8, :], bank[t], 0.5, mT_lo)
                for t in range(NT):
                    if t == 0:
                        dve.wait_ge(out_mm, L + 1)
                    else:
                        dve.wait_ge(quarter_mm, QUARTERS * (L + 1))
                    for h in range(2):
                        last = v.tensor_tensor(chunked(xs[:, t, :, P // 2 * h:P // 2 * h + P // 2]),
                                               xres[:, t, W * h:W * h + W].rearrange("q (p c) -> q p c", c=KD),
                                               bank[4 + 2 * t + h][:, :].rearrange("q (p c) -> q p c", c=KD), ALU.add)
                    last.then_inc(xs_mixed, 1)
                norm(1, g_ffn)

                dve.wait_ge(route_mm, L + 1)
                for t in range(NT):
                    last = v.scalar_tensor_tensor(out=lg[:, t, :], in0=bank[2][:, NR * t:NR * t + NR], scalar=rstd[:, t:t + 1],
                                                  in1=b_route[:, :], op0=ALU.mult, op1=ALU.add)
                last.then_inc(logits_read, 1)
                dve.drain()
                v.tensor_copy(gpad[:, :, 0:NG], lg[:, :, 0:NG])
                dve.drain()
                for t in range(NT):
                    v.max(gm8[:, t, :], gpad[:, t, :])
                dve.drain()
                for t in range(NT):
                    v.max_index(gi8[:, t, :], gm8[:, t, :], gpad[:, t, :])
                v.tensor_tensor(gsub[:, :, :], lg[:, :, 0:NG], gm8[:, :, 0:1].broadcast_to([P, NT, NG]), ALU.subtract).then_inc(gsub_ready, 1)
                dve.drain()
                v.tensor_copy(gif[:, :], gi8[:, :, 0])
                dve.drain()
                v.tensor_tensor(goh[:, :, :], iota64[:, 0:NG].unsqueeze(1).broadcast_to([P, NT, NG]),
                                gif[:, :].unsqueeze(2).broadcast_to([P, NT, NG]), ALU.is_equal)
                dve.drain()
                v.tensor_scalar(goh[:, :, :], goh[:, :, :], 1.0, -NEG, ALU.subtract, ALU.mult)
                dve.drain()
                v.tensor_tensor(elm[:, :, :].rearrange("q t (g e) -> q t g e", g=NG), lg[:, :, NG:NR].rearrange("q t (g e) -> q t g e", g=NG),
                                goh[:, :, :].unsqueeze(3).broadcast_to([P, NT, NG, EPG]), ALU.add)
                dve.drain()
                for t in range(NT):
                    v.max(e8[:, t, :], elm[:, t, :])
                dve.drain()
                for t in range(NT):
                    v.max_index(ei8[:, t, :], e8[:, t, :], elm[:, t, :])
                v.tensor_tensor(edif[:, :], e8[:, :, 1], e8[:, :, 0], ALU.subtract).then_inc(edif_ready, 1)
                dve.drain()
                v.tensor_copy(eif[:, :, :], ei8[:, :, 0:2])
                dve.drain()
                for oh, k in ((oh1, 0), (oh2, 1)):
                    v.tensor_tensor(oh[:, :, :], iota64[:, 0:NE].unsqueeze(1).broadcast_to([P, NT, NE]),
                                    eif[:, :, k:k + 1].broadcast_to([P, NT, NE]), ALU.is_equal)
                dve.drain()
                v.tensor_tensor(chosen[:, :, :], oh1[:, :, :], oh2[:, :, :], ALU.add).then_inc(chosen_ready, 1)
                dve.wait_ge(rank_mm, L + 1)
                v.tensor_scalar(rank[:, :, 0:NE], bank[5][:, 0:NT * NE].rearrange("q (t e) -> q t e", t=NT), 1.0, None, ALU.add)
                v.tensor_reduce(count[:, :], bank[5][:, 2 * NE:4 * NE].rearrange("q (t e) -> q e t", t=NT), AX.X, ALU.add)
                dve.drain()
                v.tensor_reduce(cmax[:, :], count[:, :], AX.X, ALU.max)
                v.tensor_tensor(rank[:, :, 0:NE], rank[:, :, 0:NE], chosen[:, :, :], ALU.mult)
                dve.drain()
                v.tensor_tensor(over[:, :], limits, cmax[:, 0:1].broadcast_to([P, 3]), ALU.is_lt)
                v.tensor_scalar(rank[:, :, 0:NE], rank[:, :, 0:NE], 1.0, None, ALU.subtract)
                dve.drain()
                v.tensor_reduce(npf[:, :], over[:, :], AX.X, ALU.add)
                dve.drain()
                v.tensor_scalar(npass[:, :], npf[:, :], 1.0, None, ALU.add).then_inc(routed, 1)
                def slots_of(e):
                    shape = [P, NT, 2, SLOTS]
                    v.tensor_tensor(pick.rearrange("q t (e s) -> q t e s", e=2), iota64.unsqueeze(1).unsqueeze(1).broadcast_to(shape),
                                    rank[:, :, bass.ds(e, 2)].unsqueeze(3).broadcast_to(shape), ALU.is_equal).then_inc(pick_ready, 1)
                    dve.drain()

                def weighted_slots(e):
                    shape = [P, NT, 2, SLOTS]
                    v.tensor_tensor(pickw.rearrange("q t (e s) -> q t e s", e=2), pick.rearrange("q t (e s) -> q t e s", e=2),
                                    wt[:, :, bass.ds(e, 2)].unsqueeze(3).broadcast_to(shape), ALU.mult).then_inc(pickw_ready, 1)

                def one_hot(e):
                    slots_of(e)
                    weighted_slots(e)

                slots_of(0)
                dve.wait_ge(gexp_ready, L + 1)
                v.tensor_reduce(gsum[:, :], gexp[:, :, :], AX.X, ALU.add)
                dve.wait_ge(eexp_ready, L + 1)
                v.tensor_scalar(edif[:, :], eexp[:, :], 1.0, None, ALU.add)
                dve.drain()
                v.tensor_tensor(gsum[:, :], gsum[:, :], edif[:, :], ALU.mult)
                dve.drain()
                v.reciprocal(ew[:, :, 0], gsum[:, :])
                dve.drain()
                v.tensor_tensor(ew[:, :, 1], ew[:, :, 0], eexp[:, :], ALU.mult)
                dve.drain()
                for oh, k in ((oh1, 0), (oh2, 1)):
                    v.tensor_tensor(oh[:, :, :], oh[:, :, :], ew[:, :, k:k + 1].broadcast_to([P, NT, NE]), ALU.mult)
                dve.drain()
                v.tensor_tensor(wt[:, :, 0:NE], oh1[:, :, :], oh2[:, :, :], ALU.add)
                dve.drain()
                weighted_slots(0)
                wait_apart(dve, routed, L + 1)
                dve.sem_inc(smalls_free, 1)
                n_pass = dve.value_load(npass[0:1, 0:1], min_val=1, max_val=4)

                with dve.Fori(0, n_pass) as ps:
                    with dve.Fori(0, PAIRS) as i:
                        pairs = dve.snap((p0 + ps) * PAIRS + i)
                        for h in range(2):
                            dve.wait_ge(gather_mm, 2 * pairs + h + 1)
                            v.tensor_tensor(xgT[:, 4 * h:4 * h + 4, :], bank[6 + h][:, :].rearrange("q (c s) -> q c s", c=4),
                                            g_ffn[:, 4 * h:4 * h + 4].unsqueeze(2).broadcast_to([P, 4, P]), ALU.mult).then_inc(xgT_ready, 1)
                        dve.wait_ge(slab_credit, PAIR_SLABS * pairs + RING + 4)
                        dve.wait_ge(silu_done, pairs + 1)
                        v.tensor_tensor(hid.rearrange("q c p -> q p c"), sg.rearrange("q (p c) -> q p c", c=KF),
                                        bank[5][:, :].rearrange("q (p c) -> q p c", c=KF), ALU.mult).then_inc(hid_ready, 1)
                        dve.wait_ge(hidT_mm, 2 * pairs + 2)
                        v.tensor_copy(hidT[:, 2:4, :].rearrange("q c s -> q (c s)"), bank[5][:, 0:2 * P]).then_inc(hidT_dve, 1)
                        dve.wait_ge(pickwT_mm, pairs + 1)
                        one_hot(2 * i + 2)
                        dve.wait_ge(slab_credit, PAIR_SLABS * pairs + RING + 6)
                        v.tensor_copy(ysb[:, W:D], bank[6][:, :]).then_inc(y_dve, 1)
                    dve.drain()
                    v.tensor_scalar(rank[:, :, 0:NE], rank[:, :, 0:NE], float(SLOTS), None, ALU.subtract)
                    dve.drain()
                    one_hot(0)
                dve.sem_inc(gain_free, 1)
                dve.reg_add(passes, passes, n_pass)


_INS = ["x", "norm_attn", "w_in", "qk_gain", "idx_k_gain", "diff_lambda", "diff_subln_gain", "w_proj_a",
        "w_proj_b", "w_proj_c", "w_out", "norm_ffn", "w_group", "b_group", "w_router", "b_router",
        "w_e_gate", "w_e_up", "w_e_down"]


def _constants():
    import math

    import numpy as np

    f = np.float32
    inv = (1.0 / (f(10000.0) ** (np.arange(0, HD, 2, dtype=f) / f(HD)))).astype(f)
    ang = np.arange(T, dtype=f)[:, None] * inv[None, :]
    cos, sin = np.cos(ang), np.sin(ang)
    rope = np.stack([np.concatenate([cos, cos], 1), np.concatenate([-sin, sin], 1)])
    rope = rope.reshape(2, NT, P, HD).transpose(2, 0, 1, 3)
    pos = np.arange(T).reshape(NT, P).T
    causal = np.where(np.arange(T)[None, None, :] <= pos[:, :, None], 0.0, NEG)
    i = np.arange(P)
    square = np.stack([np.eye(P), i[:, None] < i[None, :], np.ones((P, P))], 1)
    row = np.zeros((P, 72))
    row[:, 0:64] = np.arange(64)
    row[:, 64:67] = SLOTS * np.arange(1, 4)
    init = [0.8 - 0.6 * math.exp(-0.3 * layer) for layer in range(DEPTH)]
    lam = np.broadcast_to(np.array([[v, 1.0 - v] for v in init]), (P, DEPTH, 2))
    return {"c_square": square, "c_rope": rope, "c_causal": causal, "c_row": row, "c_lam": lam}


def kernel(**inputs):
    import numpy as _np
    import concourse.bacc as _bacc
    from concourse import mybir as _mybir
    from concourse.bass_utils import run_bass_kernel_spmd as _run

    nc = _bacc.Bacc("TRN2", target_bir_lowering=False, num_devices=1)
    arrays, args = {}, []
    for name in _INS:
        arrays[name] = _np.ascontiguousarray(inputs[name])
    for name, a in _constants().items():
        arrays[name] = _np.ascontiguousarray(a.astype(_np.float32))
    for name, a in arrays.items():
        args.append(nc.dram_tensor(name, a.shape, _mybir.dt.from_np(a.dtype), kind="ExternalInput").ap())
    args.append(nc.dram_tensor("out", (1, T, D), _mybir.dt.float32, kind="ExternalOutput").ap())
    trunk(nc, *args)
    r = _run(nc, [arrays], core_ids=[0])
    return r.results[0]["out"]
```
